# Optimizing a Trainium2 kernel written in Bass

```python
import math
import jax, jax.numpy as jnp
from jax import lax
import numpy as np

D_MODEL = 1024
BATCH = 1
SEQ = 256
DEPTH = 1

MIX_WIDTH = D_MODEL
MLA_WIDTH = MIX_WIDTH // 2
RET_WIDTH = MIX_WIDTH - MLA_WIDTH
MLA_HEADS = 4
MLA_NOPE_DIM = 128
MLA_ROPE_DIM = 64
MLA_QK_DIM = MLA_NOPE_DIM + MLA_ROPE_DIM
MLA_V_DIM = MLA_WIDTH // MLA_HEADS
MLA_Q_RANK = 256
MLA_KV_RANK = 128
Q_BLOCK = 128
RET_HEADS = 4
RET_HEAD_DIM = RET_WIDTH // RET_HEADS
RET_CHUNK = 128
MEM_TOKENS = 256
CROSS_HEADS = 4
CROSS_HEAD_DIM = D_MODEL // CROSS_HEADS
N_GROUPS = 4
EXPERTS_PER_GROUP = 8
N_EXPERTS = N_GROUPS * EXPERTS_PER_GROUP
TOP_K = 2
EXPERT_FF = 256
ROPE_BASE = 10000.0
EPS = 1e-6
NEG_INF = -1e30
IN_SPLITS = (MLA_Q_RANK, MLA_KV_RANK, MLA_ROPE_DIM, RET_WIDTH, RET_WIDTH, RET_WIDTH, RET_WIDTH)
IN_COLS = sum(IN_SPLITS)


def rms_norm(x, g):
    xf = x.astype(jnp.float32)
    y = xf * lax.rsqrt(jnp.mean(xf * xf, axis=-1, keepdims=True) + EPS)
    return (y * g.astype(jnp.float32)).astype(x.dtype)

def rope(x, positions):
    half = x.shape[-1] // 2
    inv_freq = ROPE_BASE ** (-jnp.arange(half, dtype=jnp.float32) / half)
    ang = positions.astype(jnp.float32)[:, :, None] * inv_freq
    cos = jnp.cos(ang)[:, :, None, :]
    sin = jnp.sin(ang)[:, :, None, :]
    xf = x.astype(jnp.float32)
    x1, x2 = xf[..., :half], xf[..., half:]
    return jnp.concatenate([x1 * cos - x2 * sin, x2 * cos + x1 * sin], axis=-1).astype(x.dtype)

def causal_block_attention(q, k, v):
    B, S, H, dq = q.shape
    dv = v.shape[-1]
    nb = S // Q_BLOCK
    scale = dq ** -0.5
    qb = q.reshape(B, nb, Q_BLOCK, H, dq).transpose(1, 0, 2, 3, 4)
    k_idx = jnp.arange(S)

    def one_block(args):
        q_blk, b = args
        s = jnp.einsum('bqhd,bkhd->bhqk', q_blk, k, preferred_element_type=jnp.float32) * scale
        q_idx = b * Q_BLOCK + jnp.arange(Q_BLOCK)
        s = jnp.where(k_idx[None, :] <= q_idx[:, None], s, NEG_INF)
        p = jax.nn.softmax(s, axis=-1).astype(v.dtype)
        return jnp.einsum('bhqk,bkhd->bqhd', p, v)

    out = lax.map(one_block, (qb, jnp.arange(nb)))
    return out.transpose(1, 0, 2, 3, 4).reshape(B, S, H, dv)

def retention_chunkwise(q, k, v):
    B, S, H, dk = q.shape
    dv = v.shape[-1]
    nc = S // RET_CHUNK

    def to_chunks(t):
        return t.astype(jnp.float32).reshape(B, nc, RET_CHUNK, H, t.shape[-1]).transpose(1, 0, 3, 2, 4)

    lg = jnp.log(1.0 - jnp.exp2(-5.0 - jnp.arange(H, dtype=jnp.float32)))
    idx = jnp.arange(RET_CHUNK, dtype=jnp.float32)
    diff = idx[:, None] - idx[None, :]
    intra = jnp.where(diff >= 0, jnp.exp(jnp.maximum(diff, 0.0)[None] * lg[:, None, None]), 0.0)
    q_decay = jnp.exp((idx + 1.0)[None] * lg[:, None])[:, :, None]
    k_decay = jnp.exp((RET_CHUNK - 1.0 - idx)[None] * lg[:, None])[:, :, None]
    chunk_decay = jnp.exp(RET_CHUNK * lg)[:, None, None]

    def step(state, qkv):
        qc, kc, vc = qkv
        scores = jnp.einsum('bhid,bhjd->bhij', qc, kc) * intra
        o = (jnp.einsum('bhij,bhjv->bhiv', scores, vc)
             + jnp.einsum('bhid,bhdv->bhiv', qc * q_decay, state))
        state = state * chunk_decay + jnp.einsum('bhjd,bhjv->bhdv', kc * k_decay, vc)
        return state, o

    state0 = jnp.zeros((B, H, dk, dv), jnp.float32)
    _, o = lax.scan(step, state0, (to_chunks(q), to_chunks(k), to_chunks(v)))
    return o.transpose(1, 0, 3, 2, 4).reshape(B, S, H, dv)

def mla_group(c_q, c_kv, k_pe, positions, q_norm_g, w_uq, kv_norm_g, w_ukv, q_qk_g, k_qk_g):
    B, S, _ = c_q.shape
    q = (rms_norm(c_q, q_norm_g) @ w_uq).reshape(B, S, MLA_HEADS, MLA_QK_DIM)
    kv = (rms_norm(c_kv, kv_norm_g) @ w_ukv).reshape(B, S, MLA_HEADS, MLA_NOPE_DIM + MLA_V_DIM)
    k_nope, v = kv[..., :MLA_NOPE_DIM], kv[..., MLA_NOPE_DIM:]
    k_rope = jnp.broadcast_to(k_pe[:, :, None, :], (B, S, MLA_HEADS, MLA_ROPE_DIM))
    k = jnp.concatenate([k_nope, k_rope], axis=-1)
    q = rms_norm(q, q_qk_g)
    k = rms_norm(k, k_qk_g)
    q = jnp.concatenate([q[..., :MLA_NOPE_DIM], rope(q[..., MLA_NOPE_DIM:], positions)], axis=-1)
    k = jnp.concatenate([k[..., :MLA_NOPE_DIM], rope(k[..., MLA_NOPE_DIM:], positions)], axis=-1)
    o = causal_block_attention(q, k, v)
    return o.reshape(B, S, MLA_WIDTH)

def retention_group(rq, rk, rv, rg, positions, gn_g):
    B, S, _ = rq.shape
    q = rope(rq.reshape(B, S, RET_HEADS, RET_HEAD_DIM), positions)
    k = rope(rk.reshape(B, S, RET_HEADS, RET_HEAD_DIM), positions) * (RET_HEAD_DIM ** -0.5)
    v = rv.reshape(B, S, RET_HEADS, RET_HEAD_DIM)
    o = retention_chunkwise(q, k, v)
    mu = jnp.mean(o, axis=-1, keepdims=True)
    var = jnp.mean(jnp.square(o - mu), axis=-1, keepdims=True)
    o = ((o - mu) * lax.rsqrt(var + EPS)).reshape(B, S, RET_WIDTH) * gn_g.astype(jnp.float32)
    return (o * jax.nn.silu(rg.astype(jnp.float32))).astype(rq.dtype)

def memory_cross_attention(h, m, w_q, w_kv, q_qk_g, k_qk_g, w_o):
    B, S, _ = h.shape
    M = m.shape[1]
    q = rms_norm((h @ w_q).reshape(B, S, CROSS_HEADS, CROSS_HEAD_DIM), q_qk_g)
    kv = m @ w_kv
    k = rms_norm(kv[..., :D_MODEL].reshape(B, M, CROSS_HEADS, CROSS_HEAD_DIM), k_qk_g)
    v = kv[..., D_MODEL:].reshape(B, M, CROSS_HEADS, CROSS_HEAD_DIM)
    s = jnp.einsum('bshd,bmhd->bhsm', q, k, preferred_element_type=jnp.float32) * (CROSS_HEAD_DIM ** -0.5)
    p = jax.nn.softmax(s, axis=-1).astype(v.dtype)
    o = jnp.einsum('bhsm,bmhd->bshd', p, v).reshape(B, S, D_MODEL)
    return o @ w_o

def hierarchical_moe(h, w_group, b_group, w_expert, b_expert, w_gate, w_up, w_down):
    def per_row(hr):
        S = hr.shape[0]
        g_logits = jnp.einsum('sd,dg->sg', hr, w_group, preferred_element_type=jnp.float32)
        g_prob = jax.nn.softmax(g_logits, axis=-1)
        g_sel = jnp.argmax(g_logits + b_group.astype(jnp.float32), axis=-1)
        g_w = jnp.take_along_axis(g_prob, g_sel[:, None], axis=-1)
        e_all = jnp.einsum('sd,de->se', hr, w_expert, preferred_element_type=jnp.float32)
        e_all = e_all.reshape(S, N_GROUPS, EXPERTS_PER_GROUP)
        e_logits = jnp.take_along_axis(e_all, g_sel[:, None, None], axis=1)[:, 0]
        e_bias = b_expert.astype(jnp.float32).reshape(N_GROUPS, EXPERTS_PER_GROUP)[g_sel]
        e_prob = jax.nn.softmax(e_logits, axis=-1)
        _, top_idx = lax.top_k(e_logits + e_bias, TOP_K)
        top_p = jnp.take_along_axis(e_prob, top_idx, axis=-1)
        top_p = top_p / jnp.sum(top_p, axis=-1, keepdims=True)
        local_w = jnp.sum(jax.nn.one_hot(top_idx, EXPERTS_PER_GROUP, dtype=jnp.float32) * top_p[..., None], axis=1)
        gate = (jax.nn.one_hot(g_sel, N_GROUPS, dtype=jnp.float32)[:, :, None]
                * local_w[:, None, :] * g_w[:, :, None]).reshape(S, N_EXPERTS)
        a = jnp.einsum('sd,edf->sef', hr, w_gate)
        u = jnp.einsum('sd,edf->sef', hr, w_up)
        act = jax.nn.silu(a) * u * gate[:, :, None].astype(hr.dtype)
        return jnp.einsum('sef,efd->sd', act, w_down)

    return lax.map(per_row, h)

def first_inputs(seed: int = 0) -> dict:
    key = jax.random.key(seed)
    ks = jax.random.split(key, 32)

    def w(k, shape, fan_in):
        return jax.random.normal(k, (DEPTH,) + shape, jnp.float32) * (fan_in ** -0.5)

    def gain(k, n):
        return 1.0 + 0.02 * jax.random.normal(k, (DEPTH, n), jnp.float32)

    def bias(k, n):
        return 0.01 * jax.random.normal(k, (DEPTH, n), jnp.float32)

    x = jax.random.normal(ks[0], (BATCH, SEQ, D_MODEL), jnp.float32)
    mem = jax.random.normal(ks[1], (BATCH, MEM_TOKENS, D_MODEL), jnp.float32)
    offsets = jax.random.randint(ks[2], (BATCH, 1), 0, 1024, dtype=jnp.int32)
    positions = offsets + jnp.arange(SEQ, dtype=jnp.int32)[None, :]
    return {
        'x': x,
        'mem': mem,
        'positions': positions,
        'attn_norm_g': gain(ks[3], D_MODEL),
        'w_in': w(ks[4], (D_MODEL, IN_COLS), D_MODEL),
        'mla_q_norm_g': gain(ks[5], MLA_Q_RANK),
        'mla_w_uq': w(ks[6], (MLA_Q_RANK, MLA_HEADS * MLA_QK_DIM), MLA_Q_RANK),
        'mla_kv_norm_g': gain(ks[7], MLA_KV_RANK),
        'mla_w_ukv': w(ks[8], (MLA_KV_RANK, MLA_HEADS * (MLA_NOPE_DIM + MLA_V_DIM)), MLA_KV_RANK),
        'mla_q_qk_g': gain(ks[9], MLA_QK_DIM),
        'mla_k_qk_g': gain(ks[10], MLA_QK_DIM),
        'ret_gn_g': gain(ks[11], RET_WIDTH),
        'w_out': w(ks[12], (MIX_WIDTH, D_MODEL), MIX_WIDTH),
        'cross_norm_g': gain(ks[13], D_MODEL),
        'mem_norm_g': gain(ks[14], D_MODEL),
        'cross_w_q': w(ks[15], (D_MODEL, D_MODEL), D_MODEL),
        'cross_w_kv': w(ks[16], (D_MODEL, 2 * D_MODEL), D_MODEL),
        'cross_q_qk_g': gain(ks[17], CROSS_HEAD_DIM),
        'cross_k_qk_g': gain(ks[18], CROSS_HEAD_DIM),
        'cross_w_o': w(ks[19], (D_MODEL, D_MODEL), D_MODEL),
        'moe_norm_g': gain(ks[20], D_MODEL),
        'router_w_group': w(ks[21], (D_MODEL, N_GROUPS), D_MODEL),
        'router_b_group': bias(ks[22], N_GROUPS),
        'router_w_expert': w(ks[23], (D_MODEL, N_EXPERTS), D_MODEL),
        'router_b_expert': bias(ks[24], N_EXPERTS),
        'expert_w_gate': w(ks[25], (N_EXPERTS, D_MODEL, EXPERT_FF), D_MODEL),
        'expert_w_up': w(ks[26], (N_EXPERTS, D_MODEL, EXPERT_FF), D_MODEL),
        'expert_w_down': w(ks[27], (N_EXPERTS, EXPERT_FF, D_MODEL), EXPERT_FF),
    }

def first_block(x, mem, positions, attn_norm_g, w_in, mla_q_norm_g, mla_w_uq, mla_kv_norm_g, mla_w_ukv,
              mla_q_qk_g, mla_k_qk_g, ret_gn_g, w_out, cross_norm_g, mem_norm_g, cross_w_q, cross_w_kv,
              cross_q_qk_g, cross_k_qk_g, cross_w_o, moe_norm_g, router_w_group, router_b_group,
              router_w_expert, router_b_expert, expert_w_gate, expert_w_up, expert_w_down):
    split_points = [int(s) for s in np.cumsum(IN_SPLITS)[:-1]]
    for l in range(DEPTH):
        h = rms_norm(x, attn_norm_g[l])
        proj = h @ w_in[l]
        c_q, c_kv, k_pe, rq, rk, rv, rg = jnp.split(proj, split_points, axis=-1)
        a_out = mla_group(c_q, c_kv, k_pe, positions, mla_q_norm_g[l], mla_w_uq[l],
                          mla_kv_norm_g[l], mla_w_ukv[l], mla_q_qk_g[l], mla_k_qk_g[l])
        r_out = retention_group(rq, rk, rv, rg, positions, ret_gn_g[l])
        x = x + jnp.concatenate([a_out, r_out], axis=-1) @ w_out[l]
        hc = rms_norm(x, cross_norm_g[l])
        m = rms_norm(mem, mem_norm_g[l])
        x = x + memory_cross_attention(hc, m, cross_w_q[l], cross_w_kv[l], cross_q_qk_g[l],
                                       cross_k_qk_g[l], cross_w_o[l])
        hm = rms_norm(x, moe_norm_g[l])
        x = x + hierarchical_moe(hm, router_w_group[l], router_b_group[l], router_w_expert[l],
                                 router_b_expert[l], expert_w_gate[l], expert_w_up[l], expert_w_down[l])
    return x


DEPTH_2 = 2

HEAD_DIM = 64
FOX_HEADS = 8
FOX_WIDTH = FOX_HEADS * HEAD_DIM
POOL_GROUPS = 4
POOL_WINDOWS = (2, 4, 8, 16)
POOL_WIDTH = D_MODEL - FOX_WIDTH
POOL_GROUP_DIM = POOL_WIDTH // POOL_GROUPS
IN_COLS_2 = 4 * FOX_WIDTH + FOX_HEADS + POOL_WIDTH
SPLITS = (FOX_WIDTH, 2 * FOX_WIDTH, 3 * FOX_WIDTH, 4 * FOX_WIDTH, 4 * FOX_WIDTH + FOX_HEADS)
RWKV_HEADS = D_MODEL // HEAD_DIM
DECAY_LORA = 64
AAA_LORA = 64
MV_LORA = 32
GATE_LORA = 160
D_FF = -(-(8 * D_MODEL) // (3 * 256)) * 256
RMS_EPS = 1e-6
GN_EPS = 64e-5
N_EVEN = (DEPTH_2 + 1) // 2
N_ODD = DEPTH_2 // 2


def _rmsnorm(x, gain):
    xf = x.astype(jnp.float32)
    y = xf * lax.rsqrt(jnp.mean(xf * xf, axis=-1, keepdims=True) + RMS_EPS)
    return (y * gain.astype(jnp.float32)).astype(x.dtype)

def _swiglu(h, w_gate, w_up, w_down):
    return (jax.nn.silu(h @ w_gate) * (h @ w_up)) @ w_down

def _token_shift(x):
    return jnp.pad(x, ((0, 0), (1, 0), (0, 0)))[:, :-1]

def _forgetting_attention(q, k, v, cum):
    b, h, s, dh = q.shape
    nb = s // Q_BLOCK
    scale = dh ** -0.5
    qb = q.reshape(b, h, nb, Q_BLOCK, dh).transpose(2, 0, 1, 3, 4)
    cb = cum.reshape(b, h, nb, Q_BLOCK).transpose(2, 0, 1, 3)
    key_pos = jnp.arange(s)

    def one_block(args):
        i, q_i, c_i = args
        q_pos = i * Q_BLOCK + jnp.arange(Q_BLOCK)
        logits = (jnp.einsum('bhqd,bhkd->bhqk', q_i, k).astype(jnp.float32) * scale
                  + c_i[..., :, None] - cum[..., None, :])
        causal = key_pos[None, :] <= q_pos[:, None]
        p = jax.nn.softmax(jnp.where(causal, logits, -1e30), axis=-1)
        return jnp.einsum('bhqk,bhkd->bhqd', p.astype(v.dtype), v)

    out = lax.map(one_block, (jnp.arange(nb), qb, cb))
    return out.transpose(1, 2, 0, 3, 4).reshape(b, h, s, dh)

def _multiscale_causal_pool(u, pool_w, pool_scale):
    b, s, _ = u.shape
    uf = u.astype(jnp.float32).reshape(b, s, POOL_GROUPS, POOL_GROUP_DIM)
    csum = jnp.cumsum(uf, axis=1)
    pos = jnp.arange(s)
    groups = []
    for g, w in enumerate(POOL_WINDOWS):
        cg = csum[:, :, g]
        prev = jnp.pad(cg, ((0, 0), (w, 0), (0, 0)))[:, :s]
        count = jnp.minimum(pos + 1, w).astype(jnp.float32)[None, :, None]
        groups.append((cg - prev) / count - uf[:, :, g])
    pooled = jnp.stack(groups, axis=2).astype(u.dtype)
    mixed = jnp.einsum('bsgc,gcd->bsgd', pooled, pool_w)
    return mixed.reshape(b, s, POOL_WIDTH) * pool_scale

def _fox_pool_mixer(h, w_in, f_bias, q_gain, k_gain, pool_w, pool_scale, w_out):
    b, s, _ = h.shape
    proj = h @ w_in
    q, k, v, og, f_logit, u = jnp.split(proj, SPLITS, axis=-1)

    def heads(t):
        return t.reshape(b, s, FOX_HEADS, HEAD_DIM)

    q = _rmsnorm(heads(q), q_gain).transpose(0, 2, 1, 3)
    k = _rmsnorm(heads(k), k_gain).transpose(0, 2, 1, 3)
    v = heads(v).transpose(0, 2, 1, 3)
    log_f = jax.nn.log_sigmoid(f_logit.astype(jnp.float32) + f_bias.astype(jnp.float32))
    cum = jnp.cumsum(log_f, axis=1).transpose(0, 2, 1)
    attn = _forgetting_attention(q, k, v, cum).transpose(0, 2, 1, 3).reshape(b, s, FOX_WIDTH)
    attn = attn * jax.nn.sigmoid(og)
    pool = _multiscale_causal_pool(u, pool_w, pool_scale)
    return jnp.concatenate([attn, pool], axis=-1) @ w_out

def _rwkv7_step(state, inp):
    r_t, w_t, k_t, v_t, a_t, b_t = inp
    sa = jnp.einsum('bhvk,bhk->bhv', state, a_t)
    state = (state * w_t[:, :, None, :] + sa[..., None] * b_t[:, :, None, :]
             + v_t[..., None] * k_t[:, :, None, :])
    return state, jnp.einsum('bhvk,bhk->bhv', state, r_t)

def _rwkv7_time_mix(h, mu, w_r, w_k, w_v, w0, w1, w2, a0, a1, a2, g1, g2,
                    k_k, k_a, r_k, ln_w, ln_b, w_o, v_first, v_mix):
    b, s, d = h.shape
    f32 = jnp.float32
    xx = _token_shift(h) - h
    xr, xw, xk, xv, xa, xg = [h + xx * mu[i] for i in range(6)]
    r = (xr @ w_r).astype(f32)
    k = (xk @ w_k).astype(f32)
    v = (xv @ w_v).astype(f32)
    w = -jax.nn.softplus(-(w0 + jnp.tanh(xw @ w1) @ w2).astype(f32)) - 0.5
    a = jax.nn.sigmoid((a0 + (xa @ a1) @ a2).astype(f32))
    g = jax.nn.sigmoid(xg @ g1) @ g2
    if v_mix is None:
        v_first = v
    else:
        v0, v1, v2 = v_mix
        v = v + (v_first - v) * jax.nn.sigmoid((v0 + (xv @ v1) @ v2).astype(f32))

    def heads(t):
        return t.reshape(b, s, RWKV_HEADS, HEAD_DIM)

    kk = heads(k * k_k.astype(f32))
    kk = kk / jnp.maximum(jnp.sqrt(jnp.sum(kk * kk, axis=-1, keepdims=True)), 1e-12)
    k = k * (1.0 + (a - 1.0) * k_a.astype(f32))
    decay = jnp.exp(-jnp.exp(w))
    rh, kh, vh, ah = heads(r), heads(k), heads(v), heads(a)
    seq_first = lambda t: t.transpose(1, 0, 2, 3)
    xs = (seq_first(rh), seq_first(heads(decay)), seq_first(kh), seq_first(vh),
          seq_first(-kk), seq_first(kk * ah))
    state0 = jnp.zeros((b, RWKV_HEADS, HEAD_DIM, HEAD_DIM), f32)
    _, ys = lax.scan(_rwkv7_step, state0, xs)
    y = ys.transpose(1, 0, 2, 3)
    mean = jnp.mean(y, axis=-1, keepdims=True)
    var = jnp.mean(jnp.square(y - mean), axis=-1, keepdims=True)
    y = ((y - mean) * lax.rsqrt(var + GN_EPS)).reshape(b, s, d) * ln_w.astype(f32) + ln_b.astype(f32)
    bonus = jnp.sum(rh * kh * r_k.astype(f32), axis=-1, keepdims=True) * vh
    y = (y + bonus.reshape(b, s, d)).astype(h.dtype)
    return (y * g) @ w_o, v_first

def second_inputs(seed: int = 0) -> dict:
    key = jax.random.key(seed)
    keys = jax.random.split(key, 40)
    counter = [0]
    f32 = jnp.float32

    def nk():
        counter[0] += 1
        return keys[counter[0] - 1]

    def nrm(shape, scale):
        return jax.random.normal(nk(), shape, f32) * scale

    def gain(shape):
        return 1.0 + 0.1 * jax.random.normal(nk(), shape, f32)

    D, F, ne, no = D_MODEL, D_FF, N_EVEN, N_ODD
    return {
        'x': nrm((BATCH, SEQ, D), 1.0),
        'mix_norm': gain((DEPTH_2, D)),
        'ffn_norm': gain((DEPTH_2, D)),
        'ffn_w_gate': nrm((DEPTH_2, D, F), D ** -0.5),
        'ffn_w_up': nrm((DEPTH_2, D, F), D ** -0.5),
        'ffn_w_down': nrm((DEPTH_2, F, D), F ** -0.5),
        'hy_w_in': nrm((ne, D, IN_COLS_2), D ** -0.5),
        'hy_f_bias': 2.0 + 0.5 * jax.random.normal(nk(), (ne, FOX_HEADS), f32),
        'hy_q_gain': gain((ne, HEAD_DIM)),
        'hy_k_gain': gain((ne, HEAD_DIM)),
        'hy_pool_w': nrm((ne, POOL_GROUPS, POOL_GROUP_DIM, POOL_GROUP_DIM), POOL_GROUP_DIM ** -0.5),
        'hy_pool_scale': gain((ne, POOL_WIDTH)),
        'hy_w_out': nrm((ne, D, D), D ** -0.5),
        'rw_mu': jax.random.uniform(nk(), (no, 6, D), f32),
        'rw_w_r': nrm((no, D, D), D ** -0.5),
        'rw_w_k': nrm((no, D, D), D ** -0.5),
        'rw_w_v': nrm((no, D, D), D ** -0.5),
        'rw_w0': nrm((no, D), 0.5),
        'rw_w1': nrm((no, D, DECAY_LORA), D ** -0.5),
        'rw_w2': nrm((no, DECAY_LORA, D), 0.5 * DECAY_LORA ** -0.5),
        'rw_a0': nrm((no, D), 0.5),
        'rw_a1': nrm((no, D, AAA_LORA), D ** -0.5),
        'rw_a2': nrm((no, AAA_LORA, D), 0.5 * AAA_LORA ** -0.5),
        'rw_g1': nrm((no, D, GATE_LORA), D ** -0.5),
        'rw_g2': nrm((no, GATE_LORA, D), GATE_LORA ** -0.5),
        'rw_k_k': gain((no, D)),
        'rw_k_a': gain((no, D)),
        'rw_r_k': nrm((no, RWKV_HEADS, HEAD_DIM), 0.1),
        'rw_ln_w': gain((no, D)),
        'rw_ln_b': nrm((no, D), 0.02),
        'rw_w_o': nrm((no, D, D), D ** -0.5),
        'rw_v0': nrm((max(no - 1, 0), D), 0.5),
        'rw_v1': nrm((max(no - 1, 0), D, MV_LORA), D ** -0.5),
        'rw_v2': nrm((max(no - 1, 0), MV_LORA, D), 0.5 * MV_LORA ** -0.5),
    }

def second_block(x, mix_norm, ffn_norm, ffn_w_gate, ffn_w_up, ffn_w_down,
              hy_w_in, hy_f_bias, hy_q_gain, hy_k_gain, hy_pool_w, hy_pool_scale, hy_w_out,
              rw_mu, rw_w_r, rw_w_k, rw_w_v, rw_w0, rw_w1, rw_w2, rw_a0, rw_a1, rw_a2,
              rw_g1, rw_g2, rw_k_k, rw_k_a, rw_r_k, rw_ln_w, rw_ln_b, rw_w_o,
              rw_v0, rw_v1, rw_v2):
    v_first = None
    for layer in range(DEPTH_2):
        h = _rmsnorm(x, mix_norm[layer])
        if layer % 2 == 0:
            e = layer // 2
            y = _fox_pool_mixer(h, hy_w_in[e], hy_f_bias[e], hy_q_gain[e], hy_k_gain[e],
                                hy_pool_w[e], hy_pool_scale[e], hy_w_out[e])
        else:
            o = layer // 2
            v_mix = None if o == 0 else (rw_v0[o - 1], rw_v1[o - 1], rw_v2[o - 1])
            y, v_first = _rwkv7_time_mix(h, rw_mu[o], rw_w_r[o], rw_w_k[o], rw_w_v[o],
                                         rw_w0[o], rw_w1[o], rw_w2[o], rw_a0[o], rw_a1[o], rw_a2[o],
                                         rw_g1[o], rw_g2[o], rw_k_k[o], rw_k_a[o], rw_r_k[o],
                                         rw_ln_w[o], rw_ln_b[o], rw_w_o[o], v_first, v_mix)
        x = x + y
        x = x + _swiglu(_rmsnorm(x, ffn_norm[layer]), ffn_w_gate[layer], ffn_w_up[layer], ffn_w_down[layer])
    return x


def setup_inputs(seed=0):
    out = dict(first_inputs(seed))
    for name, value in second_inputs(seed + 1).items():
        if name != "x":
            out[name + "_2"] = value
    return out


def reference(
    x, mem, positions, attn_norm_g, w_in, mla_q_norm_g, mla_w_uq, mla_kv_norm_g, mla_w_ukv,
    mla_q_qk_g, mla_k_qk_g, ret_gn_g, w_out, cross_norm_g, mem_norm_g, cross_w_q, cross_w_kv,
    cross_q_qk_g, cross_k_qk_g, cross_w_o, moe_norm_g, router_w_group, router_b_group,
    router_w_expert, router_b_expert, expert_w_gate, expert_w_up, expert_w_down, mix_norm_2,
    ffn_norm_2, ffn_w_gate_2, ffn_w_up_2, ffn_w_down_2, hy_w_in_2, hy_f_bias_2, hy_q_gain_2,
    hy_k_gain_2, hy_pool_w_2, hy_pool_scale_2, hy_w_out_2, rw_mu_2, rw_w_r_2, rw_w_k_2,
    rw_w_v_2, rw_w0_2, rw_w1_2, rw_w2_2, rw_a0_2, rw_a1_2, rw_a2_2, rw_g1_2, rw_g2_2, rw_k_k_2,
    rw_k_a_2, rw_r_k_2, rw_ln_w_2, rw_ln_b_2, rw_w_o_2, rw_v0_2, rw_v1_2, rw_v2_2,
):
    x = first_block(
        x, mem, positions, attn_norm_g, w_in, mla_q_norm_g, mla_w_uq, mla_kv_norm_g, mla_w_ukv,
        mla_q_qk_g, mla_k_qk_g, ret_gn_g, w_out, cross_norm_g, mem_norm_g, cross_w_q,
        cross_w_kv, cross_q_qk_g, cross_k_qk_g, cross_w_o, moe_norm_g, router_w_group,
        router_b_group, router_w_expert, router_b_expert, expert_w_gate, expert_w_up,
        expert_w_down,
    )
    return second_block(
        x, mix_norm_2, ffn_norm_2, ffn_w_gate_2, ffn_w_up_2, ffn_w_down_2, hy_w_in_2,
        hy_f_bias_2, hy_q_gain_2, hy_k_gain_2, hy_pool_w_2, hy_pool_scale_2, hy_w_out_2,
        rw_mu_2, rw_w_r_2, rw_w_k_2, rw_w_v_2, rw_w0_2, rw_w1_2, rw_w2_2, rw_a0_2, rw_a1_2,
        rw_a2_2, rw_g1_2, rw_g2_2, rw_k_k_2, rw_k_a_2, rw_r_k_2, rw_ln_w_2, rw_ln_b_2, rw_w_o_2,
        rw_v0_2, rw_v1_2, rw_v2_2,
    )


_drawn_inputs = setup_inputs


def setup_inputs(seed=0):
    import zlib

    import numpy as np

    out = dict(_drawn_inputs(seed))
    spreads = {}
    factors = {'mla_q_norm_g': 7.082,
     'mla_kv_norm_g': 8.0,
     'mla_q_qk_g': 8.0,
     'mla_k_qk_g': 8.0,
     'ret_gn_g': 13.815,
     'cross_norm_g': 8.0,
     'mem_norm_g': 4.01,
     'cross_q_qk_g': 4.271,
     'cross_k_qk_g': 4.673,
     'hy_f_bias_2': 21.808,
     'hy_q_gain_2': 118.944,
     'hy_k_gain_2': 123.4,
     'rw_k_k_2': 200.0,
     'rw_ln_b_2': 200.0,
     'moe_norm_g': 8.0,
     'router_b_group': 8.0,
     'router_b_expert': 8.0,
     'ffn_norm_2': 3.246,
     'hy_pool_scale_2': 33.063,
     'rw_w0_2': 3.654,
     'rw_w1_2': 8.0,
     'rw_w2_2': 8.0,
     'rw_a0_2': 2.776,
     'rw_a1_2': 3.354,
     'rw_a2_2': 3.321,
     'rw_k_a_2': 20.662,
     'rw_r_k_2': 2.979,
     'rw_ln_w_2': 44.842}
    for name, (base, spread) in spreads.items():
        noise = np.random.default_rng([zlib.crc32(name.encode()), seed]).standard_normal(out[name].shape)
        drawn = base * np.exp(spread * noise) if base else spread * noise
        out[name] = __import__('jax').numpy.asarray(drawn.astype(out[name].dtype))
    for name, factor in factors.items():
        out[name] = (out[name] * factor).astype(out[name].dtype)
    return out
```

```python
from contextlib import ExitStack

import numpy as np
import concourse.bass as bass
from concourse import mybir

F32 = mybir.dt.float32
I32 = mybir.dt.int32
ALU = mybir.AluOpType
ACT = mybir.ActivationFunctionType
AX = mybir.AxisListType

P = 128
S = 256
T = S // P
D = 1024
KD = D // P
EPS = 1e-6
NEG = -1e30

QR, KVR, RD, RW = 256, 128, 64, 512
H, ND, VD = 4, 128, 128
QK = ND + RD
IN1 = QR + KVR + RD + 4 * RW
G, EPG, FF = 4, 8, 256
FH, HD, FW = 8, 64, 512
IN2 = 4 * FW + FH + FW
POOLS = (2, 4, 8, 16)
DFF = 2816
RH = D // HD
GN_EPS = 64e-5
CH = 64
GL, DL = 160, 64

CONST = {}


def _constants():
    i = np.arange(P)
    parts = {}
    parts["ident"] = np.eye(P)
    causal = np.where(i[None, :] <= i[:, None], 0.0, NEG)
    parts["cmask"] = np.concatenate([causal, np.zeros((P, P)), causal], 1)
    lg = np.log(1.0 - 2.0 ** (-5.0 - np.arange(H)))
    dec = np.zeros((P, H, 3, P))
    for h in range(H):
        d = i[None, :] - i[:, None]
        diag = np.where(d >= 0, np.exp(np.maximum(d, 0) * lg[h]), 0.0)
        dec[:, h, 0] = diag
        dec[:, h, 1] = np.exp((d + P) * lg[h])
        dec[:, h, 2] = diag
    parts["decay"] = (dec * P ** -0.5).reshape(P, -1)
    half = 64
    parts["invf"] = np.repeat((10000.0 ** (-np.arange(half, dtype=np.float64) / half))[None], P, 0)
    parts["tri"] = (i[:, None] <= i[None, :]).astype(float)
    parts["ones"] = np.ones((P, P))
    pool = np.zeros((P, 4, 3, P))
    j = np.arange(S)
    for g, w in enumerate(POOLS):
        m = np.where((j[:, None] <= j[None, :]) & (j[:, None] > j[None, :] - w), 1.0, 0.0)
        m = m / np.minimum(j + 1, w)[None, :] - np.eye(S)
        pool[:, g, 0] = m[:P, :P]
        pool[:, g, 1] = m[:P, P:]
        pool[:, g, 2] = m[P:, P:]
    parts["pool"] = pool.reshape(P, -1)
    sel = np.zeros((P, FH, P))
    for h in range(FH):
        sel[h, h] = 1.0
    parts["sel"] = sel.reshape(P, -1)
    blk = i // CH
    same = blk[:, None] == blk[None, :]
    strict = same & (i[:, None] < i[None, :])
    incl = same & (i[:, None] <= i[None, :])
    parts["rwmask"] = np.concatenate([strict, incl, strict, incl], 1).astype(float)
    mid = blk * CH + CH // 2 - 1
    half_to_mid = (same & (i[:, None] <= mid[None, :])).astype(float)
    c = -np.exp(-0.5)
    parts["rwcum"] = c * (incl - half_to_mid)
    parts["rwcumx"] = c * (strict - half_to_mid)
    parts["rwmid"] = c * half_to_mid
    parts["eye2"] = np.concatenate([np.eye(CH)] * 2, 0)
    lv = []
    b = 1
    while b < CH:
        m = (i[:, None] // (2 * b) == i[None, :] // (2 * b)) & ((i[:, None] // b) % 2 == 1) & ((i[None, :] // b) % 2 == 0)
        lv.append(m)
        b *= 2
    parts["rwlev"] = np.concatenate(lv[1:], 1).astype(float)
    parts["rwlevT"] = lv[0].T.astype(float)
    parts["strictP"] = (i[:, None] < i[None, :]).astype(float)
    parts["iota"] = np.repeat(np.arange(P)[None], P, 0)
    parts["gidx"] = np.repeat(np.arange(8)[None], P, 0)
    out, at = [], 0
    for k, v in parts.items():
        CONST[k] = (at, at + v.shape[1])
        at += v.shape[1]
        out.append(v.astype(np.float32))
    return np.ascontiguousarray(np.concatenate(out, 1))


CONSTANTS = _constants()

ROWS = [("attn_norm_g", 8), ("mla_q_norm_g", 2), ("mla_kv_norm_g", 1), ("ret_gn_g", 4), ("cross_norm_g", 8),
        ("mem_norm_g", 8), ("cross_q_qk_g", 2), ("cross_k_qk_g", 2), ("moe_norm_g", 8), ("mix_norm_2", 16),
        ("ffn_norm_2", 16), ("hy_pool_scale_2", 4), ("rw_mu_2", 48)]
COL = {}
_at = 0
for _n, _r in ROWS:
    COL[_n] = _at
    _at += _r
NROWS = _at


def build(nc, out, phases="ABCDEFGO", **A):
    ctx = ExitStack()
    with ctx:
        def sb(name, shape, dt=F32):
            return ctx.enter_context(nc.sbuf_tensor(name, shape, dt))

        sems = {}

        def sem(name):
            if name not in sems:
                sems[name] = ctx.enter_context(nc.semaphore(name))
            return sems[name]

        def dram2(name, i=0):
            return A[name][i]

        BANK = [ctx.enter_context(nc.psum_tensor(f"bank{i}", [P, 512], F32)) for i in range(8)]
        RINGS = {"D": BANK[0:4], "A": BANK[4:8],
                 "GU": BANK[0:2], "TT": BANK[2:4], "Y": [BANK[4:6]], "Z": BANK[6:8],
                 "Y4": [BANK[4:8]]}
        for r in ("GU", "TT", "Y", "Z"):
            RINGS[r + "o"] = RINGS[r]
        full = {r: sem(f"full_{r}") for r in RINGS}
        moved = {r: sem(f"moved_{r}") for r in RINGS}
        jobs = {}
        filled = {r: 0 for r in RINGS}
        taken = {r: 0 for r in RINGS}

        def fill(pe, ring, name):
            n, size = filled[ring], len(RINGS[ring])
            filled[ring] += 1
            jobs[name] = (ring, n)
            if n >= size:
                pe.wait_ge(moved[ring], n - size + 1)
            return RINGS[ring][n % size]

        def take(eng, ring, name):
            n = taken[ring]
            assert jobs[name] == (ring, n), (name, jobs[name], ring, n)
            taken[ring] += 1
            eng.wait_ge(full[ring], n + 1)
            return RINGS[ring][n % len(RINGS[ring])]

        def peek(eng, name):
            ring, n = jobs[name]
            eng.wait_ge(full[ring], n + 1)
            return RINGS[ring][n % len(RINGS[ring])]

        def await_moved(eng, *names):
            need = {}
            for name in names:
                ring, n = jobs[name]
                need[ring] = max(need.get(ring, 0), n + 1)
            for ring, n in need.items():
                eng.wait_ge(moved[ring], n)

        def drained(eng, *rings):
            for r in rings:
                if filled[r]:
                    eng.wait_ge(moved[r], filled[r])

        SLOT, SLOTS = 2048, 8
        ring_w = sb("ring_w", [P, SLOTS * SLOT])
        arrived = [sem(f"arrived_{i}") for i in range(SLOTS + 4)]
        units = []
        unit_at = {}
        released = {}
        next_slot = [0]
        posted = [0] * (SLOTS + 4)
        holder = [None] * (SLOTS + 4)
        waits_for = {}

        def slot_view(slots, parts, kt, cols):
            if slots[0] < SLOTS:
                base, at = ring_w, slots[0] * SLOT
            else:
                base, at = work, EXTRA + (slots[0] - SLOTS) * SLOT
            return base[0:parts, at:at + kt * cols].rearrange("p (k n) -> p k n", k=kt)

        def place(name, slots, pieces):
            n = unit_at[name] = len(units)
            waits_for[n] = {holder[s] for s in slots} - {None}
            for s in slots:
                holder[s] = n
            posted[slots[0]] += 16 * len(pieces)
            units.append((name, pieces, slots, posted[slots[0]]))

        views = {}
        fence = {}

        def unit(name, src, kt, cols, parts=P, slot=None, pieces=None):
            s = next_slot[0] if slot is None else slot
            next_slot[0] = (s + 1) % SLOTS
            views[name] = (s,), parts, kt, cols
            place(name, (s,), [(src, None)] if pieces is None else pieces(unit_view_at(name)))

        def unit_view_at(name):
            return slot_view(*views[name])

        def unit_view(name):
            return slot_view(*views[name])

        def weights(pe, name, last_job=None):
            n = unit_at[name]
            _, _, slots, value = units[n]
            pe.wait_ge(arrived[slots[0]], value)
            if last_job is not None:
                released[n] = last_job
            return unit_view(name)

        def stream(sp, names):
            for name in names:
                n = unit_at[name]
                _, pieces, slots, _ = units[n]
                for m in sorted(waits_for[n]):
                    r = released[m]
                    if isinstance(r, str):
                        ring, k = jobs[r]
                        r = (full[ring], k + 1)
                    sp.wait_ge(*r)
                if slots[0] >= SLOTS or name.startswith("f1"):
                    for job in fence.get(name.split(".")[0], ()):
                        ring, k = jobs[job if job in jobs else "cols"]
                        sp.wait_ge(full[ring], k + 1)
                for src, dst in pieces:
                    sp.dma_start(unit_view(name) if dst is None else dst, src).then_inc(arrived[slots[0]], 16)

        def linear_units(name, w, n_cols, k=D):
            kt = k // P
            for c in range(0, n_cols, 512):
                w_ = min(512, n_cols - c)
                step = max(1, min(kt, SLOT // w_))
                for k0 in range(0, kt, step):
                    unit(f"{name}.{c // 512}.{k0}",
                         w[k0 * P:(k0 + step) * P, c:c + w_].rearrange("(k p) n -> p k n", p=P), step, w_)

        def linear(pe, name, lhsT, n_cols, rings, k=D):
            kt = k // P
            for c in range(0, n_cols, 512):
                w_ = min(512, n_cols - c)
                step = max(1, min(kt, SLOT // w_))
                last = f"{name}.{c // 512}.{T - 1}"
                wv = [weights(pe, f"{name}.{c // 512}.{k0}", last) for k0 in range(0, kt, step)]
                for t in range(T):
                    ps = fill(pe, rings[t], f"{name}.{c // 512}.{t}")
                    for kk in range(kt):
                        mm = nc.tensor.matmul(ps[:, 0:w_], lhsT[:, kk, t * P:(t + 1) * P],
                                              wv[kk // step][:, kk % step, :], start=kk == 0, stop=kk == kt - 1)
                    mm.then_inc(full[rings[t]], 1)

        def chain(eng, name):
            s, n = sem(name), [0]

            def link(ins):
                n[0] += 1
                ins.then_inc(s, 1)
                eng.wait_ge(s, n[0])
            return link

        X = sb("X", [P, T, D])
        const = sb("const", [P, CONSTANTS.shape[1]])
        cols = sb("cols", [P, P + 2])
        neghalf = sb("neghalf", [P, 32])
        rowsmall = sb("rowsmall", [P, 512])
        stat = sb("stat", [P, 256])
        cossin = sb("cossin", [P, T, 2, 64])
        post = sb("post", [P, T], I32)
        WORK = 26496
        EXTRA = 12288
        work = sb("work", [P, WORK])

        def C(name):
            a, b = CONST[name]
            return const[:, a:b]

        ident = C("ident")

        def col(name, n, i=0):
            return cols[:, COL[name] + i:COL[name] + i + n]

        def view(at, *shape):
            n = int(np.prod(shape))
            assert at + n <= WORK, (at, n)
            v = work[:, at:at + n]
            if len(shape) == 2:
                v = v.rearrange("p (a b) -> p a b", a=shape[0])
            elif len(shape) == 3:
                v = v.rearrange("p (a b c) -> p a b c", a=shape[0], b=shape[1])
            elif len(shape) == 4:
                v = v.rearrange("p (a b c d) -> p a b c d", a=shape[0], b=shape[1], c=shape[2])
            return v

        def bc(ap, n, axis):
            v = ap.unsqueeze(axis)
            shape = list(v.shape)
            shape[axis] = n
            return v.to_broadcast(shape)

        hT = view(0, KD, S)
        xn = view(2048, T, D)
        mixT = view(2048, KD, S)
        sq = view(4096, T, D)
        pe_fns, dve_fns, act_fns, pool_fns, sp_fns = [], [], [], [], []
        links = {}

        def norm_act(act, u, src, xn=xn, sq=sq, dst_stat=0):
            for t in range(T):
                nc.scalar.activation(sq[:, t], src[:, t], ACT.Square,
                                     accum_out=stat[:, dst_stat + t:dst_stat + t + 1]).then_inc(sem(f"ss_{u}"), 1)
            for t in range(T):
                act.wait_ge(sem(f"rstd_{u}"), 1)
                nc.scalar.activation(xn[:, t], src[:, t], ACT.Copy,
                                     scale=stat[:, dst_stat + 2 + t:dst_stat + 3 + t]).then_inc(sem(f"xn_{u}"), 1)

        def rsqrt(pool, dst, src, n, mul, eps, done):
            links["pool"](nc.gpsimd.tensor_scalar(dst, src, mul, eps, ALU.mult, ALU.add))
            nc.gpsimd.tensor_tensor(dst, dst, neghalf[:, 0:n], ALU.pow).then_inc(done, 1)

        def norm_pool(pool, u, dst_stat=0):
            pool.wait_ge(sem(f"ss_{u}"), T)
            rsqrt(pool, stat[:, dst_stat + 2:dst_stat + 4], stat[:, dst_stat:dst_stat + 2], 2, 1.0 / D, EPS,
                  sem(f"rstd_{u}"))

        def norm_pe(pe, u, xn=xn):
            for t in range(T):
                pe.wait_ge(sem(f"xn_{u}"), t + 1)
                for half in range(2):
                    ps = fill(pe, "D", f"hT_{u}.{t}.{half}")
                    for k in range(4):
                        kk = half * 4 + k
                        mm = nc.tensor.transpose(ps[:, k * P:(k + 1) * P], xn[:, t, kk * P:(kk + 1) * P], ident)
                    mm.then_inc(full["D"], 1)

        def norm_dve(dve, u, gain, hT=hT, gi=0):
            for t in range(T):
                for half in range(2):
                    ps = take(dve, "D", f"hT_{u}.{t}.{half}")
                    nc.vector.tensor_tensor(hT[:, half * 4:half * 4 + 4, t * P:(t + 1) * P],
                                            ps[:, :].rearrange("p (k n) -> p k n", k=4),
                                            bc(col(gain, 4, gi + half * 4), P, 2), ALU.mult).then_inc(moved["D"], 1)

        def hT_jobs(u):
            return [f"hT_{u}.{t}.{h}" for t in range(T) for h in range(2)]

        rows_in = view(18100, P)
        n_const1 = CONST["invf"][1]
        q_g, k_g, bias_e, bias_g, fbias = (rowsmall[:, 0:QK], rowsmall[:, QK:2 * QK], rowsmall[:, 384:416],
                                           rowsmall[:, 416:420], rowsmall[:, 420:428])

        def start_sp(sp):
            sp.dma_start(X[:, :, :], A["x"][0].rearrange("(t p) d -> p t d", p=P)).then_inc(sem("x_in"), 16)
            if "B" in phases:
                sp.dma_start(mem, A["mem"][0].rearrange("(t p) d -> p t d", p=P)).then_inc(sem("mem_in"), 16)
            sp.dma_start(const[:, 0:n_const1], A["const_table"][:, 0:n_const1]).then_inc(sem("const_in"), 16)

        def start_act_dma(act):
            n = 0
            for name, r in ROWS:
                src = A[name]
                flat = src.rearrange(" ".join("abc"[:len(src.shape)]) + " -> (" + " ".join("abc"[:len(src.shape)]) + ")") \
                    if len(src.shape) > 1 else src
                act.dma_start(rows_in[COL[name]:COL[name] + r, :],
                              flat.rearrange("(r c) -> r c", c=P)).then_inc(sem("rows_in"), 16)

        def start_pool_dma(pool):
            for t in range(T):
                pool.dma_start(post[:, t:t + 1], A["positions"][0, t * P:(t + 1) * P].unsqueeze(1)).then_inc(sem("pos_in"), 16)
            for dst, name in ((q_g, "mla_q_qk_g"), (k_g, "mla_k_qk_g"), (bias_e, "router_b_expert"),
                              (bias_g, "router_b_group"), (fbias, "hy_f_bias_2")):
                pool.dma_start(dst, A[name].to_broadcast([P, dst.shape[1]])).then_inc(sem("rowsmall_in"), 16)
            for i, name in enumerate(("hy_q_gain_2", "hy_k_gain_2")):
                for half in range(2):
                    pool.dma_start(cols[half * HD:(half + 1) * HD, P + i:P + i + 1],
                                   A[name][0].unsqueeze(1)).then_inc(sem("gain2_in"), 16)
            pool.dma_start(const[:, n_const1:], A["const_table"][:, n_const1:]).then_inc(sem("const2_in"), 16)
            nc.gpsimd.memset(neghalf[:, :], -0.5).then_inc(sem("neghalf"), 1)
            pool.wait_ge(sem("neghalf"), 1)

        def start_pe(pe):
            pe.wait_ge(sem("const_in"), 16)
            pe.wait_ge(sem("rows_in"), 16 * len(ROWS))
            ps = fill(pe, "D", "cols")
            nc.tensor.transpose(ps[:, 0:NROWS], rows_in[0:NROWS, :], ident[0:NROWS, 0:NROWS]).then_inc(full["D"], 1)

        def start_dve(dve):
            ps = take(dve, "D", "cols")
            nc.vector.tensor_copy(cols[:, 0:NROWS], ps[:, 0:NROWS]).then_inc(moved["D"], 1)
            dve.wait_ge(moved["D"], 1)

        ang = view(18300, 8, 64)

        def rotary_dve(dve):
            L = links["dve"]
            dve.wait_ge(sem("pos_in"), 32)
            dve.wait_ge(sem("const_in"), 16)
            L(nc.vector.tensor_copy(stat[:, 8:8 + T], post[:, :]))
            turns_i = ang[:, 4:8].bitcast(I32)
            for t in range(T):
                L(nc.vector.tensor_scalar(ang[:, 2 * t], C("invf"), stat[:, 8 + t:9 + t], None, ALU.mult))
                L(nc.vector.tensor_scalar(ang[:, 2 * t + 1], ang[:, 2 * t], float(np.pi / 2), None, ALU.add))
            L(nc.vector.tensor_scalar(ang[:, 4:8], ang[:, 0:4], float(1 / (2 * np.pi)), None, ALU.mult))
            L(nc.vector.tensor_copy(turns_i, ang[:, 4:8]))
            L(nc.vector.tensor_copy(ang[:, 4:8], turns_i))
            c1 = 6.28125
            c2 = float(np.float32(2 * np.pi - c1))
            c2h = float(np.float32(np.round((2 * np.pi - c1) * 2 ** 20) / 2 ** 20))
            for c in (c1, c2h, 2 * np.pi - c1 - c2h):
                L(nc.vector.scalar_tensor_tensor(ang[:, 0:4], ang[:, 4:8], -float(c), ang[:, 0:4], ALU.mult, ALU.add))
            L(nc.vector.tensor_scalar(ang[:, 0:4], ang[:, 0:4], 3.1415925, -3.1415925, ALU.min, ALU.max))
            nc.vector.tensor_copy(cossin[:, :, :, :], ang[:, 0:4].rearrange("p (t c) n -> p t c n", t=T)) \
                .then_inc(sem("angles"), 1)

        def rotary_act(act):
            act.wait_ge(sem("angles"), 1)
            nc.scalar.activation(cossin[:, :, :, :], cossin[:, :, :, :], ACT.Sin).then_inc(sem("cossin"), 1)

        sin_t = lambda t: cossin[:, t, 0]
        cos_t = lambda t: cossin[:, t, 1]

        def rope(eng, ve, link, x, n, half, t, scratch, step, done=None):
            cs, sn = bc(cos_t(t)[:, ::step], n, 1), bc(sin_t(t)[:, ::step], n, 1)
            x1, x2 = x[:, :, 0:half], x[:, :, half:2 * half]
            m = [scratch[:, i * n * half:(i + 1) * n * half].rearrange("p (a b) -> p a b", a=n) for i in range(4)]
            ve.tensor_tensor(m[0], x1, cs, ALU.mult)
            ve.tensor_tensor(m[1], x2, sn, ALU.mult)
            ve.tensor_tensor(m[2], x2, cs, ALU.mult)
            link(ve.tensor_tensor(m[3], x1, sn, ALU.mult))
            ve.tensor_tensor(x1, m[0], m[1], ALU.subtract)
            last = ve.tensor_tensor(x2, m[2], m[3], ALU.add)
            if done is not None:
                last.then_inc(done, 1)
            else:
                link(last)

        proj = view(6912, T, IN1)
        qk = view(11904, T, 2, H, QK)
        val = view(14976, T, H, VD)
        cn = view(16000, T, QR + KVR)
        cT = view(16768, 3, S)
        nopeT = view(17536, 2, H, S)
        ropeT = view(19584, 2, H, S)
        sc = view(11904, H, 3 * P)
        prT = view(13440, H, 3 * P)
        rqkT = view(17536, 2, H, S)
        rsc = view(19584, H, 3 * P)
        ro = view(4096, T, H, P)
        scr = view(4096, 2048)
        O = dict(cq=0, ckv=QR, kpe=QR + KVR, rq=448, rk=960, rv=1472, rg=1984)

        mem = view(11904, T, D)
        memx = view(13952, T, D)
        memsq = view(16000, T, D)
        memkv = view(22400, T, 2 * D)
        mT = view(17536, KD, S)

        if "A" in phases:
            linear_units("w_in", dram2("w_in"), IN1)
            unit("w_uq", A["mla_w_uq"][0].rearrange("(k p) n -> p k n", p=P), 2, H * QK)
            unit("w_ukv", A["mla_w_ukv"][0].rearrange("(k p) n -> p k n", p=P), 1, H * 2 * P)
            if "B" in phases:
                linear_units("w_kv", dram2("cross_w_kv"), 2 * D)
            linear_units("w_out", dram2("w_out"), D)

        def mixA_pe(pe):
            norm_pe(pe, "a")
            if "B" in phases:
                norm_pe(pe, "m", memx)
            await_moved(pe, *hT_jobs("a"))
            linear(pe, "w_in", hT, IN1, "AD")
            for t in range(T):
                pe.wait_ge(sem("cn"), 2 * (t + 1))
                ps = fill(pe, "D", f"cT.{t}")
                for k in range(3):
                    mm = nc.tensor.transpose(ps[:, k * P:(k + 1) * P], cn[:, t, k * P:(k + 1) * P], ident)
                mm.then_inc(full["D"], 1)
            await_moved(pe, "cT.1")
            uq, ukv = weights(pe, "w_uq", "uq.1.1"), weights(pe, "w_ukv", "ukv.1.1")
            for c, w_ in ((0, 512), (1, 256)):
                for t in range(T):
                    ps = fill(pe, "AD"[t], f"uq.{c}.{t}")
                    for k in range(2):
                        mm = nc.tensor.matmul(ps[:, 0:w_], cT[:, k, t * P:(t + 1) * P], uq[:, k, c * 512:c * 512 + w_],
                                              start=k == 0, stop=k == 1)
                    mm.then_inc(full["AD"[t]], 1)
            for c in range(2):
                for t in range(T):
                    ps = fill(pe, "AD"[t], f"ukv.{c}.{t}")
                    nc.tensor.matmul(ps[:, :], cT[:, 2, t * P:(t + 1) * P], ukv[:, 0, c * 512:(c + 1) * 512],
                                     start=True, stop=True).then_inc(full["AD"[t]], 1)
            if "B" in phases:
                await_moved(pe, *hT_jobs("m"))
                linear(pe, "w_kv", mT, 2 * D, "AA")
            pe.wait_ge(sem("qk_ready"), T)
            for j in range(2):
                for hp in range(2):
                    ps = fill(pe, "AD"[hp], f"nopeT.{j}.{hp}")
                    for h in range(2):
                        for t in range(T):
                            mm = nc.tensor.transpose(ps[:, h * S + t * P:h * S + (t + 1) * P],
                                                     qk[:, t, j, 2 * hp + h, 0:ND], ident)
                    mm.then_inc(full["AD"[hp]], 1)
                for hp in range(2):
                    ps = fill(pe, "AD"[hp], f"ropeT.{j}.{hp}")
                    for h in range(2):
                        for t in range(T):
                            mm = nc.tensor.transpose(ps[0:RD, h * S + t * P:h * S + (t + 1) * P],
                                                     qk[:, t, j, 2 * hp + h, ND:QK], ident)
                    mm.then_inc(full["AD"[hp]], 1)
            await_moved(pe, "ropeT.1.0", "ropeT.1.1")
            for h in range(H):
                ps = fill(pe, "D", f"score.{h}")
                for lo, hi, n in ((0, P, P), (P, 3 * P, S)):
                    tq = lo // P
                    nc.tensor.matmul(ps[:, lo:hi], nopeT[:, 0, h, tq * P:(tq + 1) * P], nopeT[:, 1, h, 0:n],
                                     start=True, stop=False)
                    mm = nc.tensor.matmul(ps[:, lo:hi], ropeT[0:RD, 0, h, tq * P:(tq + 1) * P],
                                          ropeT[0:RD, 1, h, 0:n], start=False, stop=True)
                mm.then_inc(full["D"], 1)
            pe.wait_ge(sem("rqk_ready"), T)
            for j in range(2):
                for hp in range(2):
                    ps = fill(pe, "A", f"rqkT.{j}.{hp}")
                    for h in range(2):
                        for t in range(T):
                            o = O["rq"] + j * 512 + (2 * hp + h) * P
                            mm = nc.tensor.transpose(ps[:, h * S + t * P:h * S + (t + 1) * P],
                                                     proj[:, t, o:o + P], ident)
                    mm.then_inc(full["A"], 1)
            pe.wait_ge(sem("prob"), T)
            for h in range(H):
                ps = fill(pe, "A", f"prT.{h}")
                for b in range(3):
                    mm = nc.tensor.transpose(ps[:, b * P:(b + 1) * P], sc[:, h, b * P:(b + 1) * P], ident)
                mm.then_inc(full["A"], 1)
            await_moved(pe, "rqkT.1.1")
            for h in range(H):
                ps = fill(pe, "D", f"rscore.{h}")
                nc.tensor.matmul(ps[:, 0:S], rqkT[:, 1, h, 0:P], rqkT[:, 0, h, :], start=True, stop=True)
                nc.tensor.matmul(ps[:, S:3 * P], rqkT[:, 1, h, P:S], rqkT[:, 0, h, P:S],
                                 start=True, stop=True).then_inc(full["D"], 1)
            await_moved(pe, "prT.3")
            for hp in range(2):
                ps = fill(pe, "A", f"oT.{hp}")
                for h in (2 * hp, 2 * hp + 1):
                    o = (h % 2) * S
                    nc.tensor.matmul(ps[:, o:o + S], val[:, 0, h], prT[:, h, 0:S], start=True, stop=False)
                    mm = nc.tensor.matmul(ps[:, o + P:o + S], val[:, 1, h], prT[:, h, S:3 * P], start=False, stop=True)
                mm.then_inc(full["A"], 1)
            await_moved(pe, "rscore.3")
            rv = lambda t, h: proj[:, t, O["rv"] + h * P:O["rv"] + (h + 1) * P]
            for t in range(T):
                ps = fill(pe, "D", f"ro.{t}")
                for h in range(H):
                    o = slice(h * P, (h + 1) * P)
                    if t == 0:
                        mm = nc.tensor.matmul(ps[:, o], rsc[:, h, 0:P], rv(0, h), start=True, stop=True)
                    else:
                        nc.tensor.matmul(ps[:, o], rsc[:, h, P:S], rv(0, h), start=True, stop=False)
                        mm = nc.tensor.matmul(ps[:, o], rsc[:, h, S:3 * P], rv(1, h), start=False, stop=True)
                mm.then_inc(full["D"], 1)
            for t in range(T):
                pe.wait_ge(sem("ro_gated"), t + 1)
                ps = fill(pe, "D", f"roT.{t}")
                for h in range(H):
                    mm = nc.tensor.transpose(ps[:, h * P:(h + 1) * P], ro[:, t, h], ident)
                mm.then_inc(full["D"], 1)
            await_moved(pe, "roT.1", "oT.1")
            linear(pe, "w_out", mixT, D, "DD")

        def copy_chunk_act(act, name, dst):
            ps = take(act, "A", name)
            nc.scalar.copy(dst, ps[:, 0:dst.shape[1]] if len(dst.shape) == 2 else
                           ps[:, 0:dst.shape[1] * dst.shape[2]].rearrange("p (a b) -> p a b", a=dst.shape[1])
                           ).then_inc(moved["A"], 1)

        def copy_chunk_dve(dve, name, dst):
            ps = take(dve, "D", name)
            nc.vector.tensor_copy(dst, ps[:, 0:dst.shape[1]] if len(dst.shape) == 2 else
                                  ps[:, 0:dst.shape[1] * dst.shape[2]].rearrange("p (a b) -> p a b", a=dst.shape[1])
                                  ).then_inc(moved["D"], 1)

        def mixA_act(act):
            norm_act(act, "a", X)
            if "B" in phases:
                act.wait_ge(sem("mem_in"), 16)
                norm_act(act, "m", mem, memx, memsq, 24)
            rotary_act(act)
            for c in range(5):
                w_ = min(512, IN1 - c * 512)
                copy_chunk_act(act, f"w_in.{c}.0", proj[:, 0, c * 512:c * 512 + w_])
                if c == 0:
                    await_moved(act, "w_in.0.0", "w_in.0.1")
                    for t in range(T):
                        for i, (o, w2) in enumerate(((0, QR), (QR, KVR))):
                            nc.scalar.activation(sq[:, t, o:o + w2], proj[:, t, o:o + w2], ACT.Square,
                                                 accum_out=stat[:, 16 + 2 * i + t:17 + 2 * i + t]).then_inc(sem("ss_lat"), 1)
            await_moved(act, "w_in.4.0", "w_in.4.1")
            rg = proj[:, :, O["rg"]:O["rg"] + RW]
            nc.scalar.activation(rg, rg, ACT.Silu).then_inc(sem("gate"), 1)
            for c, w_ in ((0, 512), (1, 256)):
                ps = take(act, "A", f"uq.{c}.0")
                nc.scalar.copy(qk[:, 0, 0].rearrange("p h d -> p (h d)")[:, c * 512:c * 512 + w_], ps[:, 0:w_]).then_inc(moved["A"], 1)
            for c in range(2):
                ps = take(act, "A", f"ukv.{c}.0")
                v = ps[:, :].rearrange("p (h d) -> p h d", h=2)
                nc.scalar.copy(qk[:, 0, 1, 2 * c:2 * c + 2, 0:ND], v[:, :, 0:ND])
                nc.scalar.copy(val[:, 0, 2 * c:2 * c + 2], v[:, :, ND:]).then_inc(moved["A"], 1)
            if "B" in phases:
                for c in range(4):
                    for t in range(T):
                        copy_chunk_act(act, f"w_kv.{c}.{t}", memkv[:, t, c * 512:(c + 1) * 512])
            for j in range(2):
                for kind, dst, n in (("nopeT", nopeT, P), ("ropeT", ropeT, RD)):
                    ps = take(act, "A", f"{kind}.{j}.0")
                    nc.scalar.copy(dst[0:n, j, 0:2], ps[0:n, :].rearrange("p (a b) -> p a b", a=2)).then_inc(moved["A"], 1)
            act.wait_ge(sem("nmax"), 1)
            for h in range(H):
                for t, (lo, hi) in enumerate(((0, P), (P, 3 * P))):
                    nc.scalar.activation(sc[:, h, lo:hi], sc[:, h, lo:hi], ACT.Exp, bias=stat[:, 40 + 4 * t + h:41 + 4 * t + h],
                                         accum_out=stat[:, 48 + 4 * t + h:49 + 4 * t + h]).then_inc(sem("exp"), 1)
            await_moved(act, "score.3")
            for j in range(2):
                for hp in range(2):
                    copy_chunk_act(act, f"rqkT.{j}.{hp}", rqkT[:, j, 2 * hp:2 * hp + 2])
            for h in range(H):
                copy_chunk_act(act, f"prT.{h}", prT[:, h])
            for hp in range(2):
                copy_chunk_act(act, f"oT.{hp}", mixT[:, 2 * hp:2 * hp + 2])

        def mixA_pool(pool):
            norm_pool(pool, "a")
            if "B" in phases:
                norm_pool(pool, "m", 24)
            pool.wait_ge(sem("ss_lat"), 4)
            links["pool"](nc.gpsimd.tensor_scalar(stat[:, 20:22], stat[:, 16:18], 1.0 / QR, EPS, ALU.mult, ALU.add))
            links["pool"](nc.gpsimd.tensor_scalar(stat[:, 22:24], stat[:, 18:20], 1.0 / KVR, EPS, ALU.mult, ALU.add))
            nc.gpsimd.tensor_tensor(stat[:, 20:24], stat[:, 20:24], neghalf[:, 0:4], ALU.pow).then_inc(sem("rstd_lat"), 1)
            pool.wait_ge(sem("ss_qk"), 1)
            rsqrt(pool, stat[:, 80:96], stat[:, 64:80], 16, 1.0 / QK, EPS, sem("rstd_qk"))
            pool.wait_ge(sem("ro_var"), 1)
            rsqrt(pool, stat[:, 112:120], stat[:, 96:104], 8, 1.0, EPS, sem("ro_rstd"))

        def mixA_dve(dve):
            L = links["dve"]
            rotary_dve(dve)
            norm_dve(dve, "a", "attn_norm_g")
            if "B" in phases:
                norm_dve(dve, "m", "mem_norm_g", mT)
            for c in range(5):
                w_ = min(512, IN1 - c * 512)
                copy_chunk_dve(dve, f"w_in.{c}.1", proj[:, 1, c * 512:c * 512 + w_])
                if c == 1:
                    dve.wait_ge(sem("rstd_lat"), 1)
                    await_moved(dve, "w_in.0.1")
                    for t in range(T):
                        nc.vector.tensor_scalar(cn[:, t, 0:QR], proj[:, t, 0:QR], stat[:, 20 + t:21 + t], None,
                                                ALU.mult).then_inc(sem("cn"), 1)
                        nc.vector.tensor_scalar(cn[:, t, QR:], proj[:, t, QR:QR + KVR], stat[:, 22 + t:23 + t], None,
                                                ALU.mult).then_inc(sem("cn"), 1)
            for t in range(T):
                ps = take(dve, "D", f"cT.{t}")
                nc.vector.tensor_tensor(cT[:, :, t * P:(t + 1) * P], ps[:, 0:3 * P].rearrange("p (k n) -> p k n", k=3),
                                        bc(col("mla_q_norm_g", 3), P, 2), ALU.mult).then_inc(moved["D"], 1)
            for c, w_ in ((0, 512), (1, 256)):
                ps = take(dve, "D", f"uq.{c}.1")
                nc.vector.tensor_copy(qk[:, 1, 0].rearrange("p h d -> p (h d)")[:, c * 512:c * 512 + w_], ps[:, 0:w_]).then_inc(moved["D"], 1)
            for c in range(2):
                ps = take(dve, "D", f"ukv.{c}.1")
                v = ps[:, :].rearrange("p (h d) -> p h d", h=2)
                nc.vector.tensor_copy(qk[:, 1, 1, 2 * c:2 * c + 2, 0:ND], v[:, :, 0:ND])
                nc.vector.tensor_copy(val[:, 1, 2 * c:2 * c + 2], v[:, :, ND:]).then_inc(moved["D"], 1)
            await_moved(dve, "ukv.1.0", "ukv.1.1")
            for t in range(T):
                L(nc.vector.tensor_copy(qk[:, t, 1, :, ND:], bc(proj[:, t, O["kpe"]:O["kpe"] + RD], H, 1)))
            for t in range(T):
                q_ = qk[:, t].rearrange("p j h d -> p (j h) d")
                s_ = scr[:, 0:8 * QK].rearrange("p (a b) -> p a b", a=8)
                L(nc.vector.tensor_tensor(s_, q_, q_, ALU.mult))
                r = nc.vector.reduce_sum(stat[:, 64 + 8 * t:72 + 8 * t], s_, AX.X)
                if t == 0:
                    L(r)
                else:
                    r.then_inc(sem("ss_qk"), 1)
            dve.wait_ge(sem("rowsmall_in"), 80)
            L(nc.vector.tensor_scalar(q_g, q_g, QK ** -0.5, None, ALU.mult))
            dve.wait_ge(sem("rstd_qk"), 1)
            dve.wait_ge(sem("cossin"), 1)
            for t in range(T):
                q_ = qk[:, t].rearrange("p j h d -> p (j h) d")
                L(nc.vector.tensor_tensor(q_, q_, bc(stat[:, 80 + 8 * t:88 + 8 * t], QK, 2), ALU.mult))
                for j, g_ in enumerate((q_g, k_g)):
                    L(nc.vector.tensor_tensor(qk[:, t, j], qk[:, t, j], bc(g_, H, 1), ALU.mult))
                rope(dve, nc.vector, L, q_[:, :, ND:], 8, RD // 2, t, scr, 2, sem("qk_ready"))
                dve.wait_ge(sem("qk_ready"), t + 1)
            for j in range(2):
                for kind, dst, n in (("nopeT", nopeT, P), ("ropeT", ropeT, RD)):
                    ps = take(dve, "D", f"{kind}.{j}.1")
                    nc.vector.tensor_copy(dst[0:n, j, 2:4], ps[0:n, :].rearrange("p (a b) -> p a b", a=2)).then_inc(moved["D"], 1)
            await_moved(dve, "w_in.4.0", "w_in.4.1")
            for t in range(T):
                rope(dve, nc.vector, L, proj[:, t, O["rq"]:O["rq"] + 1024].rearrange("p (a b) -> p a b", a=8), 8, 64, t,
                     view(4096, 2048) if t == 0 else scr, 1, sem("rqk_ready"))
                dve.wait_ge(sem("rqk_ready"), t + 1)
            await_moved(dve, "ropeT.1.0", "ropeT.1.1")
            for h in range(H):
                ps = take(dve, "D", f"score.{h}")
                nc.vector.tensor_tensor(sc[:, h], ps[:, 0:3 * P], C("cmask"), ALU.add).then_inc(moved["D"], 1)
            await_moved(dve, "score.3")
            L(nc.vector.tensor_reduce(stat[:, 40:44], sc[:, :, 0:P], AX.X, ALU.max, negate=True))
            nc.vector.tensor_reduce(stat[:, 44:48], sc[:, :, P:], AX.X, ALU.max, negate=True).then_inc(sem("nmax"), 1)
            dve.wait_ge(sem("exp"), 8)
            L(nc.vector.reciprocal(stat[:, 56:64], stat[:, 48:56]))
            for t, (lo, hi) in enumerate(((0, P), (P, 3 * P))):
                nc.vector.tensor_tensor(sc[:, :, lo:hi], sc[:, :, lo:hi], bc(stat[:, 56 + 4 * t:60 + 4 * t], hi - lo, 2),
                                        ALU.mult).then_inc(sem("prob"), 1)
            for h in range(H):
                ps = take(dve, "D", f"rscore.{h}")
                nc.vector.tensor_tensor(rsc[:, h], ps[:, 0:3 * P],
                                        C("decay")[:, h * 3 * P:(h + 1) * 3 * P], ALU.mult).then_inc(moved["D"], 1)
            for t in range(T):
                ps = take(dve, "D", f"ro.{t}")
                nc.vector.tensor_copy(ro[:, t].rearrange("p h d -> p (h d)"), ps[:, :]).then_inc(moved["D"], 1)
            await_moved(dve, "ro.1")
            bn = stat[:, 128:176].rearrange("p (a b) -> p a b", a=8)
            mv = stat[:, 176:192].rearrange("p (a b) -> p a b", a=8)
            for i in range(8):
                last = nc.vector.bn_stats(bn[:, i], ro[:, i // 4, i % 4])
            L(last)
            for i in range(8):
                last = nc.vector.bn_aggr(mv[:, i], bn[:, i])
            L(last)
            nc.vector.tensor_copy(stat[:, 96:104], mv[:, :, 1]).then_inc(sem("ro_var"), 1)
            dve.wait_ge(sem("ro_rstd"), 1)
            dve.wait_ge(sem("gate"), 1)
            for t in range(T):
                for h in range(H):
                    i = 4 * t + h
                    last = nc.vector.tensor_scalar(ro[:, t, h], ro[:, t, h], mv[:, i, 0:1], stat[:, 112 + i:113 + i],
                                                   ALU.subtract, ALU.mult)
                L(last)
                nc.vector.tensor_tensor(ro[:, t].rearrange("p h d -> p (h d)"), ro[:, t].rearrange("p h d -> p (h d)"),
                                        proj[:, t, O["rg"]:O["rg"] + RW], ALU.mult).then_inc(sem("ro_gated"), 1)
            for t in range(T):
                ps = take(dve, "D", f"roT.{t}")
                nc.vector.tensor_tensor(mixT[:, 4:8, t * P:(t + 1) * P], ps[:, :].rearrange("p (k n) -> p k n", k=4),
                                        bc(col("ret_gn_g", 4), P, 2), ALU.mult).then_inc(moved["D"], 1)
            residual_dve(dve, "w_out")

        def residual_dve(dve, name):
            for c in range(2):
                for t in range(T):
                    ps = take(dve, "D", f"{name}.{c}.{t}")
                    nc.vector.tensor_tensor(X[:, t, c * 512:(c + 1) * 512], X[:, t, c * 512:(c + 1) * 512], ps[:, :],
                                            ALU.add).then_inc(moved["D"], 1)

        def residual_jobs(name):
            return [f"{name}.{c}.{t}" for c in range(2) for t in range(T)] if f"{name}.0.0" in jobs else []

        pe_fns.append(("A", mixA_pe)); act_fns.append(("A", mixA_act))
        pool_fns.append(("A", mixA_pool)); dve_fns.append(("A", mixA_dve))

        DH = D // H
        cq = view(6912, T, D)
        ckT = view(8960, KD, S)
        cqT = view(11008, KD, S)
        csc = view(13056, H, T, S)
        cprT = view(15104, H, T, S)
        if "B" in phases:
            linear_units("w_cq", dram2("cross_w_q"), D)
            linear_units("w_co", dram2("cross_w_o"), D)

        def heads_act(act, u, src, n, at, sq=sq):
            w_ = src.shape[2] // n
            for t in range(T):
                if t and sq.shape[1] == 1:
                    act.wait_ge(sem(f"ss_{u}"), n * t)
                for h in range(n):
                    nc.scalar.activation(sq[:, t % sq.shape[1], h * w_:(h + 1) * w_], src[:, t, h * w_:(h + 1) * w_], ACT.Square,
                                         accum_out=stat[:, at + n * t + h:at + n * t + h + 1]).then_inc(sem(f"ss_{u}"), 1)

        def cross_pe(pe):
            norm_T = lambda name, src: [transposed(pe, "D", f"{name}.{t}.{half}", src, t, half)
                                        for t in range(T) for half in range(2)]
            pe.wait_ge(sem("ck_scaled"), 1)
            norm_T("ckT", memkv)
            norm_pe(pe, "b")
            await_moved(pe, *hT_jobs("b"))
            linear(pe, "w_cq", hT, D, "AD")
            pe.wait_ge(sem("cq_scaled"), 1)
            norm_T("cqT", cq)
            await_moved(pe, "cqT.1.1")
            for h in range(H):
                ps = fill(pe, "D", f"cscore.{h}")
                for t in range(T):
                    for k in range(2):
                        mm = nc.tensor.matmul(ps[:, t * S:(t + 1) * S], cqT[:, 2 * h + k, t * P:(t + 1) * P],
                                              ckT[:, 2 * h + k, :], start=k == 0, stop=k == 1)
                mm.then_inc(full["D"], 1)
            for h in range(H):
                pe.wait_ge(sem("cprob"), h + 1)
                ps = fill(pe, "A", f"cprT.{h}")
                for m in range(T):
                    for t in range(T):
                        mm = nc.tensor.transpose(ps[:, m * S + t * P:m * S + (t + 1) * P],
                                                 csc[:, h, t, m * P:(m + 1) * P], ident)
                mm.then_inc(full["A"], 1)
            for h in range(H):
                await_moved(pe, f"cprT.{h}")
                ps = fill(pe, "A", f"coT.{h}")
                for d in range(2):
                    for m in range(T):
                        o = D + h * DH + d * P
                        mm = nc.tensor.matmul(ps[:, d * S:(d + 1) * S], memkv[:, m, o:o + P], cprT[:, h, m],
                                              start=m == 0, stop=m == 1)
                mm.then_inc(full["A"], 1)
            await_moved(pe, "coT.3")
            linear(pe, "w_co", mixT, D, "DD")

        def transposed(pe, ring, name, src, t, half):
            ps = fill(pe, ring, name)
            for k in range(4):
                o = (half * 4 + k) * P
                mm = nc.tensor.transpose(ps[:, k * P:(k + 1) * P], src[:, t, o:o + P], ident)
            mm.then_inc(full[ring], 1)

        def cross_act(act):
            await_moved(act, "w_kv.3.1")
            heads_act(act, "ck", memkv[:, :, 0:D], H, 192, view(16000, 1, D))
            await_moved(act, *residual_jobs("w_out"))
            norm_act(act, "b", X)
            for c in range(2):
                copy_chunk_act(act, f"w_cq.{c}.0", cq[:, 0, c * 512:(c + 1) * 512])
            await_moved(act, "w_cq.1.0", "w_cq.1.1")
            heads_act(act, "cq", cq, H, 208)
            for h in range(H):
                act.wait_ge(sem("cnmax"), h + 1)
                for t in range(T):
                    nc.scalar.activation(csc[:, h, t], csc[:, h, t], ACT.Exp,
                                         bias=stat[:, 224 + 2 * h + t:225 + 2 * h + t],
                                         accum_out=stat[:, 232 + 2 * h + t:233 + 2 * h + t]).then_inc(sem("cexp"), 1)
            for h in range(H):
                copy_chunk_act(act, f"cprT.{h}", cprT[:, h])
            for h in range(H):
                copy_chunk_act(act, f"coT.{h}", mixT[:, 2 * h:2 * h + 2])

        def cross_pool(pool):
            pool.wait_ge(sem("ss_ck"), 8)
            rsqrt(pool, stat[:, 200:208], stat[:, 192:200], 8, 1.0 / DH, EPS, sem("rstd_ck"))
            norm_pool(pool, "b")
            pool.wait_ge(sem("ss_cq"), 8)
            rsqrt(pool, stat[:, 216:224], stat[:, 208:216], 8, 1.0, 256 * EPS, sem("rstd_cq"))

        def scale_heads(dve, x, n, at, done):
            for t in range(T):
                v = x[:, t].rearrange("p (h d) -> p h d", h=n)
                last = nc.vector.tensor_tensor(v, v, bc(stat[:, at + n * t:at + n * (t + 1)], v.shape[2], 2), ALU.mult)
            last.then_inc(done, 1)

        def headsT_dve(dve, name, dst, gain):
            for t in range(T):
                for half in range(2):
                    ps = take(dve, "D", f"{name}.{t}.{half}")
                    for j in range(2):
                        i = nc.vector.tensor_tensor(dst[:, half * 4 + j:half * 4 + 4:2, t * P:(t + 1) * P],
                                                    ps[:, :].rearrange("p (k n) -> p k n", k=4)[:, j::2],
                                                    bc(bc(col(gain, 1, j)[:, 0], 2, 1), P, 2), ALU.mult)
                    i.then_inc(moved["D"], 1)

        def cross_dve(dve):
            L = links["dve"]
            dve.wait_ge(sem("rstd_ck"), 1)
            scale_heads(dve, memkv[:, :, 0:D], H, 200, sem("ck_scaled"))
            headsT_dve(dve, "ckT", ckT, "cross_k_qk_g")
            norm_dve(dve, "b", "cross_norm_g")
            for c in range(2):
                copy_chunk_dve(dve, f"w_cq.{c}.1", cq[:, 1, c * 512:(c + 1) * 512])
            dve.wait_ge(sem("rstd_cq"), 1)
            scale_heads(dve, cq, H, 216, sem("cq_scaled"))
            headsT_dve(dve, "cqT", cqT, "cross_q_qk_g")
            for h in range(H):
                copy_chunk_dve(dve, f"cscore.{h}", csc[:, h])
                await_moved(dve, f"cscore.{h}")
                nc.vector.tensor_reduce(stat[:, 224 + 2 * h:226 + 2 * h], csc[:, h], AX.X, ALU.max,
                                        negate=True).then_inc(sem("cnmax"), 1)
            for h in range(H):
                dve.wait_ge(sem("cexp"), 2 * h + 2)
                r = stat[:, 240 + 2 * h:242 + 2 * h]
                L(nc.vector.reciprocal(r, stat[:, 232 + 2 * h:234 + 2 * h]))
                nc.vector.tensor_tensor(csc[:, h], csc[:, h], bc(r, S, 2), ALU.mult).then_inc(sem("cprob"), 1)
            residual_dve(dve, "w_co")

        pe_fns.append(("B", cross_pe)); act_fns.append(("B", cross_act))
        pool_fns.append(("B", cross_pool)); dve_fns.append(("B", cross_dve))

        sil = view(8576, 2, FF)
        actv = view(9088, 2, FF)
        actT = view(9600, 2, 2, P)
        GU_SLOTS = ((0, 1), (2, 3), (8, 9), (10, 11))
        D_SLOTS = (4, 5, 6, 7)

        def ffn_units(name, chunks, gate, up, down):
            for c in chunks:
                views[f"{name}.gu.{c}"] = GU_SLOTS[c % 4], P, KD, 2 * FF
                v = unit_view(f"{name}.gu.{c}")
                place(f"{name}.gu.{c}", GU_SLOTS[c % 4],
                      [(gate(c).rearrange("(k p) n -> p k n", p=P), v[:, :, 0:FF]),
                       (up(c).rearrange("(k p) n -> p k n", p=P), v[:, :, FF:])])
                views[f"{name}.d.{c}"] = (D_SLOTS[c % 4],), P, 2, D
                place(f"{name}.d.{c}", (D_SLOTS[c % 4],), [(down(c).rearrange("(k p) n -> p k n", p=P), None)])

        def gu_pe(pe, u, i, gu, hTile, middle, o=""):
            ps = fill(pe, "GU" + o, f"{u}.gu.{i}")
            for k in range(KD):
                mm = nc.tensor.matmul(ps[:, :], hTile(k), gu[:, k, :], start=k == 0, stop=k == KD - 1)
                if k == KD // 2 - 1 and middle is not None:
                    middle()
            mm.then_inc(full["GU" + o], 1)

        def tr_pe(pe, u, i, o=""):
            await_moved(pe, f"{u}.gu.{i}")
            ps = fill(pe, "TT" + o, f"{u}.T.{i}")
            for k in range(2):
                mm = nc.tensor.transpose(ps[:, k * P:(k + 1) * P], actv[:, i % 2, k * P:(k + 1) * P], ident)
            mm.then_inc(full["TT" + o], 1)

        def down_pe(pe, u, i, wd, banks, first, last, done):
            await_moved(pe, f"{u}.T.{i}")
            for c in range(2):
                for k in range(2):
                    mm = nc.tensor.matmul(banks[c][:, :], actT[:, i % 2, k], wd[:, k, c * 512:(c + 1) * 512],
                                          start=first and k == 0, stop=last and k == 1)
            mm.then_inc(done, 1)

        def step_act(act, u, i, o=""):
            ps = peek(act, f"{u}.gu.{i}")
            if i >= 2:
                await_moved(act, f"{u}.gu.{i - 2}")
            nc.scalar.activation(sil[:, i % 2], ps[:, 0:FF], ACT.Silu).then_inc(sem(f"silu_{u}"), 1)

        def stepT_act(act, u, i, down_done, o=""):
            ps = take(act, "TT" + o, f"{u}.T.{i}")
            if i >= 2:
                act.wait_ge(down_done, i - 1)
            nc.scalar.copy(actT[:, i % 2].rearrange("p a b -> p (a b)"), ps[:, 0:FF]).then_inc(moved["TT" + o], 1)

        def step_dve(dve, u, i, gate=None, o=""):
            ps = take(dve, "GU" + o, f"{u}.gu.{i}")
            dve.wait_ge(sem(f"silu_{u}"), i + 1)
            if i >= 2:
                peek(dve, f"{u}.T.{i - 2}")
            if gate is None:
                nc.vector.tensor_tensor(actv[:, i % 2], ps[:, FF:], sil[:, i % 2], ALU.mult).then_inc(moved["GU" + o], 1)
            else:
                nc.vector.scalar_tensor_tensor(actv[:, i % 2], ps[:, FF:], gate, sil[:, i % 2],
                                               ALU.mult, ALU.mult).then_inc(moved["GU" + o], 1)

        wr = work[:, 21700:21700 + KD * 36].rearrange("p (k n) -> p k n", k=KD)
        hg = view(4096, 2, KD, P)
        Sel = view(6144, T, G, P)
        SelT = view(7168, G, S)
        ysb = view(10112, 2, D)
        rt = work[:, 20480:20480 + 1000]
        Selo = view(8192 + 0, T, P)
        SelTo = view(21988, S)
        gs = work[:, 8448:8448 + 5 * EPG].rearrange("p (g e) -> p g e", g=5)
        flags = work[:, 8500:8502].bitcast(I32)

        def rtv(at, *shape):
            n = int(np.prod(shape))
            v = rt[:, at:at + n]
            if len(shape) == 2:
                v = v.rearrange("p (a b) -> p a b", a=shape[0])
            if len(shape) == 3:
                v = v.rearrange("p (a b c) -> p a b c", a=shape[0], b=shape[1])
            return v

        logit = rtv(0, T, 36)
        oh = rtv(80, T, G)
        el = rtv(100, T, EPG)
        gate8 = rtv(120, T, EPG)
        rank = rtv(140, T, 2)
        tmp = rtv(150, T, G, EPG)
        tmp8 = rtv(220, T, EPG)
        oh1 = rtv(240, T, EPG)
        oh2 = rtv(260, T, EPG)
        m1 = rtv(280, T, 1)
        m2 = rtv(284, T, 1)
        gw = rtv(288, T, 1)
        gb = rtv(292, T, G)
        ge = rtv(300, T, G)
        ee = rtv(310, T, EPG)
        bias8 = rtv(330, T, EPG)
        cnt = rtv(350, 3, G)
        ovf = rtv(364, G)
        nm = rtv(370, T, 2)
        gsum = rtv(376, T, 2)
        den = rtv(382, T, 1)
        oho = rtv(386, T, 1)
        if "C" in phases:
            eg, eu, ed = A["expert_w_gate"][0], A["expert_w_up"][0], A["expert_w_down"][0]
            fence["moe"] = ("coT.3",)
            ffn_units("moe", range(G * EPG), lambda c: eg[c], lambda c: eu[c], lambda c: ed[c])

        def moe_pe(pe):
            norm_pe(pe, "c")
            await_moved(pe, *hT_jobs("c"))
            pe.wait_ge(sem("wr_in"), 32)
            for t in range(T):
                ps = fill(pe, "D", f"logit.{t}")
                for k in range(KD):
                    mm = nc.tensor.matmul(ps[:, 0:36], hT[:, k, t * P:(t + 1) * P], wr[:, k, :], start=k == 0, stop=k == KD - 1)
                mm.then_inc(full["D"], 1)
            pe.wait_ge(sem("group_picked"), 1)
            pe.wait_ge(sem("const2_in"), 16)
            ps = fill(pe, "D", "rank")
            nc.tensor.matmul(ps[:, 0:G], C("strictP"), oh[:, 0], start=True, stop=True)
            nc.tensor.matmul(ps[:, G:2 * G], C("ones"), oh[:, 0], start=True, stop=False)
            nc.tensor.matmul(ps[:, G:2 * G], C("strictP"), oh[:, 1], start=False, stop=True)
            nc.tensor.matmul(ps[:, 2 * G:3 * G], C("ones"), oh[:, 0], start=True, stop=False)
            nc.tensor.matmul(ps[:, 2 * G:3 * G], C("ones"), oh[:, 1], start=False, stop=True).then_inc(full["D"], 1)
            drained(pe, "D", "A")

            def gather(g, sel, selT_cols, o=""):
                ps = fill(pe, "Z" + o, f"selT.{g}")
                for t in range(T):
                    mm = nc.tensor.transpose(ps[:, t * P:(t + 1) * P], sel(t), ident)
                mm.then_inc(full["Z" + o], 1)
                for half in range(2):
                    ps = fill(pe, "Z" + o, f"hg.{g}.{half}")
                    for k in range(4):
                        for t in range(T):
                            kk = half * 4 + k
                            mm = nc.tensor.matmul(ps[:, k * P:(k + 1) * P], xn[:, t, kk * P:(kk + 1) * P], sel(t),
                                                  start=t == 0, stop=t == 1)
                    mm.then_inc(full["Z" + o], 1)
                ps = fill(pe, "Z" + o, f"gs.{g}")
                pe.wait_ge(sem("gates"), 1)
                for t in range(T):
                    mm = nc.tensor.matmul(ps[:, 0:EPG], sel(t), gate8[:, t], start=t == 0, stop=t == 1)
                mm.then_inc(full["Z" + o], 1)

            def scatter(g, selT, o=""):
                await_moved(pe, f"y.{g}")
                for c in range(2):
                    for t in range(T):
                        ps = fill(pe, "Z" + o, f"x.{g}.{c}.{t}")
                        nc.tensor.matmul(ps[:, :], selT[:, t * P:(t + 1) * P], ysb[:, g % 2, c * 512:(c + 1) * 512],
                                         start=True, stop=True).then_inc(full["Z" + o], 1)

            pe.wait_ge(sem("selected"), T * G)
            gather(0, lambda t: Sel[:, t, 0], None)
            n = G * EPG
            down = sem("down_moe")
            banks = None
            for i in range(n + 1):
                if i < n:
                    g = i // EPG
                    if i % EPG == 0:
                        await_moved(pe, f"gs.{g}")
                    gu = weights(pe, f"moe.gu.{i}", f"moe.gu.{i}")
                    gu_pe(pe, "moe", i, gu, lambda k: hg[:, g % 2, k], (lambda: tr_pe(pe, "moe", i - 1)) if i else None)
                    if i % EPG == EPG - 1 and g < G - 1:
                        gather(g + 1, lambda t: Sel[:, t, g + 1], None)
                else:
                    tr_pe(pe, "moe", i - 1)
                if i:
                    j = i - 1
                    if j % EPG == 0:
                        banks = fill(pe, "Y", f"y.{j // EPG}")
                    wd = weights(pe, f"moe.d.{j}")
                    released[unit_at[f"moe.d.{j}"]] = (down, j + 1)
                    if j % EPG == EPG - 1:
                        down_pe(pe, "moe", j, wd, banks, False, True, down)
                    else:
                        down_pe(pe, "moe", j, wd, banks, j % EPG == 0, False, down)
                if i % EPG == 1 and i > 1:
                    scatter(i // EPG - 1, SelT[:, i // EPG - 1])
            scatter(G - 1, SelT[:, G - 1])
            drained(pe, "GU", "TT", "Z")
            pe.wait_ge(moved["Y"], filled["Y"])
            if "O" in phases:
                overflow_pe(pe, gather, scatter)

        def overflow(eng, body):
            eng.wait_ge(sem("flags"), 1)
            some = eng.value_load(flags[0:1, 1:2], min_val=0, max_val=1)
            with eng.If(some > 0):
                body()

        def overflow_pe(pe, gather, scatter):
            def body():
                gather(G, lambda t: Selo[:, t], None, "o")
                await_moved(pe, f"gs.{G}")
                banks = fill(pe, "Yo", f"y.{G}")
                for e in range(EPG):
                    s = e % 4
                    pe.wait_ge(sem("arrived_o"), 48 * (e + 1))
                    gu = slot_view(GU_SLOTS[s], P, KD, 2 * FF)
                    gu_pe(pe, "ovf", e, gu, lambda k: hg[:, 0, k], None, "o")
                    tr_pe(pe, "ovf", e, "o")
                    down_pe(pe, "ovf", e, slot_view((D_SLOTS[s],), P, 2, D), banks, e == 0, e == EPG - 1, sem("down_ovf"))
                scatter(G, SelTo, "o")
                drained(pe, "GUo", "TTo", "Zo")
                pe.wait_ge(moved["Yo"], 1)
            overflow(pe, body)

        def moe_y_act(act, g, o=""):
            banks = take_y(act, g, o)
            for c in range(2):
                mm = nc.scalar.copy(ysb[:, g % 2, c * 512:(c + 1) * 512], banks[c][:, :])
            mm.then_inc(moved["Y" + o], 1)

        def take_y(act, g, o):
            ring = "Y" + o
            n = taken[ring]
            assert jobs[f"y.{g}"] == (ring, n)
            taken[ring] += 1
            if o:
                act.wait_ge(sem("down_ovf"), EPG)
            else:
                act.wait_ge(sem("down_moe"), EPG * (g + 1))
            if g >= 2 and g < G:
                await_moved(act, f"x.{g - 2}.1.1")
            return RINGS[ring][0]

        def moe_act(act):
            await_moved(act, *residual_jobs("w_co"))
            norm_act(act, "c", X)
            act.wait_ge(sem("negmax_g"), 1)
            for t in range(T):
                nc.scalar.activation(ge[:, t], logit[:, t, 0:G], ACT.Exp, bias=nm[:, t, 0:1], accum_out=gsum[:, t, 0:1]).then_inc(sem("gexp"), 1)
            act.wait_ge(sem("negmax_e"), 1)
            for t in range(T):
                nc.scalar.activation(ee[:, t], el[:, t], ACT.Exp, bias=nm[:, t, 1:2], accum_out=gsum[:, t, 1:2]).then_inc(sem("eexp"), 1)
            for i in range(G * EPG):
                step_act(act, "moe", i)
                if i:
                    stepT_act(act, "moe", i - 1, sem("down_moe"))
                if i % EPG == 0 and i:
                    moe_y_act(act, i // EPG - 1)
            stepT_act(act, "moe", G * EPG - 1, sem("down_moe"))
            moe_y_act(act, G - 1)
            if "O" in phases:
                def body():
                    for e in range(EPG):
                        step_act(act, "ovf", e, "o")
                        stepT_act(act, "ovf", e, sem("down_ovf"), "o")
                    moe_y_act(act, G, "o")
                overflow(act, body)

        def moe_pool(pool):
            pool.dma_start(wr[:, :, 0:G], A["router_w_group"][0].rearrange("(k p) n -> p k n", p=P)).then_inc(sem("wr_in"), 16)
            pool.dma_start(wr[:, :, G:], A["router_w_expert"][0].rearrange("(k p) n -> p k n", p=P)).then_inc(sem("wr_in"), 16)
            norm_pool(pool, "c")

        def moe_dve(dve):
            L = links["dve"]
            V = nc.vector
            norm_dve(dve, "c", "moe_norm_g")
            for t in range(T):
                ps = take(dve, "D", f"logit.{t}")
                V.tensor_copy(logit[:, t], ps[:, 0:36]).then_inc(moved["D"], 1)
            await_moved(dve, "logit.1")
            tie = C("gidx")

            def pick(dst, v, m, n):
                L(V.tensor_reduce(m[:, :, 0], v, AX.X, ALU.max))
                L(V.tensor_tensor(tmp8[:, :, 0:n], v, bc(m[:, :, 0], n, 2), ALU.is_equal))
                L(V.tensor_tensor(dst, tmp8[:, :, 0:n], bc(tieinv[:, 0:n], T, 1), ALU.mult))
                L(V.tensor_reduce(m[:, :, 0], dst, AX.X, ALU.max))
                L(V.tensor_tensor(dst, dst, bc(m[:, :, 0], n, 2), ALU.is_equal))

            tieinv = rtv(400, 8)
            dve.wait_ge(sem("const2_in"), 16)
            L(V.tensor_scalar(tieinv, tie, -1.0, 8.0, ALU.mult, ALU.add))
            L(V.tensor_reduce(nm[:, :, 0], logit[:, :, 0:G], AX.X, ALU.max))
            V.tensor_scalar(nm[:, :, 0], nm[:, :, 0], -1.0, None, ALU.mult).then_inc(sem("negmax_g"), 1)
            L(V.tensor_tensor(gb, logit[:, :, 0:G], bc(bias_g, T, 1), ALU.add))
            pick(oh, gb, m1, G)
            V.tensor_copy(rtv(410, T, G), oh).then_inc(sem("group_picked"), 1)
            for t in range(T):
                L(V.tensor_tensor(tmp[:, t], logit[:, t, G:].rearrange("p (g e) -> p g e", g=G), bc(oh[:, t], EPG, 2), ALU.mult))
                L(V.reduce_sum(el[:, t], tmp[:, t].rearrange("p g e -> p e g"), AX.X))
                L(V.tensor_tensor(tmp[:, t], bias_e.rearrange("p (g e) -> p g e", g=G), bc(oh[:, t], EPG, 2), ALU.mult))
                L(V.reduce_sum(bias8[:, t], tmp[:, t].rearrange("p g e -> p e g"), AX.X))
            L(V.tensor_reduce(nm[:, :, 1], el, AX.X, ALU.max))
            V.tensor_scalar(nm[:, :, 1], nm[:, :, 1], -1.0, None, ALU.mult).then_inc(sem("negmax_e"), 1)
            L(V.tensor_tensor(bias8, bias8, el, ALU.add))
            pick(oh1, bias8, m1, EPG)
            L(V.scalar_tensor_tensor(bias8, oh1, -3e38, bias8, ALU.mult, ALU.add))
            pick(oh2, bias8, m1, EPG)
            L(V.tensor_tensor(oh1, oh1, oh2, ALU.add))
            ps = take(dve, "D", "rank")
            V.tensor_copy(cnt, ps[:, 0:3 * G].rearrange("p (a b) -> p a b", a=3)).then_inc(moved["D"], 1)
            await_moved(dve, "rank")
            L(V.tensor_tensor(tmp8[:, :, 0:G], cnt[:, 0:T], oh, ALU.mult))
            L(V.reduce_sum(rank[:, :, 0], tmp8[:, :, 0:G], AX.X))
            for g in range(G):
                for t in range(T):
                    V.tensor_scalar(Sel[:, t, g], C("iota"), rank[:, t, 0:1], oh[:, t, g:g + 1], ALU.is_equal, ALU.mult) \
                        .then_inc(sem("selected"), 1)
            dve.wait_ge(sem("gexp"), 2)
            dve.wait_ge(sem("eexp"), 2)
            L(V.reciprocal(gsum, gsum))
            L(V.tensor_tensor(ge, ge, oh, ALU.mult))
            L(V.reduce_sum(gw[:, :, 0], ge, AX.X))
            L(V.tensor_tensor(gw[:, :, 0], gw[:, :, 0], gsum[:, :, 0], ALU.mult))
            L(V.tensor_tensor(ee, ee, bc(gsum[:, :, 1], EPG, 2), ALU.mult))
            L(V.tensor_tensor(ee, ee, oh1, ALU.mult))
            L(V.reduce_sum(den[:, :, 0], ee, AX.X))
            L(V.reciprocal(den, den))
            L(V.tensor_tensor(den, den, gw, ALU.mult))
            V.tensor_tensor(gate8, ee, bc(den[:, :, 0], EPG, 2), ALU.mult).then_inc(sem("gates"), 1)
            L(V.tensor_scalar(ovf, cnt[:, 2], float(P), None, ALU.is_gt))
            L(V.tensor_tensor(tmp8[:, :, 0:G], oh, bc(ovf, T, 1), ALU.mult))
            L(V.reduce_sum(oho[:, :, 0], tmp8[:, :, 0:G], AX.X))
            L(V.tensor_scalar(rank[:, :, 1], rank[:, :, 0], -float(P), None, ALU.add))
            for t in range(T):
                L(V.tensor_scalar(Selo[:, t], C("iota"), rank[:, t, 1:2], oho[:, t], ALU.is_equal, ALU.mult))
            L(V.tensor_tensor(tmp8[:, 0, 0:G], ovf, tie[:, 0:G], ALU.mult))
            L(V.reduce_sum(nm[:, 0, 0:1], tmp8[:, 0, 0:G], AX.X))
            L(V.reduce_sum(nm[:, 0, 1:2], ovf, AX.X))
            V.tensor_copy(flags, nm[:, 0, :]).then_inc(sem("flags"), 1)

            def gather_dve(g, selT, o=""):
                ps = take(dve, "Z" + o, f"selT.{g}")
                V.tensor_copy(selT, ps[:, 0:S]).then_inc(moved["Z" + o], 1)
                for half in range(2):
                    ps = take(dve, "Z" + o, f"hg.{g}.{half}")
                    V.tensor_tensor(hg[:, g % 2, half * 4:half * 4 + 4], ps[:, :].rearrange("p (k n) -> p k n", k=4),
                                    bc(col("moe_norm_g", 4, half * 4), P, 2), ALU.mult).then_inc(moved["Z" + o], 1)
                ps = take(dve, "Z" + o, f"gs.{g}")
                V.tensor_copy(gs[:, g], ps[:, 0:EPG]).then_inc(moved["Z" + o], 1)

            def scatter_dve(g, o=""):
                for c in range(2):
                    for t in range(T):
                        ps = take(dve, "Z" + o, f"x.{g}.{c}.{t}")
                        V.tensor_tensor(X[:, t, c * 512:(c + 1) * 512], X[:, t, c * 512:(c + 1) * 512], ps[:, :],
                                        ALU.add).then_inc(moved["Z" + o], 1)

            gather_dve(0, SelT[:, 0])
            await_moved(dve, "gs.0")
            for i in range(G * EPG):
                g = i // EPG
                step_dve(dve, "moe", i, gs[:, g, i % EPG:i % EPG + 1])
                if i % EPG == EPG - 1 and g < G - 1:
                    gather_dve(g + 1, SelT[:, g + 1])
                    await_moved(dve, f"gs.{g + 1}")
                if i % EPG == 1 and i > 1:
                    scatter_dve(g - 1)
            scatter_dve(G - 1)
            if "O" in phases:
                def body():
                    await_moved(dve, f"x.{G - 1}.1.1")
                    gather_dve(G, SelTo, "o")
                    await_moved(dve, f"gs.{G}")
                    for e in range(EPG):
                        step_dve(dve, "ovf", e, gs[:, G, e:e + 1], "o")
                    scatter_dve(G, "o")
                    await_moved(dve, f"x.{G}.1.1")
                overflow(dve, body)
                await_moved(dve, f"x.{G - 1}.1.1")
                V.tensor_copy(rtv(420, 1), rtv(400, 1)).then_inc(sem("overflow_added"), 1)

        def overflow_sp(sp):
            def body():
                g = sp.value_load(flags[0:1, 0:1], min_val=0, max_val=G - 1)
                sp.wait_ge(sem("down_moe"), G * EPG)
                for e in range(EPG):
                    if e >= 4:
                        sp.wait_ge(sem("down_ovf"), e - 3)
                    v = slot_view(GU_SLOTS[e % 4], P, KD, 2 * FF)
                    x_ = bass.ds(g * EPG + e, 1)
                    for src, dst in ((eg, v[:, :, 0:FF]), (eu, v[:, :, FF:]), (ed, slot_view((D_SLOTS[e % 4],), P, 2, D))):
                        sp.dma_start(dst, src[x_, :, :].rearrange("o (k p) n -> p (o k) n", p=P)).then_inc(sem("arrived_o"), 16)
                    sp.wait_ge(sem("arrived_o"), 48 * (e + 1))
                sp.wait_ge(sem("down_ovf"), EPG)
            overflow(sp, body)

        pe_fns.append(("C", moe_pe)); act_fns.append(("C", moe_act))
        pool_fns.append(("C", moe_pool)); dve_fns.append(("C", moe_dve))

        def add_swiglu(ph, u, layer, after, fenced):
            n = DFF // FF
            wg, wu, wd_ = A["ffn_w_gate_2"][layer], A["ffn_w_up_2"][layer], A["ffn_w_down_2"][layer]
            if ph in phases:
                fence[u] = fenced
                ffn_units(u, range(n), lambda c: wg[:, c * FF:(c + 1) * FF], lambda c: wu[:, c * FF:(c + 1) * FF],
                          lambda c: wd_[c * FF:(c + 1) * FF, :])

            def f_pe(pe):
                down = sem(f"down_{u}")
                norm_pe(pe, u)
                drained(pe, "D", "A")
                banks = fill(pe, "Y4", f"y_{u}")
                for i in range(T * n + 1):
                    if i < T * n:
                        c, t = i // T, i % T
                        gu = weights(pe, f"{u}.gu.{c}", f"{u}.gu.{T * c + T - 1}")
                        gu_pe(pe, u, i, gu, lambda k: hT[:, k, t * P:(t + 1) * P],
                              (lambda: tr_pe(pe, u, i - 1)) if i else None)
                    else:
                        tr_pe(pe, u, i - 1)
                    if i:
                        c, t = (i - 1) // T, (i - 1) % T
                        wd = weights(pe, f"{u}.d.{c}")
                        released[unit_at[f"{u}.d.{c}"]] = (down, T * c + T)
                        down_pe(pe, u, i - 1, wd, banks[2 * t:2 * t + 2], c == 0, c == n - 1, down)
                drained(pe, "GU", "TT")
                pe.wait_ge(moved["Y4"], filled["Y4"])

            def f_act(act):
                after(act)
                norm_act(act, u, X)
                for i in range(T * n):
                    step_act(act, u, i)
                    if i:
                        stepT_act(act, u, i - 1, sem(f"down_{u}"))
                stepT_act(act, u, T * n - 1, sem(f"down_{u}"))

            def f_dve(dve):
                norm_dve(dve, u, "ffn_norm_2", gi=KD * layer)
                for i in range(T * n):
                    step_dve(dve, u, i)
                taken["Y4"] += 1
                for t in range(T):
                    dve.wait_ge(sem(f"down_{u}"), T * n - 1 + t)
                    for c in range(2):
                        last = nc.vector.tensor_tensor(X[:, t, c * 512:(c + 1) * 512], X[:, t, c * 512:(c + 1) * 512],
                                                       BANK[4 + 2 * t + c][:, :], ALU.add)
                last.then_inc(moved["Y4"], 1)

            pe_fns.append((ph, f_pe)); act_fns.append((ph, f_act)); dve_fns.append((ph, f_dve))
            pool_fns.append((ph, lambda pool: norm_pool(pool, u)))

        fproj = view(6144, T, IN2)
        fqz = view(11280, FH, S)
        fkT = view(13328, FH // 2, S)
        fsc = view(14352, FH, 3 * P)
        fprT = view(17424, FH, 3 * P)
        fo = view(4096, T, FW)
        logf = work[:, 20496:20528].rearrange("p (a b) -> p a b", a=4)
        cum = work[:, 20528:20544].rearrange("p (a b) -> p a b", a=2)
        ncumT = view(20544, S)
        fst = view(20800, 8, 16)
        pooledT = view(5120, 2, 2 * S)
        OG, OF, OU = 3 * FW, 4 * FW, 4 * FW + FH

        if "D" in phases:
            linear_units("w_fin", dram2("hy_w_in_2"), IN2)
            unit("pool_w", A["hy_pool_w_2"][0].rearrange("g c d -> c g d"), 4, P)
            linear_units("w_out2", dram2("hy_w_out_2"), D)

        def fox_pe(pe):
            norm_pe(pe, "d")
            await_moved(pe, *hT_jobs("d"))
            linear(pe, "w_fin", hT, IN2, "AD")
            pe.wait_ge(sem("const2_in"), 16)
            await_moved(pe, "w_fin.5.0", "w_fin.5.1")
            W = lambda g, b: C("pool")[:, (3 * g + b) * P:(3 * g + b + 1) * P]
            for gp in range(2):
                ps = fill(pe, "A", f"pooled.{gp}")
                for g in (2 * gp, 2 * gp + 1):
                    u = lambda t: fproj[:, t, OU + g * P:OU + (g + 1) * P]
                    o = (g % 2) * S
                    nc.tensor.matmul(ps[:, o:o + P], u(0), W(g, 0), start=True, stop=True)
                    nc.tensor.matmul(ps[:, o + P:o + S], u(0), W(g, 1), start=True, stop=False)
                    mm = nc.tensor.matmul(ps[:, o + P:o + S], u(1), W(g, 2), start=False, stop=True)
                mm.then_inc(full["A"], 1)
            pe.wait_ge(sem("logf"), 1)
            ps = fill(pe, "D", "cum")
            nc.tensor.matmul(ps[:, 0:FH], C("tri"), logf[:, 0], start=True, stop=True)
            nc.tensor.matmul(ps[:, FH:2 * FH], C("ones"), logf[:, 0], start=True, stop=False)
            nc.tensor.matmul(ps[:, FH:2 * FH], C("tri"), logf[:, 1], start=False, stop=True)
            nc.tensor.matmul(ps[0:FH, P:2 * P], logf[:, 0], C("tri"), start=True, stop=True)
            nc.tensor.matmul(ps[0:FH, 2 * P:3 * P], logf[:, 0], C("ones"), start=True, stop=False)
            nc.tensor.matmul(ps[0:FH, 2 * P:3 * P], logf[:, 1], C("tri"), start=False, stop=True).then_inc(full["D"], 1)
            await_moved(pe, "pooled.1")
            pw = weights(pe, "pool_w", "fmixed.1")
            for gp in range(2):
                ps = fill(pe, "D", f"fmixed.{gp}")
                for g in range(2):
                    mm = nc.tensor.matmul(ps[:, g * S:(g + 1) * S], pw[:, 2 * gp + g, :],
                                          pooledT[:, gp, g * S:(g + 1) * S], start=True, stop=True)
                mm.then_inc(full["D"], 1)
            for t in range(T):
                for j in range(2):
                    pe.wait_ge(sem("fqk"), T * t + j + 1)
                    ps = fill(pe, "D", f"fT.{j}.{t}")
                    for k in range(4):
                        mm = nc.tensor.transpose(ps[:, k * P:(k + 1) * P],
                                                 fproj[:, t, j * FW + k * P:j * FW + (k + 1) * P], ident)
                    mm.then_inc(full["D"], 1)
            await_moved(pe, "fT.1.1")
            for h in range(FH):
                ps = fill(pe, "D", f"fscore.{h}")
                for t, (lo, hi) in enumerate(((0, P), (P, 3 * P))):
                    nc.tensor.matmul(ps[:, lo:hi], fqz[:, h, t * P:(t + 1) * P], fkT[:, h // 2, 0:hi - lo],
                                     start=True, stop=False)
                    mm = nc.tensor.matmul(ps[:, lo:hi], C("sel")[0:FH, h * P:(h + 1) * P], ncumT[0:FH, 0:hi - lo],
                                          start=False, stop=True)
                mm.then_inc(full["D"], 1)
            for h in range(FH):
                pe.wait_ge(sem("fexp"), 2 * h + 2)
                ps = fill(pe, "A", f"fprT.{h}")
                for b in range(3):
                    mm = nc.tensor.transpose(ps[:, b * P:(b + 1) * P], fsc[:, h, b * P:(b + 1) * P], ident)
                mm.then_inc(full["A"], 1)
            await_moved(pe, f"fprT.{FH - 1}")
            v = lambda t, h: fproj[:, t, 2 * FW + h * HD:2 * FW + (h + 1) * HD]
            for t in range(T):
                ps = fill(pe, "D", f"fo.{t}")
                for h in range(FH):
                    o = slice(h * HD, (h + 1) * HD)
                    if t == 0:
                        mm = nc.tensor.matmul(ps[:, o], fprT[:, h, 0:P], v(0, h), start=True, stop=True)
                    else:
                        nc.tensor.matmul(ps[:, o], fprT[:, h, P:S], v(0, h), start=True, stop=False)
                        mm = nc.tensor.matmul(ps[:, o], fprT[:, h, S:3 * P], v(1, h), start=False, stop=True)
                mm.then_inc(full["D"], 1)
            for t in range(T):
                pe.wait_ge(sem("fgated"), t + 1)
                ps = fill(pe, "A", f"foT.{t}")
                for k in range(4):
                    mm = nc.tensor.transpose(ps[:, k * P:(k + 1) * P], fo[:, t, k * P:(k + 1) * P], ident)
                mm.then_inc(full["A"], 1)
            await_moved(pe, "foT.1", "fmixed.1")
            linear(pe, "w_out2", mixT, D, "DD")

        def fox_act(act):
            if "C" in phases:
                await_moved(act, f"x.{G - 1}.1.1")
                if "O" in phases:
                    act.wait_ge(sem("overflow_added"), 1)
            norm_act(act, "d", X)
            for c in range(6):
                w_ = min(512, IN2 - c * 512)
                copy_chunk_act(act, f"w_fin.{c}.0", fproj[:, 0, c * 512:c * 512 + w_])
            act.wait_ge(sem("absz"), 1)
            nc.scalar.activation(logf[:, 2:4], logf[:, 2:4], ACT.Exp, scale=-1.0).then_inc(sem("expz"), 1)
            act.wait_ge(sem("expz"), 1)
            nc.scalar.activation(logf[:, 2:4], logf[:, 2:4], ACT.Ln, bias=1.0).then_inc(sem("lnz"), 1)
            for gp in range(2):
                copy_chunk_act(act, f"pooled.{gp}", pooledT[:, gp])
            await_moved(act, "w_fin.3.0", "w_fin.3.1")
            og = fproj[:, :, OG:OG + FW]
            nc.scalar.activation(og, og, ACT.Sigmoid).then_inc(sem("fgate"), 1)
            for h in range(FH):
                act.wait_ge(sem("fnmax"), h // 2 + 1)
                for t, (lo, hi) in enumerate(((0, P), (P, 3 * P))):
                    nc.scalar.activation(fsc[:, h, lo:hi], fsc[:, h, lo:hi], ACT.Exp, bias=fst[:, 4 + t, h:h + 1],
                                         accum_out=fst[:, 6 + t, h:h + 1]).then_inc(sem("fexp"), 1)
                if h:
                    copy_chunk_act(act, f"fprT.{h - 1}", fprT[:, h - 1])
            copy_chunk_act(act, f"fprT.{FH - 1}", fprT[:, FH - 1])
            for t in range(T):
                ps = take(act, "A", f"foT.{t}")
                nc.scalar.copy(mixT[:, 0:4, t * P:(t + 1) * P], ps[:, :].rearrange("p (k n) -> p k n", k=4)).then_inc(moved["A"], 1)

        def fox_pool(pool):
            norm_pool(pool, "d")
            await_moved(pool, "w_fin.0.0", "w_fin.0.1")
            nc.gpsimd.memset(fqz[HD:P, 0::2, :], 0.0).then_inc(sem("fqz_zero"), 1)
            pool.wait_ge(sem("fqz_zero"), 1)
            nc.gpsimd.memset(fqz[0:HD, 1::2, :], 0.0).then_inc(sem("fqz_zero"), 1)
            pool.wait_ge(sem("fqz_zero"), 2)
            for t in range(T):
                pool.wait_ge(sem("fss"), t + 1)
                L = links["pool"]
                L(nc.gpsimd.tensor_scalar(fst[:, 2 + t, 0:FH], fst[:, t, 0:FH], 1.0, HD * EPS, ALU.mult, ALU.add))
                L(nc.gpsimd.tensor_scalar(fst[:, 2 + t, FH:], fst[:, t, FH:], 1.0 / HD, EPS, ALU.mult, ALU.add))
                nc.gpsimd.tensor_tensor(fst[:, 2 + t], fst[:, 2 + t], neghalf[:, 0:16], ALU.pow).then_inc(sem("frstd"), 1)

        def fox_dve(dve):
            L, V = links["dve"], nc.vector
            norm_dve(dve, "d", "mix_norm_2")
            for c in range(6):
                w_ = min(512, IN2 - c * 512)
                copy_chunk_dve(dve, f"w_fin.{c}.1", fproj[:, 1, c * 512:c * 512 + w_])
                if c == 1:
                    await_moved(dve, "w_fin.1.0", "w_fin.1.1")
                    for t in range(T):
                        x_ = fproj[:, t, 0:2 * FW]
                        L(V.tensor_tensor(sq[:, t], x_, x_, ALU.mult))
                        V.reduce_sum(fst[:, t], sq[:, t].rearrange("p (h d) -> p h d", h=16), AX.X).then_inc(sem("fss"), 1)
            await_moved(dve, "w_fin.4.0", "w_fin.4.1")
            dve.wait_ge(sem("rowsmall_in"), 80)
            L(V.tensor_tensor(logf[:, 0:2], fproj[:, :, OF:OF + FH], bc(fbias, T, 1), ALU.add))
            L(V.scalar_tensor_tensor(logf[:, 2:4], logf[:, 0:2], -1.0, logf[:, 0:2], ALU.mult, ALU.max))
            V.tensor_scalar(logf[:, 0:2], logf[:, 0:2], 0.0, None, ALU.min).then_inc(sem("absz"), 1)
            dve.wait_ge(sem("absz"), 1)
            dve.wait_ge(sem("lnz"), 1)
            V.tensor_tensor(logf[:, 0:2], logf[:, 0:2], logf[:, 2:4], ALU.subtract).then_inc(sem("logf"), 1)
            for t in range(T):
                dve.wait_ge(sem("frstd"), t + 1)
                for j in range(2):
                    v = fproj[:, t, j * FW:(j + 1) * FW].rearrange("p (h d) -> p h d", h=FH)
                    V.tensor_tensor(v, v, bc(fst[:, 2 + t, j * FH:(j + 1) * FH], HD, 2), ALU.mult).then_inc(sem("fqk"), 1)
            ps = take(dve, "D", "cum")
            V.tensor_copy(cum, ps[:, 0:2 * FH].rearrange("p (a b) -> p a b", a=2))
            V.tensor_scalar(ncumT[0:FH], ps[0:FH, P:3 * P], -1.0, None, ALU.mult).then_inc(moved["D"], 1)
            for gp in range(2):
                ps = take(dve, "D", f"fmixed.{gp}")
                V.tensor_tensor(mixT[:, 4 + 2 * gp:6 + 2 * gp], ps[:, :].rearrange("p (k n) -> p k n", k=2),
                                bc(col("hy_pool_scale_2", 2, 2 * gp), S, 2), ALU.mult).then_inc(moved["D"], 1)
            dve.wait_ge(sem("fqz_zero"), 2)
            dve.wait_ge(sem("gain2_in"), 64)
            for t in range(T):
                for j in range(2):
                    ps = take(dve, "D", f"fT.{j}.{t}")
                    v = ps[:, :].rearrange("p (k n) -> p k n", k=4)
                    s_ = slice(t * P, (t + 1) * P)
                    if j == 0:
                        V.tensor_scalar(fqz[0:HD, 0::2, s_], v[0:HD], cols[0:HD, P:P + 1], None, ALU.mult)
                        V.tensor_scalar(fqz[HD:, 1::2, s_], v[HD:], cols[HD:, P:P + 1], None, ALU.mult).then_inc(moved["D"], 1)
                    else:
                        V.tensor_scalar(fkT[:, :, s_], v, cols[:, P + 1:P + 2], None, ALU.mult).then_inc(moved["D"], 1)
            await_moved(dve, "cum")
            for h in range(FH):
                ps = take(dve, "D", f"fscore.{h}")
                for t, (lo, hi) in enumerate(((0, P), (P, 3 * P))):
                    last = V.scalar_tensor_tensor(fsc[:, h, lo:hi], ps[:, lo:hi], cum[:, t, h:h + 1], C("cmask")[:, lo:hi],
                                                  ALU.add, ALU.add)
                last.then_inc(moved["D"], 1)
                if h % 2:
                    await_moved(dve, f"fscore.{h}")
                    L(V.tensor_reduce(fst[:, 4, h - 1:h + 1], fsc[:, h - 1:h + 1, 0:P], AX.X, ALU.max, negate=True))
                    V.tensor_reduce(fst[:, 5, h - 1:h + 1], fsc[:, h - 1:h + 1, P:], AX.X, ALU.max, negate=True) \
                        .then_inc(sem("fnmax"), 1)
            dve.wait_ge(sem("fexp"), 2 * FH)
            L(V.reciprocal(fst[:, 6:8, 0:FH], fst[:, 6:8, 0:FH]))
            dve.wait_ge(sem("fgate"), 1)
            for t in range(T):
                ps = take(dve, "D", f"fo.{t}")
                v = fo[:, t].rearrange("p (h d) -> p h d", h=FH)
                V.tensor_tensor(v, ps[:, :].rearrange("p (h d) -> p h d", h=FH), bc(fst[:, 6 + t, 0:FH], HD, 2),
                                ALU.mult).then_inc(moved["D"], 1)
                await_moved(dve, f"fo.{t}")
                V.tensor_tensor(fo[:, t], fo[:, t], fproj[:, t, OG:OG + FW], ALU.mult).then_inc(sem("fgated"), 1)
            residual_dve(dve, "w_out2")

        pe_fns.append(("D", fox_pe)); act_fns.append(("D", fox_act))
        pool_fns.append(("D", fox_pool)); dve_fns.append(("D", fox_dve))

        add_swiglu("E", "f0", 0, lambda act: await_moved(act, *residual_jobs("w_out2")), ("fmixed.1", "fo.1"))

        dxT = view(2048, KD, S)
        xi = [view(4096, KD, S), view(6144, KD, S)]
        r_ = view(8192, T, D)
        k_ = view(10240, T, D)
        v_ = view(12288, T, D)
        a_ = view(14336, T, D)
        s_ = view(16384, T, D)
        g_ = view(18432, T, D)
        rows5 = view(20480, 5, D)
        k_k, k_a, r_k, ln_w, ln_b = (rows5[:, i] for i in range(5))
        wlow = view(25600, 1, S)
        alow = view(25856, 1, S)
        glow = view(25600, 2, S)
        rst = view(26112, 24, 16)
        fch = view(26112 + 160, 3, 8)
        fraw = view(26112 + 192, 8, T, 4)
        Ep, Em, Ex = view(0, D), view(1024, D), view(2048, D)
        kk, tmpk = view(3072, D), g_[:, 1]
        NM = view(0, 8, 512)
        AZ = view(4096, 8, 256)
        BK = view(6144, 4, 256)
        MV = view(6144, 8, HD)
        PM = view(7168, 8, P)
        RB = ring_w[:, 4 * SLOT:8 * SLOT]
        Xi = RB[:, 0:1024].rearrange("p (h n) -> p h n", h=8)
        Yi = RB[:, 1024:2048].rearrange("p (h n) -> p h n", h=8)
        UG = RB[:, 2048:3072].rearrange("p (h n) -> p h n", h=8)
        HT = RB[:, 3072:4096].rearrange("p (q n) -> p q n", q=8)
        WZ = RB[:, 4096:6144].rearrange("p (c q n) -> p c q n", c=2, q=8)
        Y0 = RB[:, 6144:7168]
        SS = RB[:, 7168:8192].rearrange("p (b q n) -> p b q n", b=2, q=8)
        NP_ = RH // 2

        if "F" in phases:
            def lora(name, w1, w2, bias):
                unit(f"{name}1", dram2(w1).rearrange("(k p) n -> p k n", p=P), KD, DL)
                unit(f"{name}2", None, 1, D, parts=DL + 1,
                     pieces=lambda v: [(dram2(w2).unsqueeze(1), v[0:DL]), (A[bias][0:1, :].unsqueeze(1), v[DL:DL + 1])])
            lora("lw", "rw_w1_2", "rw_w2_2", "rw_w0_2")
            lora("la", "rw_a1_2", "rw_a2_2", "rw_a0_2")
            linear_units("w_rk", dram2("rw_w_k_2"), D)
            linear_units("w_rr", dram2("rw_w_r_2"), D)
            linear_units("w_rv", dram2("rw_w_v_2"), D)
            unit("g1", dram2("rw_g1_2").rearrange("(k p) n -> p k n", p=P), KD, GL)
            g2 = dram2("rw_g2_2")
            unit("g2", None, 2, D, pieces=lambda v: [(g2[0:P, :], v[:, 0]), (g2[P:GL, :], v[0:GL - P, 1])])
            for i, (c, k0) in enumerate(((0, 0), (0, 4), (1, 0), (1, 4))):
                unit(f"w_ro.{c}.{k0}", dram2("rw_w_o_2")[k0 * P:(k0 + 4) * P, c * 512:(c + 1) * 512]
                     .rearrange("(k p) n -> p k n", p=P), 4, 512, slot=i)
            next_slot[0] = 0

        ORDER = (("w", 1), ("a", 4), ("k", 2), ("r", 0), ("v", 3), ("g", 5))

        def rw_heads(half):
            return range(8 * half, 8 * half + 8)

        def rwkv_pe(pe):
            norm_pe(pe, "f")
            x = lambda i: xi[i % 2]

            def low(i, name, m, job):
                w1 = weights(pe, name, job)
                pe.wait_ge(sem("xi"), i + 1)
                ps = fill(pe, "A", job)
                for o, n, c0 in ((0, min(m, P), 0),) + (((P, m - P, S),) if m > P else ()):
                    for k in range(KD):
                        mm = nc.tensor.matmul(ps[0:n, c0:c0 + S], w1[:, k, o:o + n], x(i)[:, k, :],
                                              start=k == 0, stop=k == KD - 1)
                mm.then_inc(full["A"], 1)
            for i, (name, lowT) in enumerate((("lw", wlow), ("la", alow))):
                low(i, name + "1", DL, f"{name}low")
                await_moved(pe, f"{name}low")
                if i == 0:
                    pe.wait_ge(sem("low_ones"), 2)
                w2 = weights(pe, name + "2", f"{name}.1.1")
                for c in range(2):
                    for t in range(T):
                        ps = fill(pe, "A", f"{name}.{c}.{t}")
                        nc.tensor.matmul(ps[:, :], lowT[0:DL + 1, 0, t * P:(t + 1) * P], w2[:, 0, c * 512:(c + 1) * 512],
                                         start=True, stop=True).then_inc(full["A"], 1)
            for i, name in ((2, "w_rk"), (3, "w_rr")):
                pe.wait_ge(sem("xi"), i + 1)
                linear(pe, name, x(i), D, "AD")
            await_moved(pe, "lw.1.1")
            pe.wait_ge(sem("const2_in"), 16)
            for t in range(T):
                for c in range(2):
                    for which in ("rwcum", "rwcumx"):
                        ps = fill(pe, "A", f"{which}.{c}.{t}")
                        nc.tensor.matmul(ps[:, :], C(which), s_[:, t, c * 512:(c + 1) * 512],
                                         start=True, stop=True).then_inc(full["A"], 1)
            ps = fill(pe, "D", "fraw")
            for t in range(T):
                for q in range(NP_):
                    o = (q * T + t) * 4
                    sq_ = s_[:, t, q * P:(q + 1) * P]
                    nc.tensor.matmul(ps[:, o:o + 2], sq_, C("rwcum")[:, CH - 1::CH], start=True, stop=True)
                    mm = nc.tensor.matmul(ps[:, o + 2:o + 4], sq_, C("rwmid")[:, CH - 1::CH], start=True, stop=True)
            mm.then_inc(full["D"], 1)
            pe.wait_ge(sem("xi"), 5)
            linear(pe, "w_rv", x(4), D, "AA")
            low(5, "g1", GL, "glow")
            await_moved(pe, "glow")
            w2 = weights(pe, "g2", "g.1.1")
            for t in range(T):
                for c in range(2):
                    ps = fill(pe, "A", f"g.{c}.{t}")
                    nc.tensor.matmul(ps[:, :], glow[:, 0, t * P:(t + 1) * P], w2[:, 0, c * 512:(c + 1) * 512],
                                     start=True, stop=False)
                    nc.tensor.matmul(ps[:, :], glow[0:GL - P, 1, t * P:(t + 1) * P],
                                     w2[0:GL - P, 1, c * 512:(c + 1) * 512], start=False, stop=True).then_inc(full["A"], 1)
            for t in range(T):
                pe.wait_ge(sem("hats"), t + 1)
                for half in range(2):
                    heads_pe(pe, t, half)
                scan_pe(pe, t)
            for t in range(T):
                for half in range(2):
                    if half == 0:
                        pe.wait_ge(sem("y_done"), t + 1)
                    transposed(pe, "D", f"ryT.{t}.{half}", r_, t, half)
            await_moved(pe, "ryT.1.1")
            linear(pe, "w_ro", mixT, D, "DD")

        def heads_pe(pe, t, half):
            u = f"{t}.{half}"
            for gq in range(2):
                for kind, (x0, x1) in (("AR", (s_, r_)), ("BK", (a_, k_))):
                    ps = fill(pe, "A", f"{kind}.{u}.{gq}")
                    for q in range(2):
                        o = (4 * half + 2 * gq + q) * P
                        for j, src in enumerate((x0, x1)):
                            mm = nc.tensor.transpose(ps[:, (2 * q + j) * P:(2 * q + j + 1) * P], src[:, t, o:o + P], ident)
                    mm.then_inc(full["A"], 1)
            for h in range(8):
                if h % 4 == 0:
                    await_moved(pe, f"BK.{u}.{h // 4}")
                ps = fill(pe, "D", f"NM.{u}.{h}")
                nc.tensor.matmul(ps[:, 0:S], BK[:, h // 2, 0:P], AZ[:, h, :], start=True, stop=True)
                nc.tensor.matmul(ps[:, S:], BK[:, h // 2, P:], AZ[:, h, :], start=True, stop=True).then_inc(full["D"], 1)

            def four(name, gq, lhs, rhs, ring="D"):
                ps = fill(pe, ring, f"{name}.{u}.{gq}")
                for h in range(4):
                    mm = nc.tensor.matmul(ps[:, h * P:(h + 1) * P], lhs(4 * gq + h), rhs(4 * gq + h), start=True, stop=True)
                mm.then_inc(full[ring], 1)
            for gq in range(2):
                pe.wait_ge(sem("Y2"), 4 * t + 2 * half + gq + 1)
                ps = fill(pe, "A", f"X2.{u}.{gq}")
                for h in range(4):
                    mm = nc.tensor.transpose(ps[:, h * P:(h + 1) * P], Yi[:, 4 * gq + h], ident)
                mm.then_inc(full["A"], 1)
            for gq in range(2):
                ps = fill(pe, "A", f"Mv.{u}.{gq}")
                for h in range(4):
                    hh = 4 * gq + h
                    o = (8 * half + hh) * HD
                    mm = nc.tensor.matmul(ps[:, h * HD:(h + 1) * HD], NM[:, hh, S:S + P], v_[:, t, o:o + HD],
                                          start=True, stop=True)
                mm.then_inc(full["A"], 1)
            for lv in range(5):
                for gq in range(2):
                    if lv == 0:
                        await_moved(pe, f"X2.{u}.{gq}")
                    else:
                        await_moved(pe, f"dY{lv - 1}.{u}.{gq}")
                    four(f"P{lv}", gq, lambda h: NM[:, h, 0:P], lambda h: Xi[:, h])
                for gq in range(2):
                    await_moved(pe, f"P{lv}.{u}.{gq}")
                    if lv < 4:
                        four(f"dX{lv}", gq, lambda h: Yi[:, h], lambda h: PM[:, h])
                    four(f"dY{lv}", gq, lambda h: PM[:, h], lambda h: Yi[:, h])
            for gq in range(2):
                await_moved(pe, f"dY4.{u}.{gq}", f"Mv.{u}.{gq}")
                ps = fill(pe, "A", f"UG.{u}.{gq}")
                for h in range(4):
                    hh = 4 * gq + h
                    o = (8 * half + hh) * HD
                    nc.tensor.matmul(ps[:, h * P:h * P + HD], Yi[:, hh], MV[:, hh], start=True, stop=True)
                    mm = nc.tensor.matmul(ps[:, h * P + HD:(h + 1) * P], Yi[:, hh], s_[:, t, o:o + HD], start=True, stop=True)
                mm.then_inc(full["A"], 1)
            for gq in range(2):
                await_moved(pe, f"UG.{u}.{gq}")
                ps = fill(pe, "D", f"yH.{u}.{gq}")
                for h in range(4):
                    hh = 4 * gq + h
                    o = (8 * half + hh) * HD
                    nc.tensor.matmul(ps[:, h * HD:(h + 1) * HD], NM[:, hh, P:S], UG[:, hh, 0:HD], start=True, stop=False)
                    nc.tensor.matmul(ps[:, h * HD:(h + 1) * HD], NM[:, hh, S + P:], v_[:, t, o:o + HD], start=False, stop=True)
                for h in range(4):
                    hh = 4 * gq + h
                    p = (h % 2) * HD
                    mm = nc.tensor.matmul(ps[p:p + HD, S + (h // 2) * P:S + (h // 2 + 1) * P], UG[:, hh, HD:], NM[:, hh, P:S],
                                          start=True, stop=True)
                mm.then_inc(full["D"], 1)
                for c in range(2):
                    ps = fill(pe, "D", f"WZ{c}.{u}.{gq}")
                    w = slice(c * CH, (c + 1) * CH)
                    for h in range(4):
                        hh = 4 * gq + h
                        p = (h % 2) * HD
                        o = (8 * half + hh) * HD
                        c0 = (h // 2) * P
                        nc.tensor.matmul(ps[p:p + HD, c0:c0 + HD], UG[w, hh, HD:], a_[w, t, o:o + HD], start=True, stop=True)
                        nc.tensor.matmul(ps[p:p + HD, c0 + HD:c0 + P], a_[w, t, o:o + HD], UG[w, hh, 0:HD], start=True, stop=False)
                        mm = nc.tensor.matmul(ps[p:p + HD, c0 + HD:c0 + P], k_[w, t, o:o + HD], v_[w, t, o:o + HD],
                                              start=False, stop=True)
                    mm.then_inc(full["D"], 1)

        def scan_pe(pe, t):
            await_moved(pe, f"WZ1.{t}.1.1")
            for c in range(2):
                ch = 2 * t + c
                if ch:
                    pe.wait_ge(sem("state"), ch)
                    for par in range(2):
                        ps = fill(pe, "D", f"yS.{ch}.{par}")
                        p = slice(par * HD, (par + 1) * HD)
                        for q in range(NP_):
                            mm = nc.tensor.matmul(ps[c * CH:(c + 1) * CH, q * HD:(q + 1) * HD], HT[p, q, c * CH:(c + 1) * CH],
                                                  SS[p, ch % 2, q], start=True, stop=True)
                        mm.then_inc(full["D"], 1)
                    if ch < 3:
                        for par in range(2):
                            ps = fill(pe, "D", f"S.{ch}.{par}")
                            p = slice(par * HD, (par + 1) * HD)
                            for q in range(NP_):
                                mm = nc.tensor.matmul(ps[p, q * HD:(q + 1) * HD], WZ[p, c, q, 0:HD], SS[p, ch % 2, q],
                                                      start=True, stop=True)
                            mm.then_inc(full["D"], 1)

        def rwkv_act(act):
            await_moved_y(act, "y_f0")
            norm_act(act, "f", X)
            for name, lowT, fn in (("lw", wlow, ACT.Tanh), ("la", alow, ACT.Copy)):
                ps = take(act, "A", f"{name}low")
                nc.scalar.activation(lowT[0:DL, 0, :], ps[0:DL, 0:S], fn).then_inc(moved["A"], 1)
                for c in range(2):
                    for t in range(T):
                        ps = take(act, "A", f"{name}.{c}.{t}")
                        dst = s_ if name == "lw" else a_
                        nc.scalar.activation(dst[:, t, c * 512:(c + 1) * 512], ps[:, :], ACT.Sigmoid).then_inc(moved["A"], 1)
            for name, dst in (("w_rk", k_), ("w_rr", r_)):
                for c in range(2):
                    copy_chunk_act(act, f"{name}.{c}.0", dst[:, 0, c * 512:(c + 1) * 512])
            act.wait_ge(sem("xi"), 6)
            for t in range(T):
                if t:
                    act.wait_ge(sem("hats"), t)
                for c in range(2):
                    w = slice(c * 512, (c + 1) * 512)
                    ps = take(act, "A", f"rwcum.{c}.{t}")
                    nc.scalar.activation(Ep[:, w], ps[:, :], ACT.Exp)
                    nc.scalar.activation(Em[:, w], ps[:, :], ACT.Exp, scale=-1.0).then_inc(moved["A"], 1)
                    ps = take(act, "A", f"rwcumx.{c}.{t}")
                    nc.scalar.activation(Ex[:, w], ps[:, :], ACT.Exp).then_inc(moved["A"], 1)
            act.wait_ge(sem("fsum"), 1)
            nc.scalar.activation(fch, fch, ACT.Exp).then_inc(sem("fch"), 1)
            for c in range(2):
                for t in range(T):
                    copy_chunk_act(act, f"w_rv.{c}.{t}", v_[:, t, c * 512:(c + 1) * 512])
            ps = take(act, "A", "glow")
            nc.scalar.activation(glow[:, 0], ps[:, 0:S], ACT.Sigmoid)
            nc.scalar.activation(glow[0:GL - P, 1], ps[0:GL - P, S:], ACT.Sigmoid).then_inc(moved["A"], 1)
            for t in range(T):
                if t:
                    act.wait_ge(sem("hats"), 2)
                for c in range(2):
                    copy_chunk_act(act, f"g.{c}.{t}", g_[:, t, c * 512:(c + 1) * 512])
            act.wait_ge(sem("az_zero"), 2)
            for t in range(T):
                for half in range(2):
                    u = f"{t}.{half}"
                    if t + half:
                        prev = f"{(2 * t + half - 1) // 2}.{(2 * t + half - 1) % 2}"
                        peek(act, f"WZ1.{prev}.1")
                        await_moved(act, f"WZ1.{prev}.1")
                    for gq in range(2):
                        ps = take(act, "A", f"AR.{u}.{gq}")
                        v = ps[:, :].rearrange("p (q n) -> p q n", q=2)
                        nc.scalar.copy(AZ[0:HD, 4 * gq:4 * gq + 4:2], v[0:HD])
                        nc.scalar.copy(AZ[HD:, 4 * gq + 1:4 * gq + 4:2], v[HD:]).then_inc(moved["A"], 1)
                        ps = take(act, "A", f"BK.{u}.{gq}")
                        nc.scalar.copy(BK[:, 2 * gq:2 * gq + 2], ps[:, :].rearrange("p (q n) -> p q n", q=2)).then_inc(moved["A"], 1)
                    for gq in range(2):
                        ps = take(act, "A", f"X2.{u}.{gq}")
                        nc.scalar.copy(Xi[:, 4 * gq:4 * gq + 4].rearrange("p h n -> p (h n)"), ps[:, :]).then_inc(moved["A"], 1)
                    for gq in range(2):
                        ps = take(act, "A", f"Mv.{u}.{gq}")
                        nc.scalar.copy(MV[:, 4 * gq:4 * gq + 4].rearrange("p h n -> p (h n)"), ps[:, 0:S]).then_inc(moved["A"], 1)
                    for gq in range(2):
                        ps = take(act, "A", f"UG.{u}.{gq}")
                        nc.scalar.copy(UG[:, 4 * gq:4 * gq + 4].rearrange("p h n -> p (h n)"), ps[:, :]).then_inc(moved["A"], 1)

        def rwkv_pool(pool):
            norm_pool(pool, "f")
            L = links["pool"]
            pool.wait_ge(sem("rstd_f"), 1)
            nc.gpsimd.memset(wlow[HD:HD + 1], 1.0).then_inc(sem("low_ones"), 1)
            pool.wait_ge(sem("low_ones"), 1)
            nc.gpsimd.memset(alow[HD:HD + 1], 1.0).then_inc(sem("low_ones"), 1)
            pool.wait_ge(sem("low_ones"), 2)
            for t in range(T):
                pool.wait_ge(sem("kk_ss"), t + 1)
                L(nc.gpsimd.tensor_scalar(rst[:, 2 + t], rst[:, t], 1e-24, None, ALU.max))
                nc.gpsimd.tensor_tensor(rst[:, 2 + t], rst[:, 2 + t], neghalf[:, 0:16], ALU.pow).then_inc(sem("kk_norm"), 1)
            pool.wait_ge(sem("hats"), 2)
            peek(pool, "w_rv.1.1")
            nc.gpsimd.memset(AZ[HD:, 0::2], 0.0).then_inc(sem("az_zero"), 1)
            pool.wait_ge(sem("az_zero"), 1)
            nc.gpsimd.memset(AZ[0:HD, 1::2], 0.0).then_inc(sem("az_zero"), 1)
            pool.wait_ge(sem("az_zero"), 2)
            for t in range(T):
                pool.wait_ge(sem("y_var"), t + 1)
                rsqrt(pool, rst[:, 7], rst[:, 6], 16, 1.0, GN_EPS, sem("y_rstd"))

        def rwkv_rows(sp):
            for i, name in enumerate(("rw_k_k_2", "rw_k_a_2", "rw_r_k_2", "rw_ln_w_2", "rw_ln_b_2")):
                src = A[name] if name != "rw_r_k_2" else A[name].rearrange("a h d -> a (h d)")
                sp.dma_start(rows5[:, i], src.to_broadcast([P, D])).then_inc(sem("rows5_in"), 16)

        def rwkv_dve(dve):
            L, V = links["dve"], nc.vector
            norm_dve(dve, "f", "mix_norm_2", gi=KD)
            await_moved(dve, *hT_jobs("f"))
            V.tensor_tensor(dxT[:, :, 1:], hT[:, :, 0:S - 1], hT[:, :, 1:], ALU.subtract)
            L(V.tensor_scalar(dxT[:, :, 0:1], hT[:, :, 0:1], -1.0, None, ALU.mult))

            def shift(i):
                if i >= 2:
                    peek(dve, ("lwlow", "lalow", "w_rk.1.1", "w_rr.1.1")[i - 2])
                mu = ORDER[i][1]
                for k in range(KD):
                    last = V.scalar_tensor_tensor(xi[i % 2][:, k], dxT[:, k], col("rw_mu_2", 1, 8 * mu + k), hT[:, k],
                                                  ALU.mult, ALU.add)
                last.then_inc(sem("xi"), 1)
            shift(0)
            shift(1)
            shift(2)
            shift(3)
            for c in range(2):
                copy_chunk_dve(dve, f"w_rk.{c}.1", k_[:, 1, c * 512:(c + 1) * 512])
            shift(4)
            for c in range(2):
                copy_chunk_dve(dve, f"w_rr.{c}.1", r_[:, 1, c * 512:(c + 1) * 512])
            shift(5)
            ps = take(dve, "D", "fraw")
            V.tensor_copy(fraw.rearrange("p q t c -> p (q t c)"), ps[:, 0:64]).then_inc(moved["D"], 1)
            await_moved(dve, "fraw")
            for n in range(3):
                t0, c0, t1, c1 = n // 2, n % 2, (n + 1) // 2, (n + 1) % 2
                last = V.tensor_tensor(fch[:, n], fraw[:, :, t0, c0], fraw[:, :, t1, 2 + c1], ALU.add)
            last.then_inc(sem("fsum"), 1)
            dve.wait_ge(sem("rows5_in"), 80)
            dve.wait_ge(sem("xi"), 6)
            h16 = lambda v: v.rearrange("p (h d) -> p h d", h=RH)
            await_moved(dve, "w_rk.1.0", "w_rk.1.1", "w_rr.1.0", "w_rr.1.1", "la.1.1")
            for t in range(T):
                r, k, a, s = r_[:, t], k_[:, t], a_[:, t], s_[:, t]
                L(V.tensor_tensor(kk, k, k_k, ALU.mult))
                L(V.tensor_tensor(tmpk, kk, kk, ALU.mult))
                V.reduce_sum(rst[:, t], h16(tmpk), AX.X).then_inc(sem("kk_ss"), 1)
                dve.wait_ge(sem("kk_ss"), t + 1)
                L(V.scalar_tensor_tensor(tmpk, a, -1.0, k_a, ALU.add, ALU.mult))
                L(V.scalar_tensor_tensor(k, tmpk, 1.0, k, ALU.add, ALU.mult))
                L(V.tensor_tensor(tmpk, r, k, ALU.mult))
                L(V.tensor_tensor(tmpk, tmpk, r_k, ALU.mult))
                L(V.reduce_sum(rst[:, 4 + t], h16(tmpk), AX.X))
                dve.wait_ge(sem("kk_norm"), t + 1)
                L(V.tensor_tensor(h16(kk), h16(kk), bc(rst[:, 2 + t], HD, 2), ALU.mult))
                await_moved(dve, f"rwcum.1.{t}", f"rwcumx.1.{t}")
                L(V.tensor_tensor(a, a, kk, ALU.mult))
                V.tensor_tensor(a, a, Em, ALU.mult)
                peek(dve, "fraw")
                V.scalar_tensor_tensor(s, kk, -1.0, Ex, ALU.mult, ALU.mult)
                V.tensor_tensor(r, r, Ep, ALU.mult)
                V.tensor_tensor(k, k, Em, ALU.mult).then_inc(sem("hats"), 1)
                dve.wait_ge(sem("hats"), t + 1)
            dve.wait_ge(sem("const2_in"), 16)
            peek(dve, "g.1.1")
            for t in range(T):
                for half in range(2):
                    heads_dve(dve, t, half)
                scan_dve(dve, t)
            for t in range(T):
                for half in range(2):
                    ps = take(dve, "D", f"ryT.{t}.{half}")
                    V.tensor_copy(mixT[:, half * 4:half * 4 + 4, t * P:(t + 1) * P],
                                  ps[:, :].rearrange("p (k n) -> p k n", k=4)).then_inc(moved["D"], 1)
            residual_dve(dve, "w_ro")

        def heads_dve(dve, t, half):
            V = nc.vector
            u = f"{t}.{half}"
            for h in range(8):
                ps = take(dve, "D", f"NM.{u}.{h}")
                V.tensor_tensor(NM[:, h], ps[:, :], C("rwmask"), ALU.mult).then_inc(moved["D"], 1)
                if h % 4 == 3:
                    g4 = slice(h - 3, h + 1)
                    await_moved(dve, f"NM.{u}.{h}")
                    links["dve"](V.tensor_tensor(Yi[:, g4], NM[:, g4, 0:P], bc(C("rwlevT"), 4, 1), ALU.mult))
                    V.tensor_tensor(Yi[:, g4], Yi[:, g4], bc(ident, 4, 1), ALU.add).then_inc(sem("Y2"), 1)
            four = lambda ps: ps[:, :].rearrange("p (h n) -> p h n", h=4)
            for lv in range(5):
                for gq in range(2):
                    g4 = slice(4 * gq, 4 * gq + 4)
                    ps = take(dve, "D", f"P{lv}.{u}.{gq}")
                    V.tensor_tensor(PM[:, g4], four(ps), bc(C("rwlev")[:, lv * P:(lv + 1) * P], 4, 1),
                                    ALU.mult).then_inc(moved["D"], 1)
                for gq in range(2):
                    g4 = slice(4 * gq, 4 * gq + 4)
                    if lv < 4:
                        ps = take(dve, "D", f"dX{lv}.{u}.{gq}")
                        if lv == 0:
                            await_moved(dve, f"X2.{u}.{gq}")
                        V.tensor_tensor(Xi[:, g4], Xi[:, g4], four(ps), ALU.add).then_inc(moved["D"], 1)
                    ps = take(dve, "D", f"dY{lv}.{u}.{gq}")
                    V.tensor_tensor(Yi[:, g4], Yi[:, g4], four(ps), ALU.add).then_inc(moved["D"], 1)
            for gq in range(2):
                ps = take(dve, "D", f"yH.{u}.{gq}")
                o = 512 * half + S * gq
                q2 = slice(4 * half + 2 * gq, 4 * half + 2 * gq + 2)
                V.tensor_copy(Y0[:, o:o + S], ps[:, 0:S])
                v = ps[:, S:].rearrange("p (q n) -> p q n", q=2)
                V.tensor_tensor(HT[0:HD, q2], v[0:HD], AZ[0:HD, 4 * gq:4 * gq + 4:2, P:], ALU.add)
                V.tensor_tensor(HT[HD:, q2], v[HD:], AZ[HD:, 4 * gq + 1:4 * gq + 4:2, P:], ALU.add).then_inc(moved["D"], 1)
                for c in range(2):
                    ps = take(dve, "D", f"WZ{c}.{u}.{gq}")
                    v = ps[:, 0:S].rearrange("p (q n) -> p q n", q=2)
                    V.tensor_tensor(WZ[:, c, q2, 0:HD], v[:, :, 0:HD], bc(C("eye2"), 2, 1), ALU.add)
                    V.tensor_copy(WZ[:, c, q2, HD:], v[:, :, HD:]).then_inc(moved["D"], 1)

        def scan_dve(dve, t):
            L, V = links["dve"], nc.vector
            await_moved(dve, f"WZ1.{t}.1.1")
            for c in range(2):
                ch = 2 * t + c
                if ch:
                    for par in range(2):
                        ps = take(dve, "D", f"yS.{ch}.{par}")
                        w = slice(c * CH, (c + 1) * CH)
                        y = Y0[w, :].rearrange("p (q x d) -> p q x d", q=NP_, x=2)[:, :, par]
                        V.tensor_tensor(y, y, ps[w, :].rearrange("p (q d) -> p q d", q=NP_), ALU.add).then_inc(moved["D"], 1)
                    if ch < 3:
                        for par in range(2):
                            p = slice(par * HD, (par + 1) * HD)
                            ps = take(dve, "D", f"S.{ch}.{par}")
                            V.tensor_tensor(SS[p, (ch + 1) % 2], ps[p, :].rearrange("p (q d) -> p q d", q=NP_),
                                            WZ[p, c, :, HD:], ALU.add).then_inc(moved["D"], 1)
                        await_moved(dve, f"S.{ch}.1")
                        dve.wait_ge(sem("fch"), 1)
                        nxt = SS[:, (ch + 1) % 2]
                        V.tensor_tensor(nxt, nxt, bc(fch[:, ch], HD, 2), ALU.mult).then_inc(sem("state"), 1)
                else:
                    dve.wait_ge(sem("fch"), 1)
                    V.tensor_tensor(SS[:, 1], WZ[:, 0, :, HD:], bc(fch[:, 0], HD, 2), ALU.mult).then_inc(sem("state"), 1)
            if 2 * t + 1:
                await_moved(dve, f"yS.{2 * t + 1}.1")
            y, o = Y0, r_[:, t]
            h16 = lambda v: v.rearrange("p (h d) -> p h d", h=RH)
            bn = rst[:, 12:18].rearrange("p a b -> p (a b)").rearrange("p (h s) -> p h s", h=RH)
            mv = rst[:, 18:20].rearrange("p a b -> p (a b)").rearrange("p (h s) -> p h s", h=RH)
            if t:
                dve.wait_ge(sem("y_rstd"), t)
            for h in range(RH):
                last = V.bn_stats(bn[:, h], y[:, h * HD:(h + 1) * HD])
            L(last)
            for h in range(RH):
                last = V.bn_aggr(mv[:, h], bn[:, h])
            L(last)
            V.tensor_copy(rst[:, 6], mv[:, :, 1]).then_inc(sem("y_var"), 1)
            L(V.tensor_tensor(h16(o), h16(y), bc(mv[:, :, 0], HD, 2), ALU.subtract))
            dve.wait_ge(sem("y_rstd"), t + 1)
            L(V.tensor_tensor(h16(o), h16(o), bc(rst[:, 7], HD, 2), ALU.mult))
            L(V.tensor_tensor(o, o, ln_w, ALU.mult))
            L(V.tensor_tensor(o, o, ln_b, ALU.add))
            L(V.tensor_tensor(h16(Y0), h16(v_[:, t]), bc(rst[:, 4 + t], HD, 2), ALU.mult))
            L(V.tensor_tensor(o, o, Y0, ALU.add))
            V.tensor_tensor(o, o, g_[:, t], ALU.mult).then_inc(sem("y_done"), 1)
            dve.wait_ge(sem("y_done"), t + 1)

        def await_moved_y(eng, name):
            if name in jobs:
                await_moved(eng, name)

        pe_fns.append(("F", rwkv_pe)); act_fns.append(("F", rwkv_act))
        pool_fns.append(("F", rwkv_pool)); dve_fns.append(("F", rwkv_dve))

        add_swiglu("G", "f1", 1, lambda act: await_moved(act, *residual_jobs("w_ro")), ("ryT.1.1",))

        def sp_stream(sp):
            names = [u[0] for u in units]
            cut = unit_at[f"moe.d.{G * EPG - 1}"] + 1 if "C" in phases and "O" in phases else 0
            stream(sp, names[:cut])
            if cut:
                overflow_sp(sp)
            if "F" in phases:
                first = unit_at["lw1"]
                stream(sp, names[cut:first])
                if "D" in phases:
                    peek(sp, "fo.1")
                    await_moved(sp, *residual_jobs("w_out2"))
                rwkv_rows(sp)
                stream(sp, names[first:])
            else:
                stream(sp, names[cut:])

        block = ctx.enter_context(nc.Block())

        @block.tensor
        def _(pe):
            start_pe(pe)
            for ph, f in pe_fns:
                if ph in phases:
                    f(pe)

        @block.scalar
        def _(act):
            links["act"] = chain(act, "act_step")
            start_act_dma(act)
            act.wait_ge(sem("x_in"), 16)
            for ph, f in act_fns:
                if ph in phases:
                    f(act)

        @block.vector
        def _(dve):
            links["dve"] = chain(dve, "dve_step")
            start_dve(dve)
            for ph, f in dve_fns:
                if ph in phases:
                    f(dve)

        @block.gpsimd
        def _(pool):
            links["pool"] = chain(pool, "pool_step")
            start_pool_dma(pool)
            for ph, f in pool_fns:
                if ph in phases:
                    f(pool)

        @block.sync
        def _(sp):
            start_sp(sp)
            sp_stream(sp)
            drained(sp, *[r for r in RINGS if not r.endswith("o")])
            sp.dma_start(out[0].rearrange("(t p) d -> p t d", p=P), X[:, :, :]).then_inc(sem("out"), 16)
            sp.wait_ge(sem("out"), 16)


def kernel(**inputs):
    import concourse.bacc as _bacc
    from concourse.bass_utils import run_bass_kernel_spmd as _run

    nc = _bacc.Bacc("TRN2", target_bir_lowering=False, num_devices=1)
    arrays, args = {}, {}
    for name, a in list(inputs.items()) + [("const_table", CONSTANTS)]:
        a = np.ascontiguousarray(a)
        if a.size == 0:
            continue
        arrays[name] = a
        args[name] = nc.dram_tensor(name, a.shape, mybir.dt.from_np(a.dtype), kind="ExternalInput").ap()
    out = nc.dram_tensor("y", (1, S, D), F32, kind="ExternalOutput").ap()
    build(nc, out, **args)
    r = _run(nc, [arrays], core_ids=[0])
    return r.results[0]["y"]
```

```python
from contextlib import ExitStack

import numpy as np
import concourse.bass as bass
from concourse import mybir

F32 = mybir.dt.float32
R32 = mybir.dt.float32r
I32 = mybir.dt.int32
ALU = mybir.AluOpType
ACT = mybir.ActivationFunctionType
AX = mybir.AxisListType

P = 128
S = 256
T = S // P
D = 1024
KD = D // P
EPS = 1e-6
NEG = -1e30

QR, KVR, RD, RW = 256, 128, 64, 512
H, ND, VD = 4, 128, 128
QK = ND + RD
IN1 = QR + KVR + RD + 4 * RW
G, EPG, FF = 4, 8, 256
FH, HD, FW = 8, 64, 512
IN2 = 4 * FW + FH + FW
POOLS = (2, 4, 8, 16)
DFF = 2816
RH = D // HD
GN_EPS = 64e-5
CH = 64
GL, DL = 160, 64

CONST = {}


def _constants():
    i = np.arange(P)
    parts = {}
    parts["ident"] = np.eye(P)
    causal = np.where(i[None, :] <= i[:, None], 0.0, NEG)
    parts["cmask"] = np.concatenate([causal, np.zeros((P, P)), causal], 1)
    lg = np.log(1.0 - 2.0 ** (-5.0 - np.arange(H)))
    dec = np.zeros((P, H, 3, P))
    for h in range(H):
        d = i[None, :] - i[:, None]
        diag = np.where(d >= 0, np.exp(np.maximum(d, 0) * lg[h]), 0.0)
        dec[:, h, 0] = diag
        dec[:, h, 1] = np.exp((d + P) * lg[h])
        dec[:, h, 2] = diag
    parts["decay"] = (dec * P ** -0.5).reshape(P, -1)
    half = 64
    parts["invf"] = np.repeat((10000.0 ** (-np.arange(half, dtype=np.float64) / half))[None], P, 0)
    parts["tri"] = (i[:, None] <= i[None, :]).astype(float)
    parts["ones"] = np.ones((P, P))
    pool = np.zeros((P, 4, 3, P))
    j = np.arange(S)
    for g, w in enumerate(POOLS):
        m = np.where((j[:, None] <= j[None, :]) & (j[:, None] > j[None, :] - w), 1.0, 0.0)
        m = m / np.minimum(j + 1, w)[None, :] - np.eye(S)
        pool[:, g, 0] = m[:P, :P]
        pool[:, g, 1] = m[:P, P:]
        pool[:, g, 2] = m[P:, P:]
    parts["pool"] = pool.reshape(P, -1)
    sel = np.zeros((P, FH, P))
    for h in range(FH):
        sel[h, h] = 1.0
    parts["sel"] = sel.reshape(P, -1)
    blk = i // CH
    same = blk[:, None] == blk[None, :]
    strict = same & (i[:, None] < i[None, :])
    incl = same & (i[:, None] <= i[None, :])
    parts["rwmask"] = np.concatenate([strict, incl, strict, incl], 1).astype(float)
    mid = blk * CH + CH // 2 - 1
    half_to_mid = (same & (i[:, None] <= mid[None, :])).astype(float)
    c = -np.exp(-0.5)
    parts["rwcum"] = c * (incl - half_to_mid)
    parts["rwcumx"] = c * (strict - half_to_mid)
    parts["rwmid"] = c * half_to_mid
    parts["eye2"] = np.concatenate([np.eye(CH)] * 2, 0)
    lv = []
    b = 1
    while b < CH:
        m = (i[:, None] // (2 * b) == i[None, :] // (2 * b)) & ((i[:, None] // b) % 2 == 1) & ((i[None, :] // b) % 2 == 0)
        lv.append(m)
        b *= 2
    parts["rwlev"] = np.concatenate(lv[1:], 1).astype(float)
    parts["rwlevT"] = lv[0].T.astype(float)
    parts["strictP"] = (i[:, None] < i[None, :]).astype(float)
    parts["iota"] = np.repeat(np.arange(P)[None], P, 0)
    parts["gidx"] = np.repeat(np.arange(8)[None], P, 0)
    out, at = [], 0
    for k, v in parts.items():
        CONST[k] = (at, at + v.shape[1])
        at += v.shape[1]
        out.append(v.astype(np.float32))
    return np.ascontiguousarray(np.concatenate(out, 1))


CONSTANTS = _constants()

ROWS = [("attn_norm_g", 8), ("mla_q_norm_g", 2), ("mla_kv_norm_g", 1), ("ret_gn_g", 4), ("cross_norm_g", 8),
        ("mem_norm_g", 8), ("cross_q_qk_g", 2), ("cross_k_qk_g", 2), ("moe_norm_g", 8), ("mix_norm_2", 16),
        ("ffn_norm_2", 16), ("hy_pool_scale_2", 4), ("rw_mu_2", 48)]
COL = {}
_at = 0
for _n, _r in ROWS:
    COL[_n] = _at
    _at += _r
NROWS = _at


def build(nc, out, phases="ABCDEFGO", **A):
    ctx = ExitStack()
    with ctx:
        def sb(name, shape, dt=F32):
            return ctx.enter_context(nc.sbuf_tensor(name, shape, dt))

        rounded_at, rounded_views = {}, {}

        def sb_both(name, n):
            plain = sb(name, [P, n])
            rounded_at[name] = nc.sbuf_base - 4 * n
            return plain

        def rounded(name, at, n):
            if (name, at, n) not in rounded_views:
                rounded_views[name, at, n] = nc.alloc_sbuf_tensor_at(f"{name}_rounded_{at}_{n}", [P, n], R32,
                                                                     offset=rounded_at[name] + 4 * at)
            return rounded_views[name, at, n][:, :]

        sems = {}

        def sem(name):
            if name not in sems:
                sems[name] = ctx.enter_context(nc.semaphore(name))
            return sems[name]

        def dram2(name, i=0):
            return A[name][i]

        BANK = [ctx.enter_context(nc.psum_tensor(f"bank{i}", [P, 512], F32)) for i in range(8)]
        RINGS = {"D": BANK[0:4], "A": BANK[4:8],
                 "GU": BANK[0:2], "TT": BANK[2:4], "Y": [BANK[4:6]], "Z": BANK[6:8],
                 "Y4": [BANK[4:8]],
                 "N": BANK[2:4]}
        for r in ("GU", "TT", "Y", "Z"):
            RINGS[r + "o"] = RINGS[r]
        full = {r: sem(f"full_{r}") for r in RINGS}
        moved = {r: sem(f"moved_{r}") for r in RINGS}
        jobs = {}
        filled = {r: 0 for r in RINGS}
        taken = {r: 0 for r in RINGS}

        def fill(pe, ring, name):
            n, size = filled[ring], len(RINGS[ring])
            filled[ring] += 1
            jobs[name] = (ring, n)
            if n >= size:
                pe.wait_ge(moved[ring], n - size + 1)
            return RINGS[ring][n % size]

        def take(eng, ring, name):
            n = taken[ring]
            assert jobs[name] == (ring, n), (name, jobs[name], ring, n)
            taken[ring] += 1
            eng.wait_ge(full[ring], n + 1)
            return RINGS[ring][n % len(RINGS[ring])]

        def peek(eng, name):
            ring, n = jobs[name]
            eng.wait_ge(full[ring], n + 1)
            return RINGS[ring][n % len(RINGS[ring])]

        def await_moved(eng, *names):
            need = {}
            for name in names:
                ring, n = jobs[name]
                need[ring] = max(need.get(ring, 0), n + 1)
            for ring, n in need.items():
                eng.wait_ge(moved[ring], n)

        def drained(eng, *rings):
            for r in rings:
                if filled[r]:
                    eng.wait_ge(moved[r], filled[r])

        SLOT, SLOTS = 2048, 8
        ring_w = sb_both("ring_w", SLOTS * SLOT)
        arrived = [sem(f"arrived_{i}") for i in range(SLOTS + 4)]
        units = []
        unit_at = {}
        released = {}
        next_slot = [0]
        posted = [0] * (SLOTS + 4)
        holder = [None] * (SLOTS + 4)
        waits_for = {}

        def slot_view(slots, parts, kt, cols, as_rounded=False):
            if slots[0] < SLOTS:
                name, base, at = "ring_w", ring_w, slots[0] * SLOT
            else:
                name, base, at = "work", work, EXTRA + (slots[0] - SLOTS) * SLOT
            if as_rounded:
                return rounded(name, at, kt * cols).rearrange("p (k n) -> p k n", k=kt)
            return base[0:parts, at:at + kt * cols].rearrange("p (k n) -> p k n", k=kt)

        def place(name, slots, pieces):
            n = unit_at[name] = len(units)
            waits_for[n] = {holder[s] for s in slots} - {None}
            for s in slots:
                holder[s] = n
            posted[slots[0]] += 16 * len(pieces)
            units.append((name, pieces, slots, posted[slots[0]]))

        views = {}
        fence = {}

        def unit(name, src, kt, cols, parts=P, slot=None, pieces=None):
            s = next_slot[0] if slot is None else slot
            next_slot[0] = (s + 1) % SLOTS
            views[name] = (s,), parts, kt, cols
            place(name, (s,), [(src, None)] if pieces is None else pieces(unit_view_at(name)))

        def unit_view_at(name):
            return slot_view(*views[name])

        def unit_view(name, as_rounded=False):
            return slot_view(*views[name], as_rounded)

        def weights(pe, name, last_job=None):
            n = unit_at[name]
            _, _, slots, value = units[n]
            pe.wait_ge(arrived[slots[0]], value)
            if last_job is not None:
                released[n] = last_job
            return unit_view(name)

        def stream(sp, names):
            for name in names:
                n = unit_at[name]
                _, pieces, slots, _ = units[n]
                for m in sorted(waits_for[n]):
                    r = released[m]
                    if isinstance(r, str):
                        ring, k = jobs[r]
                        r = (full[ring], k + 1)
                    sp.wait_ge(*r)
                if slots[0] >= SLOTS or name.startswith("f1"):
                    for job in fence.get(name.split(".")[0], ()):
                        ring, k = jobs[job if job in jobs else "cols"]
                        sp.wait_ge(full[ring], k + 1)
                for src, dst in pieces:
                    sp.dma_start(unit_view(name) if dst is None else dst, src).then_inc(arrived[slots[0]], 16)

        def linear_units(name, w, n_cols, k=D):
            kt = k // P
            for c in range(0, n_cols, 512):
                w_ = min(512, n_cols - c)
                step = max(1, min(kt, SLOT // w_))
                for k0 in range(0, kt, step):
                    unit(f"{name}.{c // 512}.{k0}",
                         w[k0 * P:(k0 + step) * P, c:c + w_].rearrange("(k p) n -> p k n", p=P), step, w_)

        def linear(pe, name, lhsT, n_cols, rings, k=D, second=None):
            kt = k // P
            for c in range(0, n_cols, 512):
                w_ = min(512, n_cols - c)
                step = max(1, min(kt, SLOT // w_))
                last = f"{name}.{c // 512}.{T - 1}"
                wv = [weights(pe, f"{name}.{c // 512}.{k0}", last) for k0 in range(0, kt, step)]
                for t in range(T):
                    if t and c == 0 and second is not None:
                        second()
                    ps = fill(pe, rings[t], f"{name}.{c // 512}.{t}")
                    for kk in range(kt):
                        mm = nc.tensor.matmul(ps[:, 0:w_], lhsT[:, kk, t * P:(t + 1) * P],
                                              wv[kk // step][:, kk % step, :], start=kk == 0, stop=kk == kt - 1)
                    mm.then_inc(full[rings[t]], 1)

        def chain(eng, name):
            s, n = sem(name), [0]

            def link(ins):
                n[0] += 1
                ins.then_inc(s, 1)
                eng.wait_ge(s, n[0])
            return link

        X = sb("X", [P, T, D])
        const = sb("const", [P, CONSTANTS.shape[1]])
        cols = sb("cols", [P, P + 2])
        neghalf = sb("neghalf", [P, 32])
        rowsmall = sb("rowsmall", [P, 512])
        stat = sb("stat", [P, 256])
        cossin = sb("cossin", [P, T, 2, 64])
        post = sb("post", [P, T], I32)
        WORK = 26496
        EXTRA = 12288
        work = sb_both("work", WORK)

        def C(name):
            a, b = CONST[name]
            return const[:, a:b]

        ident = C("ident")

        def col(name, n, i=0):
            return cols[:, COL[name] + i:COL[name] + i + n]

        def view(at, *shape, as_rounded=False):
            n = int(np.prod(shape))
            assert at + n <= WORK, (at, n)
            v = rounded("work", at, n) if as_rounded else work[:, at:at + n]
            if len(shape) == 2:
                v = v.rearrange("p (a b) -> p a b", a=shape[0])
            elif len(shape) == 3:
                v = v.rearrange("p (a b c) -> p a b c", a=shape[0], b=shape[1])
            elif len(shape) == 4:
                v = v.rearrange("p (a b c d) -> p a b c d", a=shape[0], b=shape[1], c=shape[2])
            return v

        def view_r(at, *shape):
            return view(at, *shape, as_rounded=True)

        def bc(ap, n, axis):
            v = ap.unsqueeze(axis)
            shape = list(v.shape)
            shape[axis] = n
            return v.to_broadcast(shape)

        hT = view(0, KD, S)
        mixT = view(2048, KD, S)
        xn = view(4096, T, D)
        sq = xn
        pe_fns, dve_fns, act_fns, pool_fns, sp_fns = [], [], [], [], []
        links = {}
        early_cuts = {}

        def norm_act(act, u, src, xn=xn, sq=sq, dst_stat=0, ready=None):
            for t in range(T):
                if ready is not None:
                    ready(t)
                nc.scalar.activation(sq[:, t], src[:, t], ACT.Square,
                                     accum_out=stat[:, dst_stat + t:dst_stat + t + 1]).then_inc(sem(f"ss_{u}"), 1)
                act.wait_ge(sem(f"rstd_{u}"), t + 1)
                nc.scalar.activation(xn[:, t], src[:, t], ACT.Copy,
                                     scale=stat[:, dst_stat + 2 + t:dst_stat + 3 + t]).then_inc(sem(f"xn_{u}"), 1)

        def rsqrt(pool, dst, src, n, mul, eps, done):
            links["pool"](nc.gpsimd.tensor_scalar(dst, src, mul, eps, ALU.mult, ALU.add))
            nc.gpsimd.tensor_tensor(dst, dst, neghalf[:, 0:n], ALU.pow).then_inc(done, 1)

        def norm_pool(pool, u, dst_stat=0):
            for t in range(T):
                pool.wait_ge(sem(f"ss_{u}"), t + 1)
                rsqrt(pool, stat[:, dst_stat + 2 + t:dst_stat + 3 + t], stat[:, dst_stat + t:dst_stat + t + 1], 1, 1.0 / D,
                      EPS, sem(f"rstd_{u}"))

        def norm_pe(pe, u, xn=xn, tiles=range(T), ring="D"):
            for t in tiles:
                pe.wait_ge(sem(f"xn_{u}"), t + 1)
                for half in range(2):
                    ps = fill(pe, ring, f"hT_{u}.{t}.{half}")
                    for k in range(4):
                        kk = half * 4 + k
                        mm = nc.tensor.transpose(ps[:, k * P:(k + 1) * P], xn[:, t, kk * P:(kk + 1) * P], ident)
                    mm.then_inc(full[ring], 1)

        def norm_dve(dve, u, gain, hT=hT, gi=0, tiles=range(T)):
            for t in tiles:
                for half in range(2):
                    ps = take(dve, "D", f"hT_{u}.{t}.{half}")
                    nc.vector.tensor_tensor(hT[:, half * 4:half * 4 + 4, t * P:(t + 1) * P],
                                            ps[:, :].rearrange("p (k n) -> p k n", k=4),
                                            bc(col(gain, 4, gi + half * 4), P, 2), ALU.mult).then_inc(moved["D"], 1)

        def hT_jobs(u, tiles=range(T)):
            return [f"hT_{u}.{t}.{h}" for t in tiles for h in range(2)]

        def norm_linear(pe, u, name, n_cols, rings):
            def second():
                norm_pe(pe, u, tiles=(1,))
                await_moved(pe, *hT_jobs(u, (1,)))
            norm_pe(pe, u, tiles=(0,))
            await_moved(pe, *hT_jobs(u, (0,)))
            linear(pe, name, hT, n_cols, rings, second=second)

        rows_in = view(18100, P)
        n_const1 = CONST["invf"][1]
        q_g, k_g, bias_e, bias_g, fbias = (rowsmall[:, 0:QK], rowsmall[:, QK:2 * QK], rowsmall[:, 384:416],
                                           rowsmall[:, 416:420], rowsmall[:, 420:428])

        def row_dma(eng, name, r):
            src = A[name]
            axes = "abc"[:len(src.shape)]
            flat = src.rearrange(" ".join(axes) + " -> (" + " ".join(axes) + ")") if len(axes) > 1 else src
            eng.dma_start(rows_in[COL[name]:COL[name] + r, :], flat.rearrange("(r c) -> r c", c=P)).then_inc(sem("rows_in"), 16)

        def start_sp(sp):
            sp.dma_start(const[:, 0:P], A["const_table"][:, 0:P]).then_inc(sem("ident_in"), 16)
            sp.dma_start(X[:, 0], A["x"][0, 0:P]).then_inc(sem("x_in"), 16)
            sp.dma_start(X[:, 1], A["x"][0, P:S]).then_inc(sem("x_in"), 16)
            for name, r in ROWS[5:]:
                row_dma(sp, name, r)

        def second_sp(sp):
            sp.dma_start(const[:, P:n_const1], A["const_table"][:, P:n_const1]).then_inc(sem("const_in"), 16)
            if "B" in phases:
                sp.dma_start(mem, A["mem"][0].rearrange("(t p) d -> p t d", p=P)).then_inc(sem("mem_in"), 16)

        def small_sp(sp):
            for dst, name in ((q_g, "mla_q_qk_g"), (k_g, "mla_k_qk_g"), (bias_e, "router_b_expert"),
                              (bias_g, "router_b_group"), (fbias, "hy_f_bias_2")):
                sp.dma_start(dst, A[name].to_broadcast([P, dst.shape[1]])).then_inc(sem("rowsmall_in"), 16)
            for i, name in enumerate(("hy_q_gain_2", "hy_k_gain_2")):
                for half in range(2):
                    sp.dma_start(cols[half * HD:(half + 1) * HD, P + i:P + i + 1],
                                 A[name][0].unsqueeze(1)).then_inc(sem("gain2_in"), 16)
            sp.dma_start(const[:, n_const1:], A["const_table"][:, n_const1:]).then_inc(sem("const2_in"), 16)

        def start_act_dma(act):
            for name, r in ROWS[:5]:
                row_dma(act, name, r)

        def start_pool(pool):
            nc.gpsimd.memset(neghalf[:, :], -0.5).then_inc(sem("neghalf"), 1)
            pool.wait_ge(sem("neghalf"), 1)
            for t in range(T):
                pool.dma_start(post[:, t:t + 1], A["positions"][0, t * P:(t + 1) * P].unsqueeze(1)).then_inc(sem("pos_in"), 16)

        def start_pe(pe):
            pe.wait_ge(sem("ident_in"), 16)
            pe.wait_ge(sem("rows_in"), 16 * len(ROWS))
            ps = fill(pe, "D", "cols")
            nc.tensor.transpose(ps[:, 0:NROWS], rows_in[0:NROWS, :], ident[0:NROWS, 0:NROWS]).then_inc(full["D"], 1)

        def start_dve(dve):
            ps = take(dve, "D", "cols")
            nc.vector.tensor_copy(cols[:, 0:NROWS], ps[:, 0:NROWS]).then_inc(moved["D"], 1)
            dve.wait_ge(moved["D"], 1)

        ang = view(18300, 8, 64)

        def rotary_dve(dve):
            L = links["dve"]
            dve.wait_ge(sem("pos_in"), 32)
            dve.wait_ge(sem("const_in"), 16)
            L(nc.vector.tensor_copy(stat[:, 8:8 + T], post[:, :]))
            turns_i = ang[:, 4:8].bitcast(I32)
            for t in range(T):
                L(nc.vector.tensor_scalar(ang[:, 2 * t], C("invf"), stat[:, 8 + t:9 + t], None, ALU.mult))
                L(nc.vector.tensor_scalar(ang[:, 2 * t + 1], ang[:, 2 * t], float(np.pi / 2), None, ALU.add))
            L(nc.vector.tensor_scalar(ang[:, 4:8], ang[:, 0:4], float(1 / (2 * np.pi)), None, ALU.mult))
            L(nc.vector.tensor_copy(turns_i, ang[:, 4:8]))
            L(nc.vector.tensor_copy(ang[:, 4:8], turns_i))
            c1 = 6.28125
            c2 = float(np.float32(2 * np.pi - c1))
            c2h = float(np.float32(np.round((2 * np.pi - c1) * 2 ** 20) / 2 ** 20))
            for c in (c1, c2h, 2 * np.pi - c1 - c2h):
                L(nc.vector.scalar_tensor_tensor(ang[:, 0:4], ang[:, 4:8], -float(c), ang[:, 0:4], ALU.mult, ALU.add))
            L(nc.vector.tensor_scalar(ang[:, 0:4], ang[:, 0:4], 3.1415925, -3.1415925, ALU.min, ALU.max))
            nc.vector.tensor_copy(cossin[:, :, :, :], ang[:, 0:4].rearrange("p (t c) n -> p t c n", t=T)) \
                .then_inc(sem("angles"), 1)

        def rotary_act(act):
            act.wait_ge(sem("angles"), 1)
            nc.scalar.activation(cossin[:, :, :, :], cossin[:, :, :, :], ACT.Sin).then_inc(sem("cossin"), 1)

        sin_t = lambda t: cossin[:, t, 0]
        cos_t = lambda t: cossin[:, t, 1]

        def rope(eng, ve, link, x, n, half, t, scratch, step, done=None):
            cs, sn = bc(cos_t(t)[:, ::step], n, 1), bc(sin_t(t)[:, ::step], n, 1)
            x1, x2 = x[:, :, 0:half], x[:, :, half:2 * half]
            m = [scratch[:, i * n * half:(i + 1) * n * half].rearrange("p (a b) -> p a b", a=n) for i in range(4)]
            ve.tensor_tensor(m[0], x1, cs, ALU.mult)
            ve.tensor_tensor(m[1], x2, sn, ALU.mult)
            ve.tensor_tensor(m[2], x2, cs, ALU.mult)
            link(ve.tensor_tensor(m[3], x1, sn, ALU.mult))
            ve.tensor_tensor(x1, m[0], m[1], ALU.subtract)
            last = ve.tensor_tensor(x2, m[2], m[3], ALU.add)
            if done is not None:
                last.then_inc(done, 1)
            else:
                link(last)

        proj = view(6912, T, IN1)
        qk = view(11904, T, 2, H, QK)
        val = view(14976, T, H, VD)
        cn = view(16000, T, QR + KVR)
        cT = view(16768, 3, S)
        nopeT = view(17536, 2, H, S)
        ropeT = view(19584, 2, H, S)
        sc = view(11904, H, 3 * P)
        prT = view(13440, H, 3 * P)
        rqkT = view(17536, 2, H, S)
        rsc = view(19584, H, 3 * P)
        ro = view(4096, T, H, P)
        scr = view(4096, 2048)
        O = dict(cq=0, ckv=QR, kpe=QR + KVR, rq=448, rk=960, rv=1472, rg=1984)

        mem = view(11904, T, D)
        memx = view(13952, T, D)
        memsq = view(16000, T, D)
        memkv = view(22400, T, 2 * D)
        mT = view(17536, KD, S)

        if "A" in phases:
            linear_units("w_in", dram2("w_in"), IN1)
            unit("w_uq", A["mla_w_uq"][0].rearrange("(k p) n -> p k n", p=P), 2, H * QK)
            unit("w_ukv", A["mla_w_ukv"][0].rearrange("(k p) n -> p k n", p=P), 1, H * 2 * P)
            if "B" in phases:
                linear_units("w_kv", dram2("cross_w_kv"), 2 * D)
            linear_units("w_out", dram2("w_out"), D)

        def mixA_pe(pe):
            norm_linear(pe, "a", "w_in", IN1, "AD")
            if "B" in phases:
                norm_pe(pe, "m", memx)
            for t in range(T):
                pe.wait_ge(sem("cn"), 2 * (t + 1))
                ps = fill(pe, "D", f"cT.{t}")
                for k in range(3):
                    mm = nc.tensor.transpose(ps[:, k * P:(k + 1) * P], cn[:, t, k * P:(k + 1) * P], ident)
                mm.then_inc(full["D"], 1)
            await_moved(pe, "cT.1")
            uq, ukv = weights(pe, "w_uq", "uq.1.1"), weights(pe, "w_ukv", "ukv.1.1")
            for c, w_ in ((0, 512), (1, 256)):
                for t in range(T):
                    ps = fill(pe, "AD"[t], f"uq.{c}.{t}")
                    for k in range(2):
                        mm = nc.tensor.matmul(ps[:, 0:w_], cT[:, k, t * P:(t + 1) * P], uq[:, k, c * 512:c * 512 + w_],
                                              start=k == 0, stop=k == 1)
                    mm.then_inc(full["AD"[t]], 1)
            for c in range(2):
                for t in range(T):
                    ps = fill(pe, "AD"[t], f"ukv.{c}.{t}")
                    nc.tensor.matmul(ps[:, :], cT[:, 2, t * P:(t + 1) * P], ukv[:, 0, c * 512:(c + 1) * 512],
                                     start=True, stop=True).then_inc(full["AD"[t]], 1)
            if "B" in phases:
                await_moved(pe, *hT_jobs("m"))
                linear(pe, "w_kv", mT, 2 * D, "AA")
            pe.wait_ge(sem("qk_ready"), T)
            for j in range(2):
                for hp in range(2):
                    ps = fill(pe, "AD"[hp], f"nopeT.{j}.{hp}")
                    for h in range(2):
                        for t in range(T):
                            mm = nc.tensor.transpose(ps[:, h * S + t * P:h * S + (t + 1) * P],
                                                     qk[:, t, j, 2 * hp + h, 0:ND], ident)
                    mm.then_inc(full["AD"[hp]], 1)
                for hp in range(2):
                    ps = fill(pe, "AD"[hp], f"ropeT.{j}.{hp}")
                    for h in range(2):
                        for t in range(T):
                            mm = nc.tensor.transpose(ps[0:RD, h * S + t * P:h * S + (t + 1) * P],
                                                     qk[:, t, j, 2 * hp + h, ND:QK], ident)
                    mm.then_inc(full["AD"[hp]], 1)
            await_moved(pe, "ropeT.1.0", "ropeT.1.1")
            for h in range(H):
                ps = fill(pe, "D", f"score.{h}")
                for lo, hi, n in ((0, P, P), (P, 3 * P, S)):
                    tq = lo // P
                    nc.tensor.matmul(ps[:, lo:hi], nopeT[:, 0, h, tq * P:(tq + 1) * P], nopeT[:, 1, h, 0:n],
                                     start=True, stop=False)
                    mm = nc.tensor.matmul(ps[:, lo:hi], ropeT[0:RD, 0, h, tq * P:(tq + 1) * P],
                                          ropeT[0:RD, 1, h, 0:n], start=False, stop=True)
                mm.then_inc(full["D"], 1)
            pe.wait_ge(sem("rqk_ready"), T)
            for j in range(2):
                for hp in range(2):
                    ps = fill(pe, "A", f"rqkT.{j}.{hp}")
                    for h in range(2):
                        for t in range(T):
                            o = O["rq"] + j * 512 + (2 * hp + h) * P
                            mm = nc.tensor.transpose(ps[:, h * S + t * P:h * S + (t + 1) * P],
                                                     proj[:, t, o:o + P], ident)
                    mm.then_inc(full["A"], 1)
            pe.wait_ge(sem("prob"), T)
            for h in range(H):
                ps = fill(pe, "A", f"prT.{h}")
                for b in range(3):
                    mm = nc.tensor.transpose(ps[:, b * P:(b + 1) * P], sc[:, h, b * P:(b + 1) * P], ident)
                mm.then_inc(full["A"], 1)
            await_moved(pe, "rqkT.1.1")
            for h in range(H):
                ps = fill(pe, "D", f"rscore.{h}")
                nc.tensor.matmul(ps[:, 0:S], rqkT[:, 1, h, 0:P], rqkT[:, 0, h, :], start=True, stop=True)
                nc.tensor.matmul(ps[:, S:3 * P], rqkT[:, 1, h, P:S], rqkT[:, 0, h, P:S],
                                 start=True, stop=True).then_inc(full["D"], 1)
            await_moved(pe, "prT.3")
            for hp in range(2):
                ps = fill(pe, "A", f"oT.{hp}")
                for h in (2 * hp, 2 * hp + 1):
                    o = (h % 2) * S
                    nc.tensor.matmul(ps[:, o:o + S], val[:, 0, h], prT[:, h, 0:S], start=True, stop=False)
                    mm = nc.tensor.matmul(ps[:, o + P:o + S], val[:, 1, h], prT[:, h, S:3 * P], start=False, stop=True)
                mm.then_inc(full["A"], 1)
            await_moved(pe, "rscore.3")
            rv = lambda t, h: proj[:, t, O["rv"] + h * P:O["rv"] + (h + 1) * P]
            for t in range(T):
                ps = fill(pe, "D", f"ro.{t}")
                for h in range(H):
                    o = slice(h * P, (h + 1) * P)
                    if t == 0:
                        mm = nc.tensor.matmul(ps[:, o], rsc[:, h, 0:P], rv(0, h), start=True, stop=True)
                    else:
                        nc.tensor.matmul(ps[:, o], rsc[:, h, P:S], rv(0, h), start=True, stop=False)
                        mm = nc.tensor.matmul(ps[:, o], rsc[:, h, S:3 * P], rv(1, h), start=False, stop=True)
                mm.then_inc(full["D"], 1)
            for t in range(T):
                pe.wait_ge(sem("ro_gated"), t + 1)
                ps = fill(pe, "D", f"roT.{t}")
                for h in range(H):
                    mm = nc.tensor.transpose(ps[:, h * P:(h + 1) * P], ro[:, t, h], ident)
                mm.then_inc(full["D"], 1)
            await_moved(pe, "roT.1", "oT.1")
            linear(pe, "w_out", mixT, D, "DD")

        def copy_chunk_act(act, name, dst):
            ps = take(act, "A", name)
            nc.scalar.copy(dst, ps[:, 0:dst.shape[1]] if len(dst.shape) == 2 else
                           ps[:, 0:dst.shape[1] * dst.shape[2]].rearrange("p (a b) -> p a b", a=dst.shape[1])
                           ).then_inc(moved["A"], 1)

        def copy_chunk_dve(dve, name, dst):
            ps = take(dve, "D", name)
            nc.vector.tensor_copy(dst, ps[:, 0:dst.shape[1]] if len(dst.shape) == 2 else
                                  ps[:, 0:dst.shape[1] * dst.shape[2]].rearrange("p (a b) -> p a b", a=dst.shape[1])
                                  ).then_inc(moved["D"], 1)

        def mixA_act(act):
            norm_act(act, "a", X)
            if "B" in phases:
                act.wait_ge(sem("mem_in"), 16)
                norm_act(act, "m", mem, memx, memsq, 24)
            rotary_act(act)
            for c in range(5):
                w_ = min(512, IN1 - c * 512)
                copy_chunk_act(act, f"w_in.{c}.0", proj[:, 0, c * 512:c * 512 + w_])
                if c == 0:
                    await_moved(act, "w_in.0.0", "w_in.0.1")
                    for t in range(T):
                        for i, (o, w2) in enumerate(((0, QR), (QR, KVR))):
                            nc.scalar.activation(sq[:, t, o:o + w2], proj[:, t, o:o + w2], ACT.Square,
                                                 accum_out=stat[:, 16 + 2 * i + t:17 + 2 * i + t]).then_inc(sem("ss_lat"), 1)
            await_moved(act, "w_in.4.0", "w_in.4.1")
            rg = proj[:, :, O["rg"]:O["rg"] + RW]
            nc.scalar.activation(rg, rg, ACT.Silu).then_inc(sem("gate"), 1)
            for c, w_ in ((0, 512), (1, 256)):
                ps = take(act, "A", f"uq.{c}.0")
                nc.scalar.copy(qk[:, 0, 0].rearrange("p h d -> p (h d)")[:, c * 512:c * 512 + w_], ps[:, 0:w_]).then_inc(moved["A"], 1)
            for c in range(2):
                ps = take(act, "A", f"ukv.{c}.0")
                v = ps[:, :].rearrange("p (h d) -> p h d", h=2)
                nc.scalar.copy(qk[:, 0, 1, 2 * c:2 * c + 2, 0:ND], v[:, :, 0:ND])
                nc.scalar.copy(val[:, 0, 2 * c:2 * c + 2], v[:, :, ND:]).then_inc(moved["A"], 1)
            if "B" in phases:
                for c in range(4):
                    for t in range(T):
                        copy_chunk_act(act, f"w_kv.{c}.{t}", memkv[:, t, c * 512:(c + 1) * 512])
            for j in range(2):
                for kind, dst, n in (("nopeT", nopeT, P), ("ropeT", ropeT, RD)):
                    ps = take(act, "A", f"{kind}.{j}.0")
                    nc.scalar.copy(dst[0:n, j, 0:2], ps[0:n, :].rearrange("p (a b) -> p a b", a=2)).then_inc(moved["A"], 1)
            act.wait_ge(sem("nmax"), 1)
            for h in range(H):
                for t, (lo, hi) in enumerate(((0, P), (P, 3 * P))):
                    nc.scalar.activation(sc[:, h, lo:hi], sc[:, h, lo:hi], ACT.Exp, bias=stat[:, 40 + 4 * t + h:41 + 4 * t + h],
                                         accum_out=stat[:, 48 + 4 * t + h:49 + 4 * t + h]).then_inc(sem("exp"), 1)
            await_moved(act, "score.3")
            for j in range(2):
                for hp in range(2):
                    copy_chunk_act(act, f"rqkT.{j}.{hp}", rqkT[:, j, 2 * hp:2 * hp + 2])
            for h in range(H):
                copy_chunk_act(act, f"prT.{h}", prT[:, h])
            for hp in range(2):
                copy_chunk_act(act, f"oT.{hp}", mixT[:, 2 * hp:2 * hp + 2])

        def mixA_pool(pool):
            norm_pool(pool, "a")
            if "B" in phases:
                norm_pool(pool, "m", 24)
            pool.wait_ge(sem("ss_lat"), 4)
            links["pool"](nc.gpsimd.tensor_scalar(stat[:, 20:22], stat[:, 16:18], 1.0 / QR, EPS, ALU.mult, ALU.add))
            links["pool"](nc.gpsimd.tensor_scalar(stat[:, 22:24], stat[:, 18:20], 1.0 / KVR, EPS, ALU.mult, ALU.add))
            nc.gpsimd.tensor_tensor(stat[:, 20:24], stat[:, 20:24], neghalf[:, 0:4], ALU.pow).then_inc(sem("rstd_lat"), 1)
            pool.wait_ge(sem("ss_qk"), 1)
            rsqrt(pool, stat[:, 80:96], stat[:, 64:80], 16, 1.0 / QK, EPS, sem("rstd_qk"))
            pool.wait_ge(sem("ro_var"), 1)
            rsqrt(pool, stat[:, 112:120], stat[:, 96:104], 8, 1.0, EPS, sem("ro_rstd"))

        def mixA_dve(dve):
            L = links["dve"]
            norm_dve(dve, "a", "attn_norm_g")
            rotary_dve(dve)
            for c in range(5):
                w_ = min(512, IN1 - c * 512)
                copy_chunk_dve(dve, f"w_in.{c}.1", proj[:, 1, c * 512:c * 512 + w_])
                if c == 1:
                    dve.wait_ge(sem("rstd_lat"), 1)
                    await_moved(dve, "w_in.0.1")
                    for t in range(T):
                        nc.vector.tensor_scalar(cn[:, t, 0:QR], proj[:, t, 0:QR], stat[:, 20 + t:21 + t], None,
                                                ALU.mult).then_inc(sem("cn"), 1)
                        nc.vector.tensor_scalar(cn[:, t, QR:], proj[:, t, QR:QR + KVR], stat[:, 22 + t:23 + t], None,
                                                ALU.mult).then_inc(sem("cn"), 1)
            if "B" in phases:
                norm_dve(dve, "m", "mem_norm_g", mT)
            for t in range(T):
                ps = take(dve, "D", f"cT.{t}")
                nc.vector.tensor_tensor(cT[:, :, t * P:(t + 1) * P], ps[:, 0:3 * P].rearrange("p (k n) -> p k n", k=3),
                                        bc(col("mla_q_norm_g", 3), P, 2), ALU.mult).then_inc(moved["D"], 1)
            for c, w_ in ((0, 512), (1, 256)):
                ps = take(dve, "D", f"uq.{c}.1")
                nc.vector.tensor_copy(qk[:, 1, 0].rearrange("p h d -> p (h d)")[:, c * 512:c * 512 + w_], ps[:, 0:w_]).then_inc(moved["D"], 1)
            for c in range(2):
                ps = take(dve, "D", f"ukv.{c}.1")
                v = ps[:, :].rearrange("p (h d) -> p h d", h=2)
                nc.vector.tensor_copy(qk[:, 1, 1, 2 * c:2 * c + 2, 0:ND], v[:, :, 0:ND])
                nc.vector.tensor_copy(val[:, 1, 2 * c:2 * c + 2], v[:, :, ND:]).then_inc(moved["D"], 1)
            await_moved(dve, "ukv.1.0", "ukv.1.1")
            for t in range(T):
                L(nc.vector.tensor_copy(qk[:, t, 1, :, ND:], bc(proj[:, t, O["kpe"]:O["kpe"] + RD], H, 1)))
            for t in range(T):
                q_ = qk[:, t].rearrange("p j h d -> p (j h) d")
                s_ = scr[:, 0:8 * QK].rearrange("p (a b) -> p a b", a=8)
                L(nc.vector.tensor_tensor(s_, q_, q_, ALU.mult))
                r = nc.vector.reduce_sum(stat[:, 64 + 8 * t:72 + 8 * t], s_, AX.X)
                if t == 0:
                    L(r)
                else:
                    r.then_inc(sem("ss_qk"), 1)
            dve.wait_ge(sem("rowsmall_in"), 80)
            L(nc.vector.tensor_scalar(q_g, q_g, QK ** -0.5, None, ALU.mult))
            dve.wait_ge(sem("rstd_qk"), 1)
            dve.wait_ge(sem("cossin"), 1)
            for t in range(T):
                q_ = qk[:, t].rearrange("p j h d -> p (j h) d")
                L(nc.vector.tensor_tensor(q_, q_, bc(stat[:, 80 + 8 * t:88 + 8 * t], QK, 2), ALU.mult))
                for j, g_ in enumerate((q_g, k_g)):
                    L(nc.vector.tensor_tensor(qk[:, t, j], qk[:, t, j], bc(g_, H, 1), ALU.mult))
                rope(dve, nc.vector, L, q_[:, :, ND:], 8, RD // 2, t, scr, 2, sem("qk_ready"))
                dve.wait_ge(sem("qk_ready"), t + 1)
            for j in range(2):
                for kind, dst, n in (("nopeT", nopeT, P), ("ropeT", ropeT, RD)):
                    ps = take(dve, "D", f"{kind}.{j}.1")
                    nc.vector.tensor_copy(dst[0:n, j, 2:4], ps[0:n, :].rearrange("p (a b) -> p a b", a=2)).then_inc(moved["D"], 1)
            await_moved(dve, "w_in.4.0", "w_in.4.1")
            for t in range(T):
                rope(dve, nc.vector, L, proj[:, t, O["rq"]:O["rq"] + 1024].rearrange("p (a b) -> p a b", a=8), 8, 64, t,
                     view(4096, 2048) if t == 0 else scr, 1, sem("rqk_ready"))
                dve.wait_ge(sem("rqk_ready"), t + 1)
            await_moved(dve, "ropeT.1.0", "ropeT.1.1")
            for h in range(H):
                ps = take(dve, "D", f"score.{h}")
                nc.vector.tensor_tensor(sc[:, h], ps[:, 0:3 * P], C("cmask"), ALU.add).then_inc(moved["D"], 1)
            await_moved(dve, "score.3")
            L(nc.vector.tensor_reduce(stat[:, 40:44], sc[:, :, 0:P], AX.X, ALU.max, negate=True))
            nc.vector.tensor_reduce(stat[:, 44:48], sc[:, :, P:], AX.X, ALU.max, negate=True).then_inc(sem("nmax"), 1)
            dve.wait_ge(sem("exp"), 8)
            L(nc.vector.reciprocal(stat[:, 56:64], stat[:, 48:56]))
            for t, (lo, hi) in enumerate(((0, P), (P, 3 * P))):
                nc.vector.tensor_tensor(sc[:, :, lo:hi], sc[:, :, lo:hi], bc(stat[:, 56 + 4 * t:60 + 4 * t], hi - lo, 2),
                                        ALU.mult).then_inc(sem("prob"), 1)
            for h in range(H):
                ps = take(dve, "D", f"rscore.{h}")
                nc.vector.tensor_tensor(rsc[:, h], ps[:, 0:3 * P],
                                        C("decay")[:, h * 3 * P:(h + 1) * 3 * P], ALU.mult).then_inc(moved["D"], 1)
            for t in range(T):
                ps = take(dve, "D", f"ro.{t}")
                nc.vector.tensor_copy(ro[:, t].rearrange("p h d -> p (h d)"), ps[:, :]).then_inc(moved["D"], 1)
            await_moved(dve, "ro.1")
            bn = stat[:, 128:176].rearrange("p (a b) -> p a b", a=8)
            mv = stat[:, 176:192].rearrange("p (a b) -> p a b", a=8)
            for i in range(8):
                last = nc.vector.bn_stats(bn[:, i], ro[:, i // 4, i % 4])
            L(last)
            for i in range(8):
                last = nc.vector.bn_aggr(mv[:, i], bn[:, i])
            L(last)
            nc.vector.tensor_copy(stat[:, 96:104], mv[:, :, 1]).then_inc(sem("ro_var"), 1)
            dve.wait_ge(sem("ro_rstd"), 1)
            dve.wait_ge(sem("gate"), 1)
            for t in range(T):
                for h in range(H):
                    i = 4 * t + h
                    last = nc.vector.tensor_scalar(ro[:, t, h], ro[:, t, h], mv[:, i, 0:1], stat[:, 112 + i:113 + i],
                                                   ALU.subtract, ALU.mult)
                L(last)
                nc.vector.tensor_tensor(ro[:, t].rearrange("p h d -> p (h d)"), ro[:, t].rearrange("p h d -> p (h d)"),
                                        proj[:, t, O["rg"]:O["rg"] + RW], ALU.mult).then_inc(sem("ro_gated"), 1)
            for t in range(T):
                ps = take(dve, "D", f"roT.{t}")
                nc.vector.tensor_tensor(mixT[:, 4:8, t * P:(t + 1) * P], ps[:, :].rearrange("p (k n) -> p k n", k=4),
                                        bc(col("ret_gn_g", 4), P, 2), ALU.mult).then_inc(moved["D"], 1)
            residual_dve(dve, "w_out")

        def residual_dve(dve, name):
            for c in range(2):
                for t in range(T):
                    ps = take(dve, "D", f"{name}.{c}.{t}")
                    nc.vector.tensor_tensor(X[:, t, c * 512:(c + 1) * 512], X[:, t, c * 512:(c + 1) * 512], ps[:, :],
                                            ALU.add).then_inc(moved["D"], 1)

        def residual_jobs(name, tiles=range(T)):
            return [f"{name}.{c}.{t}" for c in range(2) for t in tiles] if f"{name}.0.0" in jobs else []

        def after_residual(act, name):
            return lambda t: await_moved(act, *residual_jobs(name, (t,)))

        pe_fns.append(("A", mixA_pe)); act_fns.append(("A", mixA_act))
        pool_fns.append(("A", mixA_pool)); dve_fns.append(("A", mixA_dve))

        DH = D // H
        cq = view(6912, T, D)
        ckT = view(8960, KD, S)
        cqT = view(11008, KD, S)
        csc = view(13056, H, T, S)
        cprT = view(15104, H, T, S)
        if "B" in phases:
            linear_units("w_cq", dram2("cross_w_q"), D)
            linear_units("w_co", dram2("cross_w_o"), D)

        def heads_act(act, u, src, n, at, sq=sq):
            w_ = src.shape[2] // n
            for t in range(T):
                if t and sq.shape[1] == 1:
                    act.wait_ge(sem(f"ss_{u}"), n * t)
                for h in range(n):
                    nc.scalar.activation(sq[:, t % sq.shape[1], h * w_:(h + 1) * w_], src[:, t, h * w_:(h + 1) * w_], ACT.Square,
                                         accum_out=stat[:, at + n * t + h:at + n * t + h + 1]).then_inc(sem(f"ss_{u}"), 1)

        def cross_pe(pe):
            norm_T = lambda name, src: [transposed(pe, "D", f"{name}.{t}.{half}", src, t, half)
                                        for t in range(T) for half in range(2)]
            pe.wait_ge(sem("ck_scaled"), 1)
            norm_T("ckT", memkv)
            norm_linear(pe, "b", "w_cq", D, "AD")
            pe.wait_ge(sem("cq_scaled"), 1)
            norm_T("cqT", cq)
            await_moved(pe, "cqT.1.1")
            for h in range(H):
                ps = fill(pe, "D", f"cscore.{h}")
                for t in range(T):
                    for k in range(2):
                        mm = nc.tensor.matmul(ps[:, t * S:(t + 1) * S], cqT[:, 2 * h + k, t * P:(t + 1) * P],
                                              ckT[:, 2 * h + k, :], start=k == 0, stop=k == 1)
                mm.then_inc(full["D"], 1)
            for h in range(H):
                pe.wait_ge(sem("cprob"), h + 1)
                ps = fill(pe, "A", f"cprT.{h}")
                for m in range(T):
                    for t in range(T):
                        mm = nc.tensor.transpose(ps[:, m * S + t * P:m * S + (t + 1) * P],
                                                 csc[:, h, t, m * P:(m + 1) * P], ident)
                mm.then_inc(full["A"], 1)
            for h in range(H):
                await_moved(pe, f"cprT.{h}")
                ps = fill(pe, "A", f"coT.{h}")
                for d in range(2):
                    for m in range(T):
                        o = D + h * DH + d * P
                        mm = nc.tensor.matmul(ps[:, d * S:(d + 1) * S], memkv[:, m, o:o + P], cprT[:, h, m],
                                              start=m == 0, stop=m == 1)
                mm.then_inc(full["A"], 1)
            await_moved(pe, "coT.3")
            linear(pe, "w_co", mixT, D, "DD")

        def transposed(pe, ring, name, src, t, half):
            ps = fill(pe, ring, name)
            for k in range(4):
                o = (half * 4 + k) * P
                mm = nc.tensor.transpose(ps[:, k * P:(k + 1) * P], src[:, t, o:o + P], ident)
            mm.then_inc(full[ring], 1)

        def cross_act(act):
            await_moved(act, "w_kv.3.1")
            heads_act(act, "ck", memkv[:, :, 0:D], H, 192, view(16000, 1, D))
            norm_act(act, "b", X, ready=after_residual(act, "w_out"))
            for c in range(2):
                copy_chunk_act(act, f"w_cq.{c}.0", cq[:, 0, c * 512:(c + 1) * 512])
            await_moved(act, "w_cq.1.0", "w_cq.1.1")
            heads_act(act, "cq", cq, H, 208)
            for h in range(H):
                act.wait_ge(sem("cnmax"), h + 1)
                for t in range(T):
                    nc.scalar.activation(csc[:, h, t], csc[:, h, t], ACT.Exp,
                                         bias=stat[:, 224 + 2 * h + t:225 + 2 * h + t],
                                         accum_out=stat[:, 232 + 2 * h + t:233 + 2 * h + t]).then_inc(sem("cexp"), 1)
            for h in range(H):
                copy_chunk_act(act, f"cprT.{h}", cprT[:, h])
            for h in range(H):
                copy_chunk_act(act, f"coT.{h}", mixT[:, 2 * h:2 * h + 2])

        def cross_pool(pool):
            pool.wait_ge(sem("ss_ck"), 8)
            rsqrt(pool, stat[:, 200:208], stat[:, 192:200], 8, 1.0 / DH, EPS, sem("rstd_ck"))
            norm_pool(pool, "b")
            pool.wait_ge(sem("ss_cq"), 8)
            rsqrt(pool, stat[:, 216:224], stat[:, 208:216], 8, 1.0, 256 * EPS, sem("rstd_cq"))

        def scale_heads(dve, x, n, at, done):
            for t in range(T):
                v = x[:, t].rearrange("p (h d) -> p h d", h=n)
                last = nc.vector.tensor_tensor(v, v, bc(stat[:, at + n * t:at + n * (t + 1)], v.shape[2], 2), ALU.mult)
            last.then_inc(done, 1)

        def headsT_dve(dve, name, dst, gain):
            for t in range(T):
                for half in range(2):
                    ps = take(dve, "D", f"{name}.{t}.{half}")
                    for j in range(2):
                        i = nc.vector.tensor_tensor(dst[:, half * 4 + j:half * 4 + 4:2, t * P:(t + 1) * P],
                                                    ps[:, :].rearrange("p (k n) -> p k n", k=4)[:, j::2],
                                                    bc(bc(col(gain, 1, j)[:, 0], 2, 1), P, 2), ALU.mult)
                    i.then_inc(moved["D"], 1)

        def cross_dve(dve):
            L = links["dve"]
            dve.wait_ge(sem("rstd_ck"), 1)
            scale_heads(dve, memkv[:, :, 0:D], H, 200, sem("ck_scaled"))
            headsT_dve(dve, "ckT", ckT, "cross_k_qk_g")
            norm_dve(dve, "b", "cross_norm_g")
            for c in range(2):
                copy_chunk_dve(dve, f"w_cq.{c}.1", cq[:, 1, c * 512:(c + 1) * 512])
            dve.wait_ge(sem("rstd_cq"), 1)
            scale_heads(dve, cq, H, 216, sem("cq_scaled"))
            headsT_dve(dve, "cqT", cqT, "cross_q_qk_g")
            for h in range(H):
                copy_chunk_dve(dve, f"cscore.{h}", csc[:, h])
                await_moved(dve, f"cscore.{h}")
                nc.vector.tensor_reduce(stat[:, 224 + 2 * h:226 + 2 * h], csc[:, h], AX.X, ALU.max,
                                        negate=True).then_inc(sem("cnmax"), 1)
            for h in range(H):
                dve.wait_ge(sem("cexp"), 2 * h + 2)
                r = stat[:, 240 + 2 * h:242 + 2 * h]
                L(nc.vector.reciprocal(r, stat[:, 232 + 2 * h:234 + 2 * h]))
                nc.vector.tensor_tensor(csc[:, h], csc[:, h], bc(r, S, 2), ALU.mult).then_inc(sem("cprob"), 1)
            early_cuts["C"](dve)
            residual_dve(dve, "w_co")

        pe_fns.append(("B", cross_pe)); act_fns.append(("B", cross_act))
        pool_fns.append(("B", cross_pool)); dve_fns.append(("B", cross_dve))

        sil = view(8576, 2, FF)
        actv = view(9088, 2, FF)
        actT = view(9600, 2, 2, P)
        GU_SLOTS = ((0, 1), (2, 3), (8, 9), (10, 11))
        D_SLOTS = (4, 5, 6, 7)

        def ffn_units(name, chunks, gate, up, down, gu_slots=GU_SLOTS):
            for c in chunks:
                views[f"{name}.gu.{c}"] = gu_slots[c % 4], P, KD, 2 * FF
                v = unit_view(f"{name}.gu.{c}")
                place(f"{name}.gu.{c}", gu_slots[c % 4],
                      [(gate(c).rearrange("(k p) n -> p k n", p=P), v[:, :, 0:FF]),
                       (up(c).rearrange("(k p) n -> p k n", p=P), v[:, :, FF:])])
                views[f"{name}.d.{c}"] = (D_SLOTS[c % 4],), P, 2, D
                place(f"{name}.d.{c}", (D_SLOTS[c % 4],), [(down(c).rearrange("(k p) n -> p k n", p=P), None)])

        def gu_pe(pe, u, i, gu, hTile, middle, o=""):
            ps = fill(pe, "GU" + o, f"{u}.gu.{i}")
            for k in range(KD):
                mm = nc.tensor.matmul(ps[:, :], hTile(k), gu[:, k, :], start=k == 0, stop=k == KD - 1)
                if k == KD // 2 - 1 and middle is not None:
                    middle()
            mm.then_inc(full["GU" + o], 1)

        def tr_pe(pe, u, i, o=""):
            await_moved(pe, f"{u}.gu.{i}")
            ps = fill(pe, "TT" + o, f"{u}.T.{i}")
            for k in range(2):
                mm = nc.tensor.transpose(ps[:, k * P:(k + 1) * P], actv[:, i % 2, k * P:(k + 1) * P], ident)
            mm.then_inc(full["TT" + o], 1)

        def down_pe(pe, u, i, wd, banks, first, last, done):
            await_moved(pe, f"{u}.T.{i}")
            for c in range(2):
                for k in range(2):
                    mm = nc.tensor.matmul(banks[c][:, :], actT[:, i % 2, k], wd[:, k, c * 512:(c + 1) * 512],
                                          start=first and k == 0, stop=last and k == 1)
            mm.then_inc(done, 1)

        def step_act(act, u, i, o="", sil=sil):
            ps = peek(act, f"{u}.gu.{i}")
            if i >= 2:
                await_moved(act, f"{u}.gu.{i - 2}")
            nc.scalar.activation(sil[:, i % 2], ps[:, 0:FF], ACT.Silu).then_inc(sem(f"silu_{u}"), 1)

        def stepT_act(act, u, i, down_done, o=""):
            ps = take(act, "TT" + o, f"{u}.T.{i}")
            if i >= 2:
                act.wait_ge(down_done, i - 1)
            nc.scalar.copy(actT[:, i % 2].rearrange("p a b -> p (a b)"), ps[:, 0:FF]).then_inc(moved["TT" + o], 1)

        def step_dve(dve, u, i, gate=None, o=""):
            ps = take(dve, "GU" + o, f"{u}.gu.{i}")
            dve.wait_ge(sem(f"silu_{u}"), i + 1)
            if i >= 2:
                peek(dve, f"{u}.T.{i - 2}")
            if gate is None:
                nc.vector.tensor_tensor(actv[:, i % 2], ps[:, FF:], sil[:, i % 2], ALU.mult).then_inc(moved["GU" + o], 1)
            else:
                nc.vector.scalar_tensor_tensor(actv[:, i % 2], ps[:, FF:], gate, sil[:, i % 2],
                                               ALU.mult, ALU.mult).then_inc(moved["GU" + o], 1)

        wr = work[:, 25776:25776 + KD * 36].rearrange("p (k n) -> p k n", k=KD)
        hg = view(2048, 2, KD, P)
        hgh, hgl = view_r(0, 2, KD, P), view_r(2048, 2, KD, P)
        Sel = view(6144, T, G, P)
        SelT = view(7168, G, S)
        ysb = view(10112, 2, D)
        rt = work[:, 26064:26064 + 432]
        Selo = view(8192 + 0, T, P)
        SelTo = view(20480, S)
        gs = work[:, 8448:8448 + 5 * EPG].rearrange("p (g e) -> p g e", g=5)
        flags = work[:, 8500:8502].bitcast(I32)

        def rtv(at, *shape):
            n = int(np.prod(shape))
            v = rt[:, at:at + n]
            if len(shape) == 2:
                v = v.rearrange("p (a b) -> p a b", a=shape[0])
            if len(shape) == 3:
                v = v.rearrange("p (a b c) -> p a b c", a=shape[0], b=shape[1])
            return v

        logit = rtv(0, T, 36)
        oh = rtv(80, T, G)
        el = rtv(100, T, EPG)
        gate8 = rtv(120, T, EPG)
        rank = rtv(140, T, 2)
        tmp = rtv(150, T, G, EPG)
        tmp8 = rtv(220, T, EPG)
        oh1 = rtv(240, T, EPG)
        oh2 = rtv(260, T, EPG)
        m1 = rtv(280, T, 1)
        m2 = rtv(284, T, 1)
        gw = rtv(288, T, 1)
        gb = rtv(292, T, G)
        ge = rtv(300, T, G)
        ee = rtv(310, T, EPG)
        bias8 = rtv(330, T, EPG)
        cnt = rtv(350, 3, G)
        ovf = rtv(364, G)
        nm = rtv(370, T, 2)
        gsum = rtv(376, T, 2)
        den = rtv(382, T, 1)
        oho = rtv(386, T, 1)
        if "C" in phases:
            eg, eu, ed = A["expert_w_gate"][0], A["expert_w_up"][0], A["expert_w_down"][0]
            fence["moe"] = ("coT.3",)
            ffn_units("moe", range(G * EPG), lambda c: eg[c], lambda c: eu[c], lambda c: ed[c],
                      ((8, 9), (10, 11), (0, 1), (2, 3)))

        MP, MH = 4, 5
        GATHER_STEPS = (3, 4)
        high_piece = lambda j: view_r(20480 + (j % MH) * 2 * 2 * FF, 2, 2 * FF)

        def cut_moe(dve, j):
            e, q = j // MP, j % MP
            if e >= G * EPG:
                return
            if q == 0:
                _, _, slots, value = units[unit_at[f"moe.gu.{e}"]]
                dve.wait_ge(arrived[slots[0]], value)
            if j >= MH:
                e_, q_ = (j - MH) // MP, (j - MH) % MP
                if q_ < MP - 1:
                    dve.wait_ge(sem("pieces_used"), (MP - 1) * e_ + q_ + 1)
                else:
                    peek(dve, f"moe.gu.{e_}")
            k2 = slice(2 * q, 2 * q + 2)
            split(high_piece(j), unit_view(f"moe.gu.{e}", True)[:, k2], unit_view(f"moe.gu.{e}")[:, k2], sem("cut_moe"))

        def gu_moe_pe(pe, e, half, middle):
            released[unit_at[f"moe.gu.{e}"]] = f"moe.gu.{e}"
            low = unit_view(f"moe.gu.{e}", True)
            ps = fill(pe, "GU", f"moe.gu.{e}")
            for k in range(KD):
                q = k // 2
                if k % 2 == 0:
                    pe.wait_ge(sem("cut_moe"), MP * e + q + 1)
                mm = three_passes(ps[:, :], (hgh[:, half, k], hgl[:, half, k]), (high_piece(MP * e + q)[:, k % 2], low[:, k]),
                                  k == 0, k == KD - 1)
                if k % 2 == 1 and q < MP - 1:
                    mm.then_inc(sem("pieces_used"), 1)
                if k == KD // 2 - 1 and middle is not None:
                    middle()
            mm.then_inc(full["GU"], 1)

        def moe_pe(pe):
            pe.wait_ge(sem("wr_in"), 32)
            for t in range(T):
                norm_pe(pe, "c", tiles=(t,))
                await_moved(pe, *hT_jobs("c", (t,)))
                ps = fill(pe, "D", f"logit.{t}")
                for k in range(KD):
                    mm = nc.tensor.matmul(ps[:, 0:36], hT[:, k, t * P:(t + 1) * P], wr[:, k, :], start=k == 0, stop=k == KD - 1)
                mm.then_inc(full["D"], 1)
            pe.wait_ge(sem("group_picked"), 1)
            pe.wait_ge(sem("const2_in"), 16)
            ps = fill(pe, "D", "rank")
            nc.tensor.matmul(ps[:, 0:G], C("strictP"), oh[:, 0], start=True, stop=True)
            nc.tensor.matmul(ps[:, G:2 * G], C("ones"), oh[:, 0], start=True, stop=False)
            nc.tensor.matmul(ps[:, G:2 * G], C("strictP"), oh[:, 1], start=False, stop=True)
            nc.tensor.matmul(ps[:, 2 * G:3 * G], C("ones"), oh[:, 0], start=True, stop=False)
            nc.tensor.matmul(ps[:, 2 * G:3 * G], C("ones"), oh[:, 1], start=False, stop=True).then_inc(full["D"], 1)
            drained(pe, "D", "A")

            def gather(g, sel, part, o=""):
                if part == 0:
                    ps = fill(pe, "Z" + o, f"selT.{g}")
                    for t in range(T):
                        mm = nc.tensor.transpose(ps[:, t * P:(t + 1) * P], sel(t), ident)
                    mm.then_inc(full["Z" + o], 1)
                for half in (part,):
                    ps = fill(pe, "Z" + o, f"hg.{g}.{half}")
                    for k in range(4):
                        for t in range(T):
                            kk = half * 4 + k
                            mm = nc.tensor.matmul(ps[:, k * P:(k + 1) * P], xn[:, t, kk * P:(kk + 1) * P], sel(t),
                                                  start=t == 0, stop=t == 1)
                    mm.then_inc(full["Z" + o], 1)
                if part == 0:
                    return
                ps = fill(pe, "Z" + o, f"gs.{g}")
                pe.wait_ge(sem("gates"), 1)
                for t in range(T):
                    mm = nc.tensor.matmul(ps[:, 0:EPG], sel(t), gate8[:, t], start=t == 0, stop=t == 1)
                mm.then_inc(full["Z" + o], 1)

            def scatter(g, selT, o=""):
                await_moved(pe, f"y.{g}")
                for c in range(2):
                    for t in range(T):
                        ps = fill(pe, "Z" + o, f"x.{g}.{c}.{t}")
                        nc.tensor.matmul(ps[:, :], selT[:, t * P:(t + 1) * P], ysb[:, g % 2, c * 512:(c + 1) * 512],
                                         start=True, stop=True).then_inc(full["Z" + o], 1)

            pe.wait_ge(sem("selected"), T * G)
            for part in range(2):
                gather(0, lambda t: Sel[:, t, 0], part)
            n = G * EPG
            down = sem("down_moe")
            banks = None
            for i in range(n + 1):
                if i < n:
                    g = i // EPG
                    if i % EPG == 0:
                        await_moved(pe, f"gs.{g}")
                        pe.wait_ge(sem("tile_cut"), g + 1)
                    gu_moe_pe(pe, i, g % 2, (lambda: tr_pe(pe, "moe", i - 1)) if i else None)
                    if i % EPG in GATHER_STEPS and g < G - 1:
                        gather(g + 1, lambda t: Sel[:, t, g + 1], GATHER_STEPS.index(i % EPG))
                else:
                    tr_pe(pe, "moe", i - 1)
                if i:
                    j = i - 1
                    if j % EPG == 0:
                        banks = fill(pe, "Y", f"y.{j // EPG}")
                    wd = weights(pe, f"moe.d.{j}")
                    released[unit_at[f"moe.d.{j}"]] = (down, j + 1)
                    if j % EPG == EPG - 1:
                        down_pe(pe, "moe", j, wd, banks, False, True, down)
                    else:
                        down_pe(pe, "moe", j, wd, banks, j % EPG == 0, False, down)
                if i % EPG == 1 and i > 1:
                    scatter(i // EPG - 1, SelT[:, i // EPG - 1])
            scatter(G - 1, SelT[:, G - 1])
            drained(pe, "GU", "TT", "Z")
            pe.wait_ge(moved["Y"], filled["Y"])
            if "O" in phases:
                overflow_pe(pe, gather, scatter)

        def overflow(eng, body):
            eng.wait_ge(sem("flags"), 1)
            some = eng.value_load(flags[0:1, 1:2], min_val=0, max_val=1)
            with eng.If(some > 0):
                body()

        def overflow_pe(pe, gather, scatter):
            def body():
                for part in range(2):
                    gather(G, lambda t: Selo[:, t], part, "o")
                await_moved(pe, f"gs.{G}")
                banks = fill(pe, "Yo", f"y.{G}")
                for e in range(EPG):
                    s = e % 4
                    pe.wait_ge(sem("arrived_o"), 48 * (e + 1))
                    gu = slot_view(GU_SLOTS[s], P, KD, 2 * FF)
                    gu_pe(pe, "ovf", e, gu, lambda k: hg[:, 0, k], None, "o")
                    tr_pe(pe, "ovf", e, "o")
                    down_pe(pe, "ovf", e, slot_view((D_SLOTS[s],), P, 2, D), banks, e == 0, e == EPG - 1, sem("down_ovf"))
                scatter(G, SelTo, "o")
                drained(pe, "GUo", "TTo", "Zo")
                pe.wait_ge(moved["Yo"], 1)
            overflow(pe, body)

        def moe_y_act(act, g, o=""):
            banks = take_y(act, g, o)
            for c in range(2):
                mm = nc.scalar.copy(ysb[:, g % 2, c * 512:(c + 1) * 512], banks[c][:, :])
            mm.then_inc(moved["Y" + o], 1)

        def take_y(act, g, o):
            ring = "Y" + o
            n = taken[ring]
            assert jobs[f"y.{g}"] == (ring, n)
            taken[ring] += 1
            if o:
                act.wait_ge(sem("down_ovf"), EPG)
            else:
                act.wait_ge(sem("down_moe"), EPG * (g + 1))
            if g >= 2 and g < G:
                await_moved(act, f"x.{g - 2}.1.1")
            return RINGS[ring][0]

        def moe_act(act):
            norm_act(act, "c", X, ready=after_residual(act, "w_co"))
            act.wait_ge(sem("negmax_g"), 1)
            for t in range(T):
                nc.scalar.activation(ge[:, t], logit[:, t, 0:G], ACT.Exp, bias=nm[:, t, 0:1], accum_out=gsum[:, t, 0:1]).then_inc(sem("gexp"), 1)
            act.wait_ge(sem("negmax_e"), 1)
            for t in range(T):
                nc.scalar.activation(ee[:, t], el[:, t], ACT.Exp, bias=nm[:, t, 1:2], accum_out=gsum[:, t, 1:2]).then_inc(sem("eexp"), 1)
            for i in range(G * EPG):
                if i:
                    stepT_act(act, "moe", i - 1, sem("down_moe"))
                step_act(act, "moe", i)
                if i % EPG == 0 and i:
                    moe_y_act(act, i // EPG - 1)
            stepT_act(act, "moe", G * EPG - 1, sem("down_moe"))
            moe_y_act(act, G - 1)
            if "O" in phases:
                def body():
                    for e in range(EPG):
                        step_act(act, "ovf", e, "o")
                        stepT_act(act, "ovf", e, sem("down_ovf"), "o")
                    moe_y_act(act, G, "o")
                overflow(act, body)

        def moe_pool(pool):
            if "B" in phases:
                peek(pool, "coT.3")
            pool.dma_start(wr[:, :, 0:G], A["router_w_group"][0].rearrange("(k p) n -> p k n", p=P)).then_inc(sem("wr_in"), 16)
            pool.dma_start(wr[:, :, G:], A["router_w_expert"][0].rearrange("(k p) n -> p k n", p=P)).then_inc(sem("wr_in"), 16)
            norm_pool(pool, "c")

        def first_cuts_moe(dve):
            if "C" in phases:
                if "B" in phases:
                    peek(dve, "coT.3")
                for j in range(MH):
                    cut_moe(dve, j)
        early_cuts["C"] = first_cuts_moe

        def moe_dve(dve):
            L = links["dve"]
            if "B" not in phases:
                first_cuts_moe(dve)
            V = nc.vector
            for t in range(T):
                norm_dve(dve, "c", "moe_norm_g", tiles=(t,))
                ps = take(dve, "D", f"logit.{t}")
                V.tensor_copy(logit[:, t], ps[:, 0:36]).then_inc(moved["D"], 1)
            await_moved(dve, "logit.1")
            tie = C("gidx")

            def pick(dst, v, m, n):
                L(V.tensor_reduce(m[:, :, 0], v, AX.X, ALU.max))
                L(V.tensor_tensor(tmp8[:, :, 0:n], v, bc(m[:, :, 0], n, 2), ALU.is_equal))
                L(V.tensor_tensor(dst, tmp8[:, :, 0:n], bc(tieinv[:, 0:n], T, 1), ALU.mult))
                L(V.tensor_reduce(m[:, :, 0], dst, AX.X, ALU.max))
                L(V.tensor_tensor(dst, dst, bc(m[:, :, 0], n, 2), ALU.is_equal))

            tieinv = rtv(400, 8)
            dve.wait_ge(sem("const2_in"), 16)
            L(V.tensor_scalar(tieinv, tie, -1.0, 8.0, ALU.mult, ALU.add))
            L(V.tensor_reduce(nm[:, :, 0], logit[:, :, 0:G], AX.X, ALU.max))
            V.tensor_scalar(nm[:, :, 0], nm[:, :, 0], -1.0, None, ALU.mult).then_inc(sem("negmax_g"), 1)
            L(V.tensor_tensor(gb, logit[:, :, 0:G], bc(bias_g, T, 1), ALU.add))
            pick(oh, gb, m1, G)
            V.tensor_copy(rtv(410, T, G), oh).then_inc(sem("group_picked"), 1)
            for t in range(T):
                L(V.tensor_tensor(tmp[:, t], logit[:, t, G:].rearrange("p (g e) -> p g e", g=G), bc(oh[:, t], EPG, 2), ALU.mult))
                L(V.reduce_sum(el[:, t], tmp[:, t].rearrange("p g e -> p e g"), AX.X))
                L(V.tensor_tensor(tmp[:, t], bias_e.rearrange("p (g e) -> p g e", g=G), bc(oh[:, t], EPG, 2), ALU.mult))
                L(V.reduce_sum(bias8[:, t], tmp[:, t].rearrange("p g e -> p e g"), AX.X))
            L(V.tensor_reduce(nm[:, :, 1], el, AX.X, ALU.max))
            V.tensor_scalar(nm[:, :, 1], nm[:, :, 1], -1.0, None, ALU.mult).then_inc(sem("negmax_e"), 1)
            L(V.tensor_tensor(bias8, bias8, el, ALU.add))
            pick(oh1, bias8, m1, EPG)
            L(V.scalar_tensor_tensor(bias8, oh1, -3e38, bias8, ALU.mult, ALU.add))
            pick(oh2, bias8, m1, EPG)
            L(V.tensor_tensor(oh1, oh1, oh2, ALU.add))
            ps = take(dve, "D", "rank")
            V.tensor_copy(cnt, ps[:, 0:3 * G].rearrange("p (a b) -> p a b", a=3)).then_inc(moved["D"], 1)
            await_moved(dve, "rank")
            L(V.tensor_tensor(tmp8[:, :, 0:G], cnt[:, 0:T], oh, ALU.mult))
            L(V.reduce_sum(rank[:, :, 0], tmp8[:, :, 0:G], AX.X))
            for g in range(G):
                for t in range(T):
                    V.tensor_scalar(Sel[:, t, g], C("iota"), rank[:, t, 0:1], oh[:, t, g:g + 1], ALU.is_equal, ALU.mult) \
                        .then_inc(sem("selected"), 1)
            dve.wait_ge(sem("gexp"), 2)
            dve.wait_ge(sem("eexp"), 2)
            L(V.reciprocal(gsum, gsum))
            L(V.tensor_tensor(ge, ge, oh, ALU.mult))
            L(V.reduce_sum(gw[:, :, 0], ge, AX.X))
            L(V.tensor_tensor(gw[:, :, 0], gw[:, :, 0], gsum[:, :, 0], ALU.mult))
            L(V.tensor_tensor(ee, ee, bc(gsum[:, :, 1], EPG, 2), ALU.mult))
            L(V.tensor_tensor(ee, ee, oh1, ALU.mult))
            L(V.reduce_sum(den[:, :, 0], ee, AX.X))
            L(V.reciprocal(den, den))
            L(V.tensor_tensor(den, den, gw, ALU.mult))
            V.tensor_tensor(gate8, ee, bc(den[:, :, 0], EPG, 2), ALU.mult).then_inc(sem("gates"), 1)
            L(V.tensor_scalar(ovf, cnt[:, 2], float(P), None, ALU.is_gt))
            L(V.tensor_tensor(tmp8[:, :, 0:G], oh, bc(ovf, T, 1), ALU.mult))
            L(V.reduce_sum(oho[:, :, 0], tmp8[:, :, 0:G], AX.X))
            L(V.tensor_scalar(rank[:, :, 1], rank[:, :, 0], -float(P), None, ALU.add))
            for t in range(T):
                L(V.tensor_scalar(Selo[:, t], C("iota"), rank[:, t, 1:2], oho[:, t], ALU.is_equal, ALU.mult))
            L(V.tensor_tensor(tmp8[:, 0, 0:G], ovf, tie[:, 0:G], ALU.mult))
            L(V.reduce_sum(nm[:, 0, 0:1], tmp8[:, 0, 0:G], AX.X))
            L(V.reduce_sum(nm[:, 0, 1:2], ovf, AX.X))
            V.tensor_copy(flags, nm[:, 0, :]).then_inc(sem("flags"), 1)

            def gather_dve(g, selT, part, o=""):
                if part == 0:
                    ps = take(dve, "Z" + o, f"selT.{g}")
                    V.tensor_copy(selT, ps[:, 0:S]).then_inc(moved["Z" + o], 1)
                for half in (part,):
                    ps = take(dve, "Z" + o, f"hg.{g}.{half}")
                    V.tensor_tensor(hg[:, g % 2, half * 4:half * 4 + 4], ps[:, :].rearrange("p (k n) -> p k n", k=4),
                                    bc(col("moe_norm_g", 4, half * 4), P, 2), ALU.mult).then_inc(moved["Z" + o], 1)
                if part == 0:
                    return
                if not o:
                    await_moved(dve, f"hg.{g}.1")
                    split(hgh[:, g % 2], hgl[:, g % 2], hg[:, g % 2], sem("tile_cut"))
                ps = take(dve, "Z" + o, f"gs.{g}")
                V.tensor_copy(gs[:, g], ps[:, 0:EPG]).then_inc(moved["Z" + o], 1)

            def scatter_dve(g, o=""):
                for c in range(2):
                    for t in range(T):
                        ps = take(dve, "Z" + o, f"x.{g}.{c}.{t}")
                        V.tensor_tensor(X[:, t, c * 512:(c + 1) * 512], X[:, t, c * 512:(c + 1) * 512], ps[:, :],
                                        ALU.add).then_inc(moved["Z" + o], 1)

            for part in range(2):
                gather_dve(0, SelT[:, 0], part)
            for i in range(G * EPG):
                g = i // EPG
                for q in range(1, MP):
                    cut_moe(dve, MP * (i + 1) + q)
                if i % EPG == 0:
                    await_moved(dve, f"gs.{g}")
                step_dve(dve, "moe", i, gs[:, g, i % EPG:i % EPG + 1])
                if i % EPG in GATHER_STEPS and g < G - 1:
                    gather_dve(g + 1, SelT[:, g + 1], GATHER_STEPS.index(i % EPG))
                cut_moe(dve, MP * (i + 2))
                if i % EPG == 1 and i > 1:
                    scatter_dve(g - 1)
            scatter_dve(G - 1)
            if "O" in phases:
                def body():
                    await_moved(dve, f"x.{G - 1}.1.1")
                    for part in range(2):
                        gather_dve(G, SelTo, part, "o")
                    await_moved(dve, f"gs.{G}")
                    for e in range(EPG):
                        step_dve(dve, "ovf", e, gs[:, G, e:e + 1], "o")
                    scatter_dve(G, "o")
                    await_moved(dve, f"x.{G}.1.1")
                overflow(dve, body)
                await_moved(dve, f"x.{G - 1}.1.1")
                V.tensor_copy(rtv(420, 1), rtv(400, 1)).then_inc(sem("overflow_added"), 1)

        def overflow_sp(sp):
            def body():
                g = sp.value_load(flags[0:1, 0:1], min_val=0, max_val=G - 1)
                sp.wait_ge(sem("down_moe"), G * EPG)
                for e in range(EPG):
                    if e >= 4:
                        sp.wait_ge(sem("down_ovf"), e - 3)
                    v = slot_view(GU_SLOTS[e % 4], P, KD, 2 * FF)
                    x_ = bass.ds(g * EPG + e, 1)
                    for src, dst in ((eg, v[:, :, 0:FF]), (eu, v[:, :, FF:]), (ed, slot_view((D_SLOTS[e % 4],), P, 2, D))):
                        sp.dma_start(dst, src[x_, :, :].rearrange("o (k p) n -> p (o k) n", p=P)).then_inc(sem("arrived_o"), 16)
                    sp.wait_ge(sem("arrived_o"), 48 * (e + 1))
                sp.wait_ge(sem("down_ovf"), EPG)
            overflow(sp, body)

        pe_fns.append(("C", moe_pe)); act_fns.append(("C", moe_act))
        pool_fns.append(("C", moe_pool)); dve_fns.append(("C", moe_dve))

        hTh, hTl = view_r(6144, KD, S), view_r(0, KD, S)
        s_sil = view(24576, 2, FF)
        s_actv = view(25088, 2, FF)
        s_actTh = view_r(25600, 2, 2, P)
        s_actTl = view_r(8192, 2, 2, P)
        HIGH_AT = (20480, 22528, 10240, 2048, 4096)
        PIECES = 2

        def split(high, low, value, done):
            links["dve"](nc.vector.tensor_copy(high, value))
            return nc.vector.tensor_tensor(low, value, high.bitcast(F32), ALU.subtract).then_inc(done, 1)

        def three_passes(out, lhsT, rhs, first, last):
            nc.tensor.matmul(out, lhsT[0], rhs[0], start=first, stop=False)
            nc.tensor.matmul(out, lhsT[0], rhs[1], start=False, stop=False)
            return nc.tensor.matmul(out, lhsT[1], rhs[0], start=False, stop=last)

        def add_swiglu(ph, u, layer, after, fenced, gu_slots=GU_SLOTS):
            n = DFF // FF
            wg, wu, wd_ = A["ffn_w_gate_2"][layer], A["ffn_w_up_2"][layer], A["ffn_w_down_2"][layer]
            if ph in phases:
                fence[u] = fenced
                ffn_units(u, range(n), lambda c: wg[:, c * FF:(c + 1) * FF], lambda c: wu[:, c * FF:(c + 1) * FF],
                          lambda c: wd_[c * FF:(c + 1) * FF, :], gu_slots)

            def high_slot(j):
                at = HIGH_AT[j % len(HIGH_AT)]
                return view_r(at, KD // 2, 2 * FF) if j % 3 < 2 else view_r(at, 2, D)

            def low_slot(j, as_rounded=True):
                c, kind = j // 3, j % 3
                if kind == 2:
                    return unit_view(f"{u}.d.{c}", as_rounded)
                return unit_view(f"{u}.gu.{c}", as_rounded)[:, kind * KD // 2:(kind + 1) * KD // 2]

            def cut_ready(j, piece=PIECES - 1):
                return PIECES * j + piece + 1

            def cut(dve, piece_no):
                j, piece = piece_no // PIECES, piece_no % PIECES
                if j >= 3 * n:
                    return
                c, kind = j // 3, j % 3
                if piece == 0:
                    _, _, slots, value = units[unit_at[f"{u}.{'d' if kind == 2 else 'gu'}.{c}"]]
                    dve.wait_ge(arrived[slots[0]], value)
                    before = j - len(HIGH_AT)
                    if before >= 0:
                        cb = before // 3
                        if before % 3 == 2:
                            dve.wait_ge(sem(f"down_{u}"), T * cb + T)
                        else:
                            peek(dve, f"{u}.gu.{T * cb + T - 1}")
                h = high_slot(j)
                k = h.shape[1] // PIECES
                s_ = slice(piece * k, (piece + 1) * k)
                split(h[:, s_], low_slot(j)[:, s_], low_slot(j, False)[:, s_], sem(f"cut_{u}"))

            def gu3_pe(pe, i, middle):
                c, t = i // T, i % T
                released[unit_at[f"{u}.gu.{c}"]] = f"{u}.gu.{T * c + T - 1}"
                ps = fill(pe, "GU", f"{u}.gu.{i}")
                tok = slice(t * P, (t + 1) * P)
                for k in range(KD):
                    j, kk = 3 * c + k // 4, k % 4
                    if kk % 2 == 0 and t == 0:
                        pe.wait_ge(sem(f"cut_{u}"), cut_ready(j, kk // 2))
                    mm = three_passes(ps[:, :], (hTh[:, k, tok], hTl[:, k, tok]), (high_slot(j)[:, kk], low_slot(j)[:, kk]),
                                      k == 0, k == KD - 1)
                    if k == KD // 2 - 1 and middle is not None:
                        middle()
                mm.then_inc(full["GU"], 1)

            def tr3_pe(pe, i):
                await_moved(pe, f"{u}.gu.{i}")
                ps = fill(pe, "TT", f"{u}.T.{i}")
                for k in range(2):
                    mm = nc.tensor.transpose(ps[:, k * P:(k + 1) * P], s_actv[:, i % 2, k * P:(k + 1) * P], ident)
                mm.then_inc(full["TT"], 1)

            def down3_pe(pe, i, banks):
                c, t = i // T, i % T
                released[unit_at[f"{u}.d.{c}"]] = (sem(f"down_{u}"), T * c + T)
                j = 3 * c + 2
                await_moved(pe, f"{u}.T.{i}")
                pe.wait_ge(sem(f"cut_{u}"), cut_ready(j))
                for half in range(2):
                    o = slice(half * 512, (half + 1) * 512)
                    for k in range(2):
                        mm = three_passes(banks[2 * t + half][:, :], (s_actTh[:, i % 2, k], s_actTl[:, i % 2, k]),
                                          (high_slot(j)[:, k, o], low_slot(j)[:, k, o]),
                                          c == 0 and k == 0, c == n - 1 and k == 1)
                mm.then_inc(sem(f"down_{u}"), 1)

            def f_pe(pe):
                norm_pe(pe, u, tiles=(0,))
                drained(pe, "D", "A")
                banks = fill(pe, "Y4", f"y_{u}")
                for i in range(T * n + 1):
                    if i == 1:
                        norm_pe(pe, u, tiles=(1,), ring="N")
                    if i < T:
                        pe.wait_ge(sem(f"input_cut_{u}"), i + 1)
                    if i < T * n:
                        gu3_pe(pe, i, (lambda: tr3_pe(pe, i - 1)) if i else None)
                    else:
                        tr3_pe(pe, i - 1)
                    if i:
                        down3_pe(pe, i - 1, banks)
                drained(pe, "GU", "TT")
                pe.wait_ge(moved["Y4"], filled["Y4"])

            def f_act(act):
                norm_act(act, u, X, ready=after(act))
                for i in range(T * n):
                    step_act(act, u, i, sil=s_sil)

            def f_dve(dve):
                if {"E": "D", "G": "F"}[ph] not in phases:
                    first_cuts(dve)
                piece = 2 * PIECES
                for t in range(T):
                    for half in range(2):
                        ps = take(dve, "DN"[t], f"hT_{u}.{t}.{half}")
                        h4, tok = slice(half * 4, half * 4 + 4), slice(t * P, (t + 1) * P)
                        nc.vector.tensor_tensor(hT[:, h4, tok], ps[:, :].rearrange("p (k n) -> p k n", k=4),
                                                bc(col("ffn_norm_2", 4, KD * layer + half * 4), P, 2),
                                                ALU.mult).then_inc(moved["DN"[t]], 1)
                    await_moved(dve, f"hT_{u}.{t}.1")
                    split(hTh[:, :, tok], hTl[:, :, tok], hT[:, :, tok], sem(f"input_cut_{u}"))
                    if t == 0:
                        for _ in range(PIECES):
                            cut(dve, piece)
                            piece += 1
                for i in range(T * n):
                    ps = take(dve, "GU", f"{u}.gu.{i}")
                    dve.wait_ge(sem(f"silu_{u}"), i + 1)
                    if i >= 2:
                        peek(dve, f"{u}.T.{i - 2}")
                    nc.vector.tensor_tensor(s_actv[:, i % 2], ps[:, FF:], s_sil[:, i % 2], ALU.mult).then_inc(moved["GU"], 1)
                    cut(dve, piece)
                    ps = take(dve, "TT", f"{u}.T.{i}")
                    if i >= 2:
                        dve.wait_ge(sem(f"down_{u}"), i - 1)
                    v, hi, lo = ps[:, 0:FF], *(x[:, i % 2].rearrange("p a b -> p (a b)") for x in (s_actTh, s_actTl))
                    split(hi, lo, v, moved["TT"])
                    cut(dve, piece + 1)
                    cut(dve, piece + 2)
                    piece += 3
                taken["Y4"] += 1
                for t in range(T):
                    dve.wait_ge(sem(f"down_{u}"), T * n - 1 + t)
                    for c in range(2):
                        last = nc.vector.tensor_tensor(X[:, t, c * 512:(c + 1) * 512], X[:, t, c * 512:(c + 1) * 512],
                                                       BANK[4 + 2 * t + c][:, :], ALU.add)
                    last.then_inc(moved["Y4"] if t else sem(f"added_{u}"), 1)

            def first_cuts(dve):
                if ph in phases:
                    for p_ in range(2 * PIECES):
                        cut(dve, p_)
            early_cuts[ph] = first_cuts

            pe_fns.append((ph, f_pe)); act_fns.append((ph, f_act)); dve_fns.append((ph, f_dve))
            pool_fns.append((ph, lambda pool: norm_pool(pool, u)))

        fproj = view(6144, T, IN2)
        fqz = view(11280, FH, S)
        fkT = view(13328, FH // 2, S)
        fsc = view(14352, FH, 3 * P)
        fprT = view(17424, FH, 3 * P)
        fo = view(4096, T, FW)
        logf = work[:, 20496:20528].rearrange("p (a b) -> p a b", a=4)
        cum = work[:, 20528:20544].rearrange("p (a b) -> p a b", a=2)
        ncumT = view(20544, S)
        fst = view(20800, 8, 16)
        pooledT = view(5120, 2, 2 * S)
        OG, OF, OU = 3 * FW, 4 * FW, 4 * FW + FH

        if "D" in phases:
            linear_units("w_fin", dram2("hy_w_in_2"), IN2)
            unit("pool_w", A["hy_pool_w_2"][0].rearrange("g c d -> c g d"), 4, P)
            linear_units("w_out2", dram2("hy_w_out_2"), D)

        def fox_pe(pe):
            norm_linear(pe, "d", "w_fin", IN2, "AD")
            pe.wait_ge(sem("const2_in"), 16)
            await_moved(pe, "w_fin.5.0", "w_fin.5.1")
            W = lambda g, b: C("pool")[:, (3 * g + b) * P:(3 * g + b + 1) * P]
            for gp in range(2):
                ps = fill(pe, "A", f"pooled.{gp}")
                for g in (2 * gp, 2 * gp + 1):
                    u = lambda t: fproj[:, t, OU + g * P:OU + (g + 1) * P]
                    o = (g % 2) * S
                    nc.tensor.matmul(ps[:, o:o + P], u(0), W(g, 0), start=True, stop=True)
                    nc.tensor.matmul(ps[:, o + P:o + S], u(0), W(g, 1), start=True, stop=False)
                    mm = nc.tensor.matmul(ps[:, o + P:o + S], u(1), W(g, 2), start=False, stop=True)
                mm.then_inc(full["A"], 1)
            pe.wait_ge(sem("logf"), 1)
            ps = fill(pe, "D", "cum")
            nc.tensor.matmul(ps[:, 0:FH], C("tri"), logf[:, 0], start=True, stop=True)
            nc.tensor.matmul(ps[:, FH:2 * FH], C("ones"), logf[:, 0], start=True, stop=False)
            nc.tensor.matmul(ps[:, FH:2 * FH], C("tri"), logf[:, 1], start=False, stop=True)
            nc.tensor.matmul(ps[0:FH, P:2 * P], logf[:, 0], C("tri"), start=True, stop=True)
            nc.tensor.matmul(ps[0:FH, 2 * P:3 * P], logf[:, 0], C("ones"), start=True, stop=False)
            nc.tensor.matmul(ps[0:FH, 2 * P:3 * P], logf[:, 1], C("tri"), start=False, stop=True).then_inc(full["D"], 1)
            await_moved(pe, "pooled.1")
            pw = weights(pe, "pool_w", "fmixed.1")
            for gp in range(2):
                ps = fill(pe, "D", f"fmixed.{gp}")
                for g in range(2):
                    mm = nc.tensor.matmul(ps[:, g * S:(g + 1) * S], pw[:, 2 * gp + g, :],
                                          pooledT[:, gp, g * S:(g + 1) * S], start=True, stop=True)
                mm.then_inc(full["D"], 1)
            for t in range(T):
                for j in range(2):
                    pe.wait_ge(sem("fqk"), T * t + j + 1)
                    ps = fill(pe, "D", f"fT.{j}.{t}")
                    for k in range(4):
                        mm = nc.tensor.transpose(ps[:, k * P:(k + 1) * P],
                                                 fproj[:, t, j * FW + k * P:j * FW + (k + 1) * P], ident)
                    mm.then_inc(full["D"], 1)
            await_moved(pe, "fT.1.1")
            for h in range(FH):
                ps = fill(pe, "D", f"fscore.{h}")
                for t, (lo, hi) in enumerate(((0, P), (P, 3 * P))):
                    nc.tensor.matmul(ps[:, lo:hi], fqz[:, h, t * P:(t + 1) * P], fkT[:, h // 2, 0:hi - lo],
                                     start=True, stop=False)
                    mm = nc.tensor.matmul(ps[:, lo:hi], C("sel")[0:FH, h * P:(h + 1) * P], ncumT[0:FH, 0:hi - lo],
                                          start=False, stop=True)
                mm.then_inc(full["D"], 1)
            for h in range(FH):
                pe.wait_ge(sem("fexp"), 2 * h + 2)
                ps = fill(pe, "A", f"fprT.{h}")
                for b in range(3):
                    mm = nc.tensor.transpose(ps[:, b * P:(b + 1) * P], fsc[:, h, b * P:(b + 1) * P], ident)
                mm.then_inc(full["A"], 1)
            await_moved(pe, f"fprT.{FH - 1}")
            v = lambda t, h: fproj[:, t, 2 * FW + h * HD:2 * FW + (h + 1) * HD]
            for t in range(T):
                ps = fill(pe, "D", f"fo.{t}")
                for h in range(FH):
                    o = slice(h * HD, (h + 1) * HD)
                    if t == 0:
                        mm = nc.tensor.matmul(ps[:, o], fprT[:, h, 0:P], v(0, h), start=True, stop=True)
                    else:
                        nc.tensor.matmul(ps[:, o], fprT[:, h, P:S], v(0, h), start=True, stop=False)
                        mm = nc.tensor.matmul(ps[:, o], fprT[:, h, S:3 * P], v(1, h), start=False, stop=True)
                mm.then_inc(full["D"], 1)
            for t in range(T):
                pe.wait_ge(sem("fgated"), t + 1)
                ps = fill(pe, "A", f"foT.{t}")
                for k in range(4):
                    mm = nc.tensor.transpose(ps[:, k * P:(k + 1) * P], fo[:, t, k * P:(k + 1) * P], ident)
                mm.then_inc(full["A"], 1)
            await_moved(pe, "foT.1", "fmixed.1")
            linear(pe, "w_out2", mixT, D, "DD")

        def fox_act(act):
            if "C" in phases:
                await_moved(act, f"x.{G - 1}.1.1")
                if "O" in phases:
                    act.wait_ge(sem("overflow_added"), 1)
            norm_act(act, "d", X)
            for c in range(6):
                w_ = min(512, IN2 - c * 512)
                copy_chunk_act(act, f"w_fin.{c}.0", fproj[:, 0, c * 512:c * 512 + w_])
            act.wait_ge(sem("absz"), 1)
            nc.scalar.activation(logf[:, 2:4], logf[:, 2:4], ACT.Exp, scale=-1.0).then_inc(sem("expz"), 1)
            act.wait_ge(sem("expz"), 1)
            nc.scalar.activation(logf[:, 2:4], logf[:, 2:4], ACT.Ln, bias=1.0).then_inc(sem("lnz"), 1)
            for gp in range(2):
                copy_chunk_act(act, f"pooled.{gp}", pooledT[:, gp])
            await_moved(act, "w_fin.3.0", "w_fin.3.1")
            og = fproj[:, :, OG:OG + FW]
            nc.scalar.activation(og, og, ACT.Sigmoid).then_inc(sem("fgate"), 1)
            for h in range(FH):
                act.wait_ge(sem("fnmax"), h // 2 + 1)
                for t, (lo, hi) in enumerate(((0, P), (P, 3 * P))):
                    nc.scalar.activation(fsc[:, h, lo:hi], fsc[:, h, lo:hi], ACT.Exp, bias=fst[:, 4 + t, h:h + 1],
                                         accum_out=fst[:, 6 + t, h:h + 1]).then_inc(sem("fexp"), 1)
                if h:
                    copy_chunk_act(act, f"fprT.{h - 1}", fprT[:, h - 1])
            copy_chunk_act(act, f"fprT.{FH - 1}", fprT[:, FH - 1])
            for t in range(T):
                ps = take(act, "A", f"foT.{t}")
                nc.scalar.copy(mixT[:, 0:4, t * P:(t + 1) * P], ps[:, :].rearrange("p (k n) -> p k n", k=4)).then_inc(moved["A"], 1)

        def fox_pool(pool):
            norm_pool(pool, "d")
            await_moved(pool, "w_fin.0.0", "w_fin.0.1")
            nc.gpsimd.memset(fqz[HD:P, 0::2, :], 0.0).then_inc(sem("fqz_zero"), 1)
            pool.wait_ge(sem("fqz_zero"), 1)
            nc.gpsimd.memset(fqz[0:HD, 1::2, :], 0.0).then_inc(sem("fqz_zero"), 1)
            pool.wait_ge(sem("fqz_zero"), 2)
            for t in range(T):
                pool.wait_ge(sem("fss"), t + 1)
                L = links["pool"]
                L(nc.gpsimd.tensor_scalar(fst[:, 2 + t, 0:FH], fst[:, t, 0:FH], 1.0, HD * EPS, ALU.mult, ALU.add))
                L(nc.gpsimd.tensor_scalar(fst[:, 2 + t, FH:], fst[:, t, FH:], 1.0 / HD, EPS, ALU.mult, ALU.add))
                nc.gpsimd.tensor_tensor(fst[:, 2 + t], fst[:, 2 + t], neghalf[:, 0:16], ALU.pow).then_inc(sem("frstd"), 1)

        def fox_dve(dve):
            L, V = links["dve"], nc.vector
            norm_dve(dve, "d", "mix_norm_2")
            for c in range(6):
                w_ = min(512, IN2 - c * 512)
                copy_chunk_dve(dve, f"w_fin.{c}.1", fproj[:, 1, c * 512:c * 512 + w_])
                if c == 1:
                    await_moved(dve, "w_fin.1.0", "w_fin.1.1")
                    for t in range(T):
                        x_ = fproj[:, t, 0:2 * FW]
                        L(V.tensor_tensor(sq[:, t], x_, x_, ALU.mult))
                        V.reduce_sum(fst[:, t], sq[:, t].rearrange("p (h d) -> p h d", h=16), AX.X).then_inc(sem("fss"), 1)
            await_moved(dve, "w_fin.4.0", "w_fin.4.1")
            dve.wait_ge(sem("rowsmall_in"), 80)
            L(V.tensor_tensor(logf[:, 0:2], fproj[:, :, OF:OF + FH], bc(fbias, T, 1), ALU.add))
            L(V.scalar_tensor_tensor(logf[:, 2:4], logf[:, 0:2], -1.0, logf[:, 0:2], ALU.mult, ALU.max))
            V.tensor_scalar(logf[:, 0:2], logf[:, 0:2], 0.0, None, ALU.min).then_inc(sem("absz"), 1)
            dve.wait_ge(sem("absz"), 1)
            dve.wait_ge(sem("lnz"), 1)
            V.tensor_tensor(logf[:, 0:2], logf[:, 0:2], logf[:, 2:4], ALU.subtract).then_inc(sem("logf"), 1)
            for t in range(T):
                dve.wait_ge(sem("frstd"), t + 1)
                for j in range(2):
                    v = fproj[:, t, j * FW:(j + 1) * FW].rearrange("p (h d) -> p h d", h=FH)
                    V.tensor_tensor(v, v, bc(fst[:, 2 + t, j * FH:(j + 1) * FH], HD, 2), ALU.mult).then_inc(sem("fqk"), 1)
            ps = take(dve, "D", "cum")
            V.tensor_copy(cum, ps[:, 0:2 * FH].rearrange("p (a b) -> p a b", a=2))
            V.tensor_scalar(ncumT[0:FH], ps[0:FH, P:3 * P], -1.0, None, ALU.mult).then_inc(moved["D"], 1)
            for gp in range(2):
                ps = take(dve, "D", f"fmixed.{gp}")
                V.tensor_tensor(mixT[:, 4 + 2 * gp:6 + 2 * gp], ps[:, :].rearrange("p (k n) -> p k n", k=2),
                                bc(col("hy_pool_scale_2", 2, 2 * gp), S, 2), ALU.mult).then_inc(moved["D"], 1)
            dve.wait_ge(sem("fqz_zero"), 2)
            dve.wait_ge(sem("gain2_in"), 64)
            for t in range(T):
                for j in range(2):
                    ps = take(dve, "D", f"fT.{j}.{t}")
                    v = ps[:, :].rearrange("p (k n) -> p k n", k=4)
                    s_ = slice(t * P, (t + 1) * P)
                    if j == 0:
                        V.tensor_scalar(fqz[0:HD, 0::2, s_], v[0:HD], cols[0:HD, P:P + 1], None, ALU.mult)
                        V.tensor_scalar(fqz[HD:, 1::2, s_], v[HD:], cols[HD:, P:P + 1], None, ALU.mult).then_inc(moved["D"], 1)
                    else:
                        V.tensor_scalar(fkT[:, :, s_], v, cols[:, P + 1:P + 2], None, ALU.mult).then_inc(moved["D"], 1)
            await_moved(dve, "cum")
            for h in range(FH):
                ps = take(dve, "D", f"fscore.{h}")
                for t, (lo, hi) in enumerate(((0, P), (P, 3 * P))):
                    last = V.scalar_tensor_tensor(fsc[:, h, lo:hi], ps[:, lo:hi], cum[:, t, h:h + 1], C("cmask")[:, lo:hi],
                                                  ALU.add, ALU.add)
                last.then_inc(moved["D"], 1)
                if h % 2:
                    await_moved(dve, f"fscore.{h}")
                    L(V.tensor_reduce(fst[:, 4, h - 1:h + 1], fsc[:, h - 1:h + 1, 0:P], AX.X, ALU.max, negate=True))
                    V.tensor_reduce(fst[:, 5, h - 1:h + 1], fsc[:, h - 1:h + 1, P:], AX.X, ALU.max, negate=True) \
                        .then_inc(sem("fnmax"), 1)
            dve.wait_ge(sem("fexp"), 2 * FH)
            L(V.reciprocal(fst[:, 6:8, 0:FH], fst[:, 6:8, 0:FH]))
            dve.wait_ge(sem("fgate"), 1)
            for t in range(T):
                ps = take(dve, "D", f"fo.{t}")
                v = fo[:, t].rearrange("p (h d) -> p h d", h=FH)
                V.tensor_tensor(v, ps[:, :].rearrange("p (h d) -> p h d", h=FH), bc(fst[:, 6 + t, 0:FH], HD, 2),
                                ALU.mult).then_inc(moved["D"], 1)
                await_moved(dve, f"fo.{t}")
                V.tensor_tensor(fo[:, t], fo[:, t], fproj[:, t, OG:OG + FW], ALU.mult).then_inc(sem("fgated"), 1)
            early_cuts["E"](dve)
            residual_dve(dve, "w_out2")

        pe_fns.append(("D", fox_pe)); act_fns.append(("D", fox_act))
        pool_fns.append(("D", fox_pool)); dve_fns.append(("D", fox_dve))

        add_swiglu("E", "f0", 0, lambda act: after_residual(act, "w_out2"), ("fmixed.1", "fo.1"))

        dxT = view(2048, KD, S)
        xi = [view(4096, KD, S), view(6144, KD, S)]
        r_ = view(8192, T, D)
        k_ = view(10240, T, D)
        v_ = view(12288, T, D)
        a_ = view(14336, T, D)
        s_ = view(16384, T, D)
        g_ = view(18432, T, D)
        rows5 = view(20480, 5, D)
        k_k, k_a, r_k, ln_w, ln_b = (rows5[:, i] for i in range(5))
        wlow = view(25600, 1, S)
        alow = view(25856, 1, S)
        glow = view(25600, 2, S)
        rst = view(26112, 24, 16)
        fch = view(26112 + 160, 3, 8)
        fraw = view(26112 + 192, 8, T, 4)
        Ep, Em, Ex = view(0, D), view(1024, D), view(2048, D)
        kk, tmpk = view(3072, D), g_[:, 1]
        NM = view(0, 8, 512)
        AZ = view(4096, 8, 256)
        BK = view(6144, 4, 256)
        MV = view(6144, 8, HD)
        PM = view(7168, 8, P)
        RB = ring_w[:, 4 * SLOT:8 * SLOT]
        Xi = RB[:, 0:1024].rearrange("p (h n) -> p h n", h=8)
        Yi = RB[:, 1024:2048].rearrange("p (h n) -> p h n", h=8)
        UG = RB[:, 2048:3072].rearrange("p (h n) -> p h n", h=8)
        HT = RB[:, 3072:4096].rearrange("p (q n) -> p q n", q=8)
        WZ = RB[:, 4096:6144].rearrange("p (c q n) -> p c q n", c=2, q=8)
        Y0 = RB[:, 6144:7168]
        SS = RB[:, 7168:8192].rearrange("p (b q n) -> p b q n", b=2, q=8)
        NP_ = RH // 2

        if "F" in phases:
            def lora(name, w1, w2, bias):
                unit(f"{name}1", dram2(w1).rearrange("(k p) n -> p k n", p=P), KD, DL)
                unit(f"{name}2", None, 1, D, parts=DL + 1,
                     pieces=lambda v: [(dram2(w2).unsqueeze(1), v[0:DL]), (A[bias][0:1, :].unsqueeze(1), v[DL:DL + 1])])
            lora("lw", "rw_w1_2", "rw_w2_2", "rw_w0_2")
            lora("la", "rw_a1_2", "rw_a2_2", "rw_a0_2")
            linear_units("w_rk", dram2("rw_w_k_2"), D)
            linear_units("w_rr", dram2("rw_w_r_2"), D)
            linear_units("w_rv", dram2("rw_w_v_2"), D)
            unit("g1", dram2("rw_g1_2").rearrange("(k p) n -> p k n", p=P), KD, GL)
            g2 = dram2("rw_g2_2")
            unit("g2", None, 2, D, pieces=lambda v: [(g2[0:P, :], v[:, 0]), (g2[P:GL, :], v[0:GL - P, 1])])
            for i, (c, k0) in enumerate(((0, 0), (0, 4), (1, 0), (1, 4))):
                unit(f"w_ro.{c}.{k0}", dram2("rw_w_o_2")[k0 * P:(k0 + 4) * P, c * 512:(c + 1) * 512]
                     .rearrange("(k p) n -> p k n", p=P), 4, 512, slot=i)
            next_slot[0] = 0

        ORDER = (("w", 1), ("a", 4), ("k", 2), ("r", 0), ("v", 3), ("g", 5))

        def rw_heads(half):
            return range(8 * half, 8 * half + 8)

        def rwkv_pe(pe):
            norm_pe(pe, "f")
            x = lambda i: xi[i % 2]

            def low(i, name, m, job):
                w1 = weights(pe, name, job)
                pe.wait_ge(sem("xi"), i + 1)
                ps = fill(pe, "A", job)
                for o, n, c0 in ((0, min(m, P), 0),) + (((P, m - P, S),) if m > P else ()):
                    for k in range(KD):
                        mm = nc.tensor.matmul(ps[0:n, c0:c0 + S], w1[:, k, o:o + n], x(i)[:, k, :],
                                              start=k == 0, stop=k == KD - 1)
                mm.then_inc(full["A"], 1)
            for i, (name, lowT) in enumerate((("lw", wlow), ("la", alow))):
                low(i, name + "1", DL, f"{name}low")
                await_moved(pe, f"{name}low")
                if i == 0:
                    pe.wait_ge(sem("low_ones"), 2)
                w2 = weights(pe, name + "2", f"{name}.1.1")
                for c in range(2):
                    for t in range(T):
                        ps = fill(pe, "A", f"{name}.{c}.{t}")
                        nc.tensor.matmul(ps[:, :], lowT[0:DL + 1, 0, t * P:(t + 1) * P], w2[:, 0, c * 512:(c + 1) * 512],
                                         start=True, stop=True).then_inc(full["A"], 1)
            for i, name in ((2, "w_rk"), (3, "w_rr")):
                pe.wait_ge(sem("xi"), i + 1)
                linear(pe, name, x(i), D, "AD")
            await_moved(pe, "lw.1.1")
            pe.wait_ge(sem("const2_in"), 16)
            def cumulative(t):
                for c in range(2):
                    for which in ("rwcum", "rwcumx"):
                        ps = fill(pe, "A", f"{which}.{c}.{t}")
                        nc.tensor.matmul(ps[:, :], C(which), s_[:, t, c * 512:(c + 1) * 512],
                                         start=True, stop=True).then_inc(full["A"], 1)
            cumulative(0)
            ps = fill(pe, "D", "fraw")
            for t in range(T):
                for q in range(NP_):
                    o = (q * T + t) * 4
                    sq_ = s_[:, t, q * P:(q + 1) * P]
                    nc.tensor.matmul(ps[:, o:o + 2], sq_, C("rwcum")[:, CH - 1::CH], start=True, stop=True)
                    mm = nc.tensor.matmul(ps[:, o + 2:o + 4], sq_, C("rwmid")[:, CH - 1::CH], start=True, stop=True)
            mm.then_inc(full["D"], 1)
            pe.wait_ge(sem("xi"), 5)
            linear(pe, "w_rv", x(4), D, "AA")
            cumulative(1)
            low(5, "g1", GL, "glow")
            await_moved(pe, "glow")
            w2 = weights(pe, "g2", "g.1.1")
            for t in range(T):
                for c in range(2):
                    ps = fill(pe, "A", f"g.{c}.{t}")
                    nc.tensor.matmul(ps[:, :], glow[:, 0, t * P:(t + 1) * P], w2[:, 0, c * 512:(c + 1) * 512],
                                     start=True, stop=False)
                    nc.tensor.matmul(ps[:, :], glow[0:GL - P, 1, t * P:(t + 1) * P],
                                     w2[0:GL - P, 1, c * 512:(c + 1) * 512], start=False, stop=True).then_inc(full["A"], 1)
            for t in range(T):
                pe.wait_ge(sem("hats"), t + 1)
                for half in range(2):
                    heads_pe(pe, t, half)
                scan_pe(pe, t)
            for t in range(T):
                pe.wait_ge(sem("y_done"), t + 1)
                for half in range(2):
                    transposed(pe, "D", f"ryT.{t}.{half}", r_, t, half)
                await_moved(pe, f"ryT.{t}.1")
                for c in range(2):
                    wv = [weights(pe, f"w_ro.{c}.{k0}", f"w_ro.{c}.1") for k0 in (0, 4)]
                    ps = fill(pe, "D", f"w_ro.{c}.{t}")
                    for k in range(KD):
                        mm = nc.tensor.matmul(ps[:, :], mixT[:, k, t * P:(t + 1) * P], wv[k // 4][:, k % 4, :],
                                              start=k == 0, stop=k == KD - 1)
                    mm.then_inc(full["D"], 1)

        def heads_pe(pe, t, half):
            u = f"{t}.{half}"
            for gq in range(2):
                for kind, (x0, x1) in (("AR", (s_, r_)), ("BK", (a_, k_))):
                    ps = fill(pe, "A", f"{kind}.{u}.{gq}")
                    for q in range(2):
                        o = (4 * half + 2 * gq + q) * P
                        for j, src in enumerate((x0, x1)):
                            mm = nc.tensor.transpose(ps[:, (2 * q + j) * P:(2 * q + j + 1) * P], src[:, t, o:o + P], ident)
                    mm.then_inc(full["A"], 1)
            for h in range(8):
                if h % 4 == 0:
                    await_moved(pe, f"BK.{u}.{h // 4}")
                ps = fill(pe, "D", f"NM.{u}.{h}")
                nc.tensor.matmul(ps[:, 0:S], BK[:, h // 2, 0:P], AZ[:, h, :], start=True, stop=True)
                nc.tensor.matmul(ps[:, S:], BK[:, h // 2, P:], AZ[:, h, :], start=True, stop=True).then_inc(full["D"], 1)

            def four(name, gq, lhs, rhs, ring="D"):
                ps = fill(pe, ring, f"{name}.{u}.{gq}")
                for h in range(4):
                    mm = nc.tensor.matmul(ps[:, h * P:(h + 1) * P], lhs(4 * gq + h), rhs(4 * gq + h), start=True, stop=True)
                mm.then_inc(full[ring], 1)
            for gq in range(2):
                pe.wait_ge(sem("Y2"), 4 * t + 2 * half + gq + 1)
                ps = fill(pe, "A", f"X2.{u}.{gq}")
                for h in range(4):
                    mm = nc.tensor.transpose(ps[:, h * P:(h + 1) * P], Yi[:, 4 * gq + h], ident)
                mm.then_inc(full["A"], 1)
            for gq in range(2):
                ps = fill(pe, "A", f"Mv.{u}.{gq}")
                for h in range(4):
                    hh = 4 * gq + h
                    o = (8 * half + hh) * HD
                    mm = nc.tensor.matmul(ps[:, h * HD:(h + 1) * HD], NM[:, hh, S:S + P], v_[:, t, o:o + HD],
                                          start=True, stop=True)
                mm.then_inc(full["A"], 1)
            for lv in range(5):
                for gq in range(2):
                    if lv == 0:
                        await_moved(pe, f"X2.{u}.{gq}")
                    else:
                        await_moved(pe, f"dY{lv - 1}.{u}.{gq}")
                    four(f"P{lv}", gq, lambda h: NM[:, h, 0:P], lambda h: Xi[:, h])
                for gq in range(2):
                    await_moved(pe, f"P{lv}.{u}.{gq}")
                    if lv < 4:
                        four(f"dX{lv}", gq, lambda h: Yi[:, h], lambda h: PM[:, h])
                    four(f"dY{lv}", gq, lambda h: PM[:, h], lambda h: Yi[:, h])
            for gq in range(2):
                await_moved(pe, f"dY4.{u}.{gq}", f"Mv.{u}.{gq}")
                ps = fill(pe, "A", f"UG.{u}.{gq}")
                for h in range(4):
                    hh = 4 * gq + h
                    o = (8 * half + hh) * HD
                    nc.tensor.matmul(ps[:, h * P:h * P + HD], Yi[:, hh], MV[:, hh], start=True, stop=True)
                    mm = nc.tensor.matmul(ps[:, h * P + HD:(h + 1) * P], Yi[:, hh], s_[:, t, o:o + HD], start=True, stop=True)
                mm.then_inc(full["A"], 1)
            for gq in range(2):
                await_moved(pe, f"UG.{u}.{gq}")
                ps = fill(pe, "D", f"yH.{u}.{gq}")
                for h in range(4):
                    hh = 4 * gq + h
                    o = (8 * half + hh) * HD
                    nc.tensor.matmul(ps[:, h * HD:(h + 1) * HD], NM[:, hh, P:S], UG[:, hh, 0:HD], start=True, stop=False)
                    nc.tensor.matmul(ps[:, h * HD:(h + 1) * HD], NM[:, hh, S + P:], v_[:, t, o:o + HD], start=False, stop=True)
                for h in range(4):
                    hh = 4 * gq + h
                    p = (h % 2) * HD
                    mm = nc.tensor.matmul(ps[p:p + HD, S + (h // 2) * P:S + (h // 2 + 1) * P], UG[:, hh, HD:], NM[:, hh, P:S],
                                          start=True, stop=True)
                mm.then_inc(full["D"], 1)
                for c in range(2):
                    ps = fill(pe, "D", f"WZ{c}.{u}.{gq}")
                    w = slice(c * CH, (c + 1) * CH)
                    for h in range(4):
                        hh = 4 * gq + h
                        p = (h % 2) * HD
                        o = (8 * half + hh) * HD
                        c0 = (h // 2) * P
                        nc.tensor.matmul(ps[p:p + HD, c0:c0 + HD], UG[w, hh, HD:], a_[w, t, o:o + HD], start=True, stop=True)
                        nc.tensor.matmul(ps[p:p + HD, c0 + HD:c0 + P], a_[w, t, o:o + HD], UG[w, hh, 0:HD], start=True, stop=False)
                        mm = nc.tensor.matmul(ps[p:p + HD, c0 + HD:c0 + P], k_[w, t, o:o + HD], v_[w, t, o:o + HD],
                                              start=False, stop=True)
                    mm.then_inc(full["D"], 1)

        def scan_pe(pe, t):
            await_moved(pe, f"WZ1.{t}.1.1")
            for c in range(2):
                ch = 2 * t + c
                if ch:
                    pe.wait_ge(sem("state"), ch)
                    for par in range(2):
                        ps = fill(pe, "D", f"yS.{ch}.{par}")
                        p = slice(par * HD, (par + 1) * HD)
                        for q in range(NP_):
                            mm = nc.tensor.matmul(ps[c * CH:(c + 1) * CH, q * HD:(q + 1) * HD], HT[p, q, c * CH:(c + 1) * CH],
                                                  SS[p, ch % 2, q], start=True, stop=True)
                        mm.then_inc(full["D"], 1)
                    if ch < 3:
                        for par in range(2):
                            ps = fill(pe, "D", f"S.{ch}.{par}")
                            p = slice(par * HD, (par + 1) * HD)
                            for q in range(NP_):
                                mm = nc.tensor.matmul(ps[p, q * HD:(q + 1) * HD], WZ[p, c, q, 0:HD], SS[p, ch % 2, q],
                                                      start=True, stop=True)
                            mm.then_inc(full["D"], 1)

        def rwkv_act(act):
            norm_act(act, "f", X, ready=lambda t: await_moved(act, "y_f0") if "E" in phases else None)
            for name, lowT, fn in (("lw", wlow, ACT.Tanh), ("la", alow, ACT.Copy)):
                ps = take(act, "A", f"{name}low")
                nc.scalar.activation(lowT[0:DL, 0, :], ps[0:DL, 0:S], fn).then_inc(moved["A"], 1)
                for c in range(2):
                    for t in range(T):
                        ps = take(act, "A", f"{name}.{c}.{t}")
                        dst = s_ if name == "lw" else a_
                        nc.scalar.activation(dst[:, t, c * 512:(c + 1) * 512], ps[:, :], ACT.Sigmoid).then_inc(moved["A"], 1)
            for name, dst in (("w_rk", k_), ("w_rr", r_)):
                for c in range(2):
                    copy_chunk_act(act, f"{name}.{c}.0", dst[:, 0, c * 512:(c + 1) * 512])
            act.wait_ge(sem("xi"), 6)
            for t in range(T):
                if t:
                    act.wait_ge(sem("hats"), t)
                for c in range(2):
                    w = slice(c * 512, (c + 1) * 512)
                    ps = take(act, "A", f"rwcum.{c}.{t}")
                    nc.scalar.activation(Ep[:, w], ps[:, :], ACT.Exp)
                    nc.scalar.activation(Em[:, w], ps[:, :], ACT.Exp, scale=-1.0).then_inc(moved["A"], 1)
                    ps = take(act, "A", f"rwcumx.{c}.{t}")
                    nc.scalar.activation(Ex[:, w], ps[:, :], ACT.Exp).then_inc(moved["A"], 1)
                if t == 0:
                    for c in range(2):
                        for t_ in range(T):
                            copy_chunk_act(act, f"w_rv.{c}.{t_}", v_[:, t_, c * 512:(c + 1) * 512])
            act.wait_ge(sem("fsum"), 1)
            nc.scalar.activation(fch, fch, ACT.Exp).then_inc(sem("fch"), 1)
            ps = take(act, "A", "glow")
            nc.scalar.activation(glow[:, 0], ps[:, 0:S], ACT.Sigmoid)
            nc.scalar.activation(glow[0:GL - P, 1], ps[0:GL - P, S:], ACT.Sigmoid).then_inc(moved["A"], 1)
            for t in range(T):
                if t:
                    act.wait_ge(sem("hats"), 2)
                for c in range(2):
                    copy_chunk_act(act, f"g.{c}.{t}", g_[:, t, c * 512:(c + 1) * 512])
            act.wait_ge(sem("az_zero"), 2)
            for t in range(T):
                for half in range(2):
                    u = f"{t}.{half}"
                    if t + half:
                        prev = f"{(2 * t + half - 1) // 2}.{(2 * t + half - 1) % 2}"
                        peek(act, f"WZ1.{prev}.1")
                        await_moved(act, f"WZ1.{prev}.1")
                    for gq in range(2):
                        ps = take(act, "A", f"AR.{u}.{gq}")
                        v = ps[:, :].rearrange("p (q n) -> p q n", q=2)
                        nc.scalar.copy(AZ[0:HD, 4 * gq:4 * gq + 4:2], v[0:HD])
                        nc.scalar.copy(AZ[HD:, 4 * gq + 1:4 * gq + 4:2], v[HD:]).then_inc(moved["A"], 1)
                        ps = take(act, "A", f"BK.{u}.{gq}")
                        nc.scalar.copy(BK[:, 2 * gq:2 * gq + 2], ps[:, :].rearrange("p (q n) -> p q n", q=2)).then_inc(moved["A"], 1)
                    for gq in range(2):
                        ps = take(act, "A", f"X2.{u}.{gq}")
                        nc.scalar.copy(Xi[:, 4 * gq:4 * gq + 4].rearrange("p h n -> p (h n)"), ps[:, :]).then_inc(moved["A"], 1)
                    for gq in range(2):
                        ps = take(act, "A", f"Mv.{u}.{gq}")
                        nc.scalar.copy(MV[:, 4 * gq:4 * gq + 4].rearrange("p h n -> p (h n)"), ps[:, 0:S]).then_inc(moved["A"], 1)
                    for gq in range(2):
                        ps = take(act, "A", f"UG.{u}.{gq}")
                        nc.scalar.copy(UG[:, 4 * gq:4 * gq + 4].rearrange("p h n -> p (h n)"), ps[:, :]).then_inc(moved["A"], 1)

        def rwkv_pool(pool):
            norm_pool(pool, "f")
            L = links["pool"]
            pool.wait_ge(sem("rstd_f"), T)
            nc.gpsimd.memset(wlow[HD:HD + 1], 1.0).then_inc(sem("low_ones"), 1)
            pool.wait_ge(sem("low_ones"), 1)
            nc.gpsimd.memset(alow[HD:HD + 1], 1.0).then_inc(sem("low_ones"), 1)
            pool.wait_ge(sem("low_ones"), 2)
            for t in range(T):
                pool.wait_ge(sem("kk_ss"), t + 1)
                L(nc.gpsimd.tensor_scalar(rst[:, 2 + t], rst[:, t], 1e-24, None, ALU.max))
                nc.gpsimd.tensor_tensor(rst[:, 2 + t], rst[:, 2 + t], neghalf[:, 0:16], ALU.pow).then_inc(sem("kk_norm"), 1)
            pool.wait_ge(sem("hats"), 2)
            peek(pool, "w_rv.1.1")
            nc.gpsimd.memset(AZ[HD:, 0::2], 0.0).then_inc(sem("az_zero"), 1)
            pool.wait_ge(sem("az_zero"), 1)
            nc.gpsimd.memset(AZ[0:HD, 1::2], 0.0).then_inc(sem("az_zero"), 1)
            pool.wait_ge(sem("az_zero"), 2)
            for t in range(T):
                pool.wait_ge(sem("y_var"), t + 1)
                rsqrt(pool, rst[:, 8 + t], rst[:, 6 + t], 16, 1.0, GN_EPS, sem("y_rstd"))
                if t == 0:
                    pool.wait_ge(sem("y_rstd"), 1)
                    await_moved(pool, "g.1.0")
                    group_norm(L, nc.gpsimd, t, lambda: None)
                    pool.wait_ge(sem("y_done"), 1)

        def rwkv_rows(sp):
            for i, name in enumerate(("rw_k_k_2", "rw_k_a_2", "rw_r_k_2", "rw_ln_w_2", "rw_ln_b_2")):
                src = A[name] if name != "rw_r_k_2" else A[name].rearrange("a h d -> a (h d)")
                sp.dma_start(rows5[:, i], src.to_broadcast([P, D])).then_inc(sem("rows5_in"), 16)

        def rwkv_dve(dve):
            L, V = links["dve"], nc.vector
            norm_dve(dve, "f", "mix_norm_2", gi=KD)
            await_moved(dve, *hT_jobs("f"))
            V.tensor_tensor(dxT[:, :, 1:], hT[:, :, 0:S - 1], hT[:, :, 1:], ALU.subtract)
            L(V.tensor_scalar(dxT[:, :, 0:1], hT[:, :, 0:1], -1.0, None, ALU.mult))

            def shift(i):
                if i >= 2:
                    peek(dve, ("lwlow", "lalow", "w_rk.1.1", "w_rr.1.1")[i - 2])
                mu = ORDER[i][1]
                for k in range(KD):
                    last = V.scalar_tensor_tensor(xi[i % 2][:, k], dxT[:, k], col("rw_mu_2", 1, 8 * mu + k), hT[:, k],
                                                  ALU.mult, ALU.add)
                last.then_inc(sem("xi"), 1)
            shift(0)
            shift(1)
            shift(2)
            shift(3)
            for c in range(2):
                copy_chunk_dve(dve, f"w_rk.{c}.1", k_[:, 1, c * 512:(c + 1) * 512])
            shift(4)
            for c in range(2):
                copy_chunk_dve(dve, f"w_rr.{c}.1", r_[:, 1, c * 512:(c + 1) * 512])
            shift(5)
            ps = take(dve, "D", "fraw")
            V.tensor_copy(fraw.rearrange("p q t c -> p (q t c)"), ps[:, 0:64]).then_inc(moved["D"], 1)
            await_moved(dve, "fraw")
            for n in range(3):
                t0, c0, t1, c1 = n // 2, n % 2, (n + 1) // 2, (n + 1) % 2
                last = V.tensor_tensor(fch[:, n], fraw[:, :, t0, c0], fraw[:, :, t1, 2 + c1], ALU.add)
            last.then_inc(sem("fsum"), 1)
            dve.wait_ge(sem("rows5_in"), 80)
            dve.wait_ge(sem("xi"), 6)
            h16 = lambda v: v.rearrange("p (h d) -> p h d", h=RH)
            await_moved(dve, "w_rk.1.0", "w_rk.1.1", "w_rr.1.0", "w_rr.1.1", "la.1.1")
            for t in range(T):
                r, k, a, s = r_[:, t], k_[:, t], a_[:, t], s_[:, t]
                L(V.tensor_tensor(kk, k, k_k, ALU.mult))
                L(V.tensor_tensor(tmpk, kk, kk, ALU.mult))
                V.reduce_sum(rst[:, t], h16(tmpk), AX.X).then_inc(sem("kk_ss"), 1)
                dve.wait_ge(sem("kk_ss"), t + 1)
                L(V.scalar_tensor_tensor(tmpk, a, -1.0, k_a, ALU.add, ALU.mult))
                L(V.scalar_tensor_tensor(k, tmpk, 1.0, k, ALU.add, ALU.mult))
                L(V.tensor_tensor(tmpk, r, k, ALU.mult))
                L(V.tensor_tensor(tmpk, tmpk, r_k, ALU.mult))
                L(V.reduce_sum(rst[:, 4 + t], h16(tmpk), AX.X))
                dve.wait_ge(sem("kk_norm"), t + 1)
                L(V.tensor_tensor(h16(kk), h16(kk), bc(rst[:, 2 + t], HD, 2), ALU.mult))
                await_moved(dve, f"rwcum.1.{t}", f"rwcumx.1.{t}")
                L(V.tensor_tensor(a, a, kk, ALU.mult))
                V.tensor_tensor(a, a, Em, ALU.mult)
                peek(dve, "fraw")
                V.scalar_tensor_tensor(s, kk, -1.0, Ex, ALU.mult, ALU.mult)
                V.tensor_tensor(r, r, Ep, ALU.mult)
                V.tensor_tensor(k, k, Em, ALU.mult).then_inc(sem("hats"), 1)
                dve.wait_ge(sem("hats"), t + 1)
            dve.wait_ge(sem("const2_in"), 16)
            peek(dve, "g.1.1")
            for t in range(T):
                for half in range(2):
                    heads_dve(dve, t, half)
                scan_dve(dve, t)
            for t in range(T):
                if t:
                    group_norm_dve(dve, t)
                for half in range(2):
                    ps = take(dve, "D", f"ryT.{t}.{half}")
                    V.tensor_copy(mixT[:, half * 4:half * 4 + 4, t * P:(t + 1) * P],
                                  ps[:, :].rearrange("p (k n) -> p k n", k=4)).then_inc(moved["D"], 1)
                if t:
                    early_cuts["G"](dve)
                for c in range(2):
                    ps = take(dve, "D", f"w_ro.{c}.{t}")
                    x_ = X[:, t, c * 512:(c + 1) * 512]
                    V.tensor_tensor(x_, x_, ps[:, :], ALU.add).then_inc(moved["D"], 1)

        def heads_dve(dve, t, half):
            V = nc.vector
            u = f"{t}.{half}"
            for h in range(8):
                ps = take(dve, "D", f"NM.{u}.{h}")
                V.tensor_tensor(NM[:, h], ps[:, :], C("rwmask"), ALU.mult).then_inc(moved["D"], 1)
                if h % 4 == 3:
                    g4 = slice(h - 3, h + 1)
                    await_moved(dve, f"NM.{u}.{h}")
                    links["dve"](V.tensor_tensor(Yi[:, g4], NM[:, g4, 0:P], bc(C("rwlevT"), 4, 1), ALU.mult))
                    V.tensor_tensor(Yi[:, g4], Yi[:, g4], bc(ident, 4, 1), ALU.add).then_inc(sem("Y2"), 1)
            four = lambda ps: ps[:, :].rearrange("p (h n) -> p h n", h=4)
            for lv in range(5):
                for gq in range(2):
                    g4 = slice(4 * gq, 4 * gq + 4)
                    ps = take(dve, "D", f"P{lv}.{u}.{gq}")
                    V.tensor_tensor(PM[:, g4], four(ps), bc(C("rwlev")[:, lv * P:(lv + 1) * P], 4, 1),
                                    ALU.mult).then_inc(moved["D"], 1)
                for gq in range(2):
                    g4 = slice(4 * gq, 4 * gq + 4)
                    if lv < 4:
                        ps = take(dve, "D", f"dX{lv}.{u}.{gq}")
                        if lv == 0:
                            await_moved(dve, f"X2.{u}.{gq}")
                        V.tensor_tensor(Xi[:, g4], Xi[:, g4], four(ps), ALU.add).then_inc(moved["D"], 1)
                    ps = take(dve, "D", f"dY{lv}.{u}.{gq}")
                    V.tensor_tensor(Yi[:, g4], Yi[:, g4], four(ps), ALU.add).then_inc(moved["D"], 1)
            for gq in range(2):
                ps = take(dve, "D", f"yH.{u}.{gq}")
                if t:
                    dve.wait_ge(sem("y_done"), 1)
                o = 512 * half + S * gq
                q2 = slice(4 * half + 2 * gq, 4 * half + 2 * gq + 2)
                V.tensor_copy(Y0[:, o:o + S], ps[:, 0:S])
                v = ps[:, S:].rearrange("p (q n) -> p q n", q=2)
                V.tensor_tensor(HT[0:HD, q2], v[0:HD], AZ[0:HD, 4 * gq:4 * gq + 4:2, P:], ALU.add)
                V.tensor_tensor(HT[HD:, q2], v[HD:], AZ[HD:, 4 * gq + 1:4 * gq + 4:2, P:], ALU.add).then_inc(moved["D"], 1)
                for c in range(2):
                    ps = take(dve, "D", f"WZ{c}.{u}.{gq}")
                    v = ps[:, 0:S].rearrange("p (q n) -> p q n", q=2)
                    V.tensor_tensor(WZ[:, c, q2, 0:HD], v[:, :, 0:HD], bc(C("eye2"), 2, 1), ALU.add)
                    V.tensor_copy(WZ[:, c, q2, HD:], v[:, :, HD:]).then_inc(moved["D"], 1)

        def scan_dve(dve, t):
            L, V = links["dve"], nc.vector
            await_moved(dve, f"WZ1.{t}.1.1")
            for c in range(2):
                ch = 2 * t + c
                if ch:
                    for par in range(2):
                        ps = take(dve, "D", f"yS.{ch}.{par}")
                        w = slice(c * CH, (c + 1) * CH)
                        y = Y0[w, :].rearrange("p (q x d) -> p q x d", q=NP_, x=2)[:, :, par]
                        V.tensor_tensor(y, y, ps[w, :].rearrange("p (q d) -> p q d", q=NP_), ALU.add).then_inc(moved["D"], 1)
                    if ch < 3:
                        for par in range(2):
                            p = slice(par * HD, (par + 1) * HD)
                            ps = take(dve, "D", f"S.{ch}.{par}")
                            V.tensor_tensor(SS[p, (ch + 1) % 2], ps[p, :].rearrange("p (q d) -> p q d", q=NP_),
                                            WZ[p, c, :, HD:], ALU.add).then_inc(moved["D"], 1)
                        await_moved(dve, f"S.{ch}.1")
                        dve.wait_ge(sem("fch"), 1)
                        nxt = SS[:, (ch + 1) % 2]
                        V.tensor_tensor(nxt, nxt, bc(fch[:, ch], HD, 2), ALU.mult).then_inc(sem("state"), 1)
                else:
                    dve.wait_ge(sem("fch"), 1)
                    V.tensor_tensor(SS[:, 1], WZ[:, 0, :, HD:], bc(fch[:, 0], HD, 2), ALU.mult).then_inc(sem("state"), 1)
            await_moved(dve, f"yS.{2 * t + 1}.1")
            for h in range(RH):
                last = V.bn_stats(bn_y[:, h], Y0[:, h * HD:(h + 1) * HD])
            L(last)
            for h in range(RH):
                last = V.bn_aggr(mv_y[t][:, h], bn_y[:, h])
            L(last)
            V.tensor_copy(rst[:, 6 + t], mv_y[t][:, :, 1]).then_inc(sem("y_var"), 1)

        bn_y = rst[:, 12:18].rearrange("p a b -> p (a b)").rearrange("p (h s) -> p h s", h=RH)
        mv_y = [rst[:, a:a + 2].rearrange("p a b -> p (a b)").rearrange("p (h s) -> p h s", h=RH) for a in (18, 20)]

        def group_norm(link, e, t, rstd_ready):
            h16 = lambda v: v.rearrange("p (h d) -> p h d", h=RH)
            o = r_[:, t]
            link(e.tensor_tensor(h16(o), h16(Y0), bc(mv_y[t][:, :, 0], HD, 2), ALU.subtract))
            rstd_ready()
            link(e.tensor_tensor(h16(o), h16(o), bc(rst[:, 8 + t], HD, 2), ALU.mult))
            link(e.tensor_tensor(o, o, ln_w, ALU.mult))
            link(e.tensor_tensor(o, o, ln_b, ALU.add))
            link(e.tensor_tensor(h16(Y0), h16(v_[:, t]), bc(rst[:, 4 + t], HD, 2), ALU.mult))
            link(e.tensor_tensor(o, o, Y0, ALU.add))
            e.tensor_tensor(o, o, g_[:, t], ALU.mult).then_inc(sem("y_done"), 1)

        def group_norm_dve(dve, t):
            group_norm(links["dve"], nc.vector, t, lambda: dve.wait_ge(sem("y_rstd"), t + 1))
            dve.wait_ge(sem("y_done"), t + 1)

        pe_fns.append(("F", rwkv_pe)); act_fns.append(("F", rwkv_act))
        pool_fns.append(("F", rwkv_pool)); dve_fns.append(("F", rwkv_dve))

        add_swiglu("G", "f1", 1, lambda act: after_residual(act, "w_ro"), ("ryT.1.1",),
                   ((8, 9), (10, 11), (0, 1), (2, 3)))

        def sp_stream(sp):
            names = [u[0] for u in units]
            cut = unit_at[f"moe.d.{G * EPG - 1}"] + 1 if "C" in phases and "O" in phases else 0
            few = min(8, cut)
            stream(sp, names[:few // 2])
            second_sp(sp)
            stream(sp, names[few // 2:few])
            small_sp(sp)
            stream(sp, names[few:cut])
            if cut:
                overflow_sp(sp)
            if "F" in phases:
                at = unit_at["w_rr.0.0"]
                stream(sp, names[cut:at])
                if "E" in phases:
                    sp.wait_ge(sem("down_f0"), T * (DFF // FF))
                rwkv_rows(sp)
                stream(sp, names[at:])
            else:
                stream(sp, names[cut:])

        block = ctx.enter_context(nc.Block())

        @block.tensor
        def _(pe):
            start_pe(pe)
            for ph, f in pe_fns:
                if ph in phases:
                    f(pe)

        @block.scalar
        def _(act):
            links["act"] = chain(act, "act_step")
            start_act_dma(act)
            act.wait_ge(sem("x_in"), 16 * T)
            for ph, f in act_fns:
                if ph in phases:
                    f(act)

        @block.vector
        def _(dve):
            links["dve"] = chain(dve, "dve_step")
            dve.wait_ge(sem("x_in"), 16 * T)
            start_dve(dve)
            for ph, f in dve_fns:
                if ph in phases:
                    f(dve)

        @block.gpsimd
        def _(pool):
            links["pool"] = chain(pool, "pool_step")
            start_pool(pool)
            for ph, f in pool_fns:
                if ph in phases:
                    f(pool)

        @block.sync
        def _(sp):
            start_sp(sp)
            sp_stream(sp)
            drained(sp, *[r for r in RINGS if not r.endswith("o")])
            sp.dma_start(out[0].rearrange("(t p) d -> p t d", p=P), X[:, :, :]).then_inc(sem("out"), 16)
            sp.wait_ge(sem("out"), 16)


def kernel(**inputs):
    import concourse.bacc as _bacc
    from concourse.bass_utils import run_bass_kernel_spmd as _run

    nc = _bacc.Bacc("TRN2", target_bir_lowering=False, num_devices=1)
    arrays, args = {}, {}
    for name, a in list(inputs.items()) + [("const_table", CONSTANTS)]:
        a = np.ascontiguousarray(a)
        if a.size == 0:
            continue
        arrays[name] = a
        args[name] = nc.dram_tensor(name, a.shape, mybir.dt.from_np(a.dtype), kind="ExternalInput").ap()
    out = nc.dram_tensor("y", (1, S, D), F32, kind="ExternalOutput").ap()
    build(nc, out, **args)
    r = _run(nc, [arrays], core_ids=[0])
    return r.results[0]["y"]
```
